# Optimizing a Trainium2 kernel written in Bass

```python
import jax, jax.numpy as jnp
from jax import lax
import numpy as np
import math

D_MODEL = 1024
BATCH = 1
SEQ = 256
DEPTH = 2

N_CONV_LAYERS = DEPTH // 2
N_MLA_LAYERS = DEPTH - N_CONV_LAYERS
CONV_WIDTH = 3
V_HEAD_DIM = 128
N_HEADS = D_MODEL // V_HEAD_DIM
QK_NOPE_DIM = 128
QK_ROPE_DIM = 64
KV_LORA_RANK = D_MODEL // 4
Q_LORA_RANK = 3 * D_MODEL // 8
D_FF = -(-8 * D_MODEL // (3 * 256)) * 256
ROPE_THETA = 10000.0
RMS_EPS = 1e-6
Q_BLOCK = 128


def rms_norm(x, g):
    xf = x.astype(jnp.float32)
    y = xf * lax.rsqrt(jnp.mean(xf * xf, axis=-1, keepdims=True) + RMS_EPS)
    return (y * g.astype(jnp.float32)).astype(x.dtype)

def rope_tables(positions):
    inv_freq = ROPE_THETA ** (-jnp.arange(0, QK_ROPE_DIM, 2, dtype=jnp.float32) / QK_ROPE_DIM)
    ang = positions.astype(jnp.float32)[..., None] * inv_freq
    return jnp.cos(ang), jnp.sin(ang)

def apply_rope(x, cos, sin):
    cos = cos.astype(x.dtype)
    sin = sin.astype(x.dtype)
    x1, x2 = jnp.split(x, 2, axis=-1)
    return jnp.concatenate([x1 * cos - x2 * sin, x1 * sin + x2 * cos], axis=-1)

def short_conv_mixer(h, w_in, conv_w, w_out):
    s = h.shape[1]
    u = h @ w_in
    gate_b, gate_c, val = jnp.split(u, 3, axis=-1)
    z = gate_c * val
    zp = jnp.pad(z, ((0, 0), (CONV_WIDTH - 1, 0), (0, 0)))
    conv = sum(conv_w[k] * zp[:, k:k + s] for k in range(CONV_WIDTH))
    return (gate_b * conv) @ w_out

def swiglu_ffn(h, w13, w2):
    g, u = jnp.split(h @ w13, 2, axis=-1)
    return (jax.nn.silu(g) * u) @ w2

def shared_mla_kv(h, kv_norm_g, w_dkv, kv_latent_norm_g, w_ukv, cos, sin):
    b, s, _ = h.shape
    hn = rms_norm(h, kv_norm_g)
    ckv = hn @ w_dkv
    c_lat = rms_norm(ckv[..., :KV_LORA_RANK], kv_latent_norm_g)
    k_pe = apply_rope(ckv[..., KV_LORA_RANK:], cos, sin)
    kv = (c_lat @ w_ukv).reshape(b, s, N_HEADS, QK_NOPE_DIM + V_HEAD_DIM)
    k_nope, v = kv[..., :QK_NOPE_DIM], kv[..., QK_NOPE_DIM:]
    return k_nope, k_pe, v

def causal_block_attention(q_nope, q_pe, k_nope, k_pe, v):
    b, s = q_nope.shape[:2]
    nb = s // Q_BLOCK
    qn = q_nope.reshape(b, nb, Q_BLOCK, N_HEADS, QK_NOPE_DIM).transpose(1, 0, 2, 3, 4)
    qr = q_pe.reshape(b, nb, Q_BLOCK, N_HEADS, QK_ROPE_DIM).transpose(1, 0, 2, 3, 4)
    starts = jnp.arange(nb, dtype=jnp.int32) * Q_BLOCK
    k_idx = jnp.arange(s, dtype=jnp.int32)
    scale = (QK_NOPE_DIM + QK_ROPE_DIM) ** -0.5
    neg = jnp.finfo(jnp.float32).min

    def one_block(args):
        qn_b, qr_b, start = args
        sc = (jnp.einsum('bqhd,bkhd->bhqk', qn_b, k_nope)
              + jnp.einsum('bqhr,bkr->bhqk', qr_b, k_pe))
        sc = sc.astype(jnp.float32) * scale
        q_idx = start + jnp.arange(Q_BLOCK, dtype=jnp.int32)
        mask = k_idx[None, :] <= q_idx[:, None]
        p = jax.nn.softmax(jnp.where(mask, sc, neg), axis=-1).astype(v.dtype)
        return jnp.einsum('bhqk,bkhd->bqhd', p, v)

    out = lax.map(one_block, (qn, qr, starts))
    return out.transpose(1, 0, 2, 3, 4).reshape(b, s, N_HEADS, V_HEAD_DIM)

def mla_mixer(h, w_dq, q_norm_g, w_uq, w_o, k_nope, k_pe, v, cos_h, sin_h):
    b, s, _ = h.shape
    cq = rms_norm(h @ w_dq, q_norm_g)
    q = (cq @ w_uq).reshape(b, s, N_HEADS, QK_NOPE_DIM + QK_ROPE_DIM)
    q_nope = q[..., :QK_NOPE_DIM]
    q_pe = apply_rope(q[..., QK_NOPE_DIM:], cos_h, sin_h)
    attn = causal_block_attention(q_nope, q_pe, k_nope, k_pe, v)
    return attn.reshape(b, s, N_HEADS * V_HEAD_DIM) @ w_o

def first_inputs(seed: int = 0) -> dict:
    key = jax.random.key(seed)
    ks = iter(jax.random.split(key, 32))
    f32 = jnp.float32
    res_scale = (2 * DEPTH) ** -0.5

    def w(shape, fan_in, extra=1.0):
        return jax.random.normal(next(ks), shape, f32) * (fan_in ** -0.5) * extra

    def gain(shape):
        return 1.0 + 0.02 * jax.random.normal(next(ks), shape, f32)

    na, nm = N_CONV_LAYERS, N_MLA_LAYERS
    x = jax.random.normal(next(ks), (BATCH, SEQ, D_MODEL), f32)
    positions = jnp.broadcast_to(jnp.arange(SEQ, dtype=jnp.int32), (BATCH, SEQ))
    return {
        "x": x,
        "positions": positions,
        "conv_norm_g": gain((na, D_MODEL)),
        "conv_w_in": w((na, D_MODEL, 3 * D_MODEL), D_MODEL),
        "conv_w": w((na, CONV_WIDTH, D_MODEL), CONV_WIDTH),
        "conv_w_out": w((na, D_MODEL, D_MODEL), D_MODEL, res_scale),
        "conv_ffn_norm_g": gain((na, D_MODEL)),
        "conv_ffn_w13": w((na, D_MODEL, 2 * D_FF), D_MODEL),
        "conv_ffn_w2": w((na, D_FF, D_MODEL), D_FF, res_scale),
        "kv_norm_g": gain((D_MODEL,)),
        "w_dkv": w((D_MODEL, KV_LORA_RANK + QK_ROPE_DIM), D_MODEL),
        "kv_latent_norm_g": gain((KV_LORA_RANK,)),
        "w_ukv": w((KV_LORA_RANK, N_HEADS * (QK_NOPE_DIM + V_HEAD_DIM)), KV_LORA_RANK),
        "mla_norm_g": gain((nm, D_MODEL)),
        "mla_w_dq": w((nm, D_MODEL, Q_LORA_RANK), D_MODEL),
        "mla_q_norm_g": gain((nm, Q_LORA_RANK)),
        "mla_w_uq": w((nm, Q_LORA_RANK, N_HEADS * (QK_NOPE_DIM + QK_ROPE_DIM)), Q_LORA_RANK),
        "mla_w_o": w((nm, N_HEADS * V_HEAD_DIM, D_MODEL), N_HEADS * V_HEAD_DIM, res_scale),
        "mla_ffn_norm_g": gain((nm, D_MODEL)),
        "mla_ffn_w13": w((nm, D_MODEL, 2 * D_FF), D_MODEL),
        "mla_ffn_w2": w((nm, D_FF, D_MODEL), D_FF, res_scale),
        "final_norm_g": gain((D_MODEL,)),
    }

def first_block(x, positions,
              conv_norm_g, conv_w_in, conv_w, conv_w_out,
              conv_ffn_norm_g, conv_ffn_w13, conv_ffn_w2,
              kv_norm_g, w_dkv, kv_latent_norm_g, w_ukv,
              mla_norm_g, mla_w_dq, mla_q_norm_g, mla_w_uq, mla_w_o,
              mla_ffn_norm_g, mla_ffn_w13, mla_ffn_w2,
              final_norm_g):
    cos, sin = rope_tables(positions)
    cos_h, sin_h = cos[:, :, None, :], sin[:, :, None, :]
    h = x
    k_nope = k_pe = v = None
    for i in range(DEPTH):
        if i < N_CONV_LAYERS:
            h = h + short_conv_mixer(rms_norm(h, conv_norm_g[i]), conv_w_in[i], conv_w[i], conv_w_out[i])
            h = h + swiglu_ffn(rms_norm(h, conv_ffn_norm_g[i]), conv_ffn_w13[i], conv_ffn_w2[i])
        else:
            if i == N_CONV_LAYERS:
                k_nope, k_pe, v = shared_mla_kv(h, kv_norm_g, w_dkv, kv_latent_norm_g, w_ukv, cos, sin)
            j = i - N_CONV_LAYERS
            h = h + mla_mixer(rms_norm(h, mla_norm_g[j]), mla_w_dq[j], mla_q_norm_g[j], mla_w_uq[j],
                              mla_w_o[j], k_nope, k_pe, v, cos_h, sin_h)
            h = h + swiglu_ffn(rms_norm(h, mla_ffn_norm_g[j]), mla_ffn_w13[j], mla_ffn_w2[j])
    return rms_norm(h, final_norm_g)


DEPTH_2 = 1

CHUNK = 64
LEFT_CHUNKS = 8
A_HEADS = 8
A_HEAD_DIM = 64
A_WIDTH = A_HEADS * A_HEAD_DIM
REL_CLIP = 128
B_HEADS = 4
B_HEAD_DIM = 128
B_WIDTH = B_HEADS * B_HEAD_DIM
CONV_K = 4
PEER_HEADS = 8
N_KEYS = 128
N_EXPERTS = N_KEYS * N_KEYS
PEER_TOPK = 16
D_KEY = 256
PEER_BLOCK = 128
EPS = 1e-6
IN_SIZES = [A_WIDTH, A_WIDTH, A_WIDTH, 2 * B_WIDTH, B_WIDTH, B_WIDTH, B_HEADS, B_HEADS, D_MODEL, D_MODEL]
IN_COLS = sum(IN_SIZES)


def rmsnorm(x, g):
    xf = x.astype(jnp.float32)
    y = xf * lax.rsqrt(jnp.mean(xf * xf, axis=-1, keepdims=True) + EPS)
    return (y * g.astype(jnp.float32)).astype(x.dtype)

def modulate(h, shift, scale):
    return h * (1.0 + scale[:, None, :]) + shift[:, None, :]

def causal_depthwise_conv(u, w, b):
    C = u.shape[-1]
    out = lax.conv_general_dilated(
        u, w[:, None, :].astype(u.dtype), window_strides=(1,), padding=[(CONV_K - 1, 0)],
        dimension_numbers=("NWC", "WIO", "NWC"), feature_group_count=C)
    return out + b

def chunk_band_attention(q, k, v, rel_bias):
    B, S, H, dh = q.shape
    nc = S // CHUNK
    pad = LEFT_CHUNKS * CHUNK
    band = pad + CHUNK
    kp = jnp.pad(k, ((0, 0), (pad, 0), (0, 0), (0, 0)))
    vp = jnp.pad(v, ((0, 0), (pad, 0), (0, 0), (0, 0)))
    qc = q.reshape(B, nc, CHUNK, H, dh).transpose(1, 0, 2, 3, 4)
    k_idx = jnp.arange(band)
    rel = jnp.clip(jnp.arange(CHUNK)[:, None] + pad - k_idx[None, :], -REL_CLIP, REL_CLIP) + REL_CLIP
    bias = rel_bias[:, rel].astype(jnp.float32)
    scale = dh ** -0.5

    def one_chunk(args):
        j, qj = args
        kj = lax.dynamic_slice_in_dim(kp, j * CHUNK, band, axis=1)
        vj = lax.dynamic_slice_in_dim(vp, j * CHUNK, band, axis=1)
        s = jnp.einsum("blhd,bkhd->bhlk", qj, kj).astype(jnp.float32) * scale + bias
        valid = (j * CHUNK + k_idx - pad) >= 0
        s = jnp.where(valid[None, None, None, :], s, -jnp.inf)
        p = jax.nn.softmax(s, axis=-1).astype(vj.dtype)
        return jnp.einsum("bhlk,bkhd->blhd", p, vj)

    out = lax.map(one_chunk, (jnp.arange(nc), qc))
    return out.transpose(1, 0, 2, 3, 4).reshape(B, S, H * dh)

def mlstm_chunkwise(q, k, v, i_pre, f_pre):
    B, S, H, d = q.shape
    nc = S // CHUNK
    k = k * (d ** -0.5)
    to_c = lambda t: t.reshape(B, nc, CHUNK, H, d).transpose(1, 0, 3, 2, 4)
    qc, kc, vc = to_c(q), to_c(k), to_c(v)
    li = i_pre.astype(jnp.float32).reshape(B, nc, CHUNK, H).transpose(1, 0, 3, 2)
    lf = jax.nn.log_sigmoid(f_pre.astype(jnp.float32)).reshape(B, nc, CHUNK, H).transpose(1, 0, 3, 2)
    a = jnp.cumsum(lf, axis=-1)
    A = a[..., -1]
    causal = jnp.tril(jnp.ones((CHUNK, CHUNK), dtype=bool))

    def step(carry, inp):
        C, n, m = carry
        qj, kj, vj, aj, Aj, lij = inp
        D = aj[..., :, None] - aj[..., None, :] + lij[..., None, :]
        D = jnp.where(causal, D, -jnp.inf)
        inter = aj + m[..., None]
        m_row = jnp.maximum(inter, jnp.max(D, axis=-1))
        w_inter = jnp.exp(inter - m_row)
        Wd = jnp.exp(D - m_row[..., None])
        qk = jnp.einsum("bhld,bhsd->bhls", qj, kj).astype(jnp.float32) * Wd
        num = w_inter[..., None] * jnp.einsum("bhld,bhde->bhle", qj, C) + jnp.einsum("bhls,bhse->bhle", qk, vj)
        den = w_inter * jnp.einsum("bhld,bhd->bhl", qj, n) + jnp.sum(qk, axis=-1)
        h = num / jnp.maximum(jnp.abs(den), jnp.exp(-m_row))[..., None]
        g = Aj[..., None] - aj + lij
        m_new = jnp.maximum(Aj + m, jnp.max(g, axis=-1))
        decay = jnp.exp(Aj + m - m_new)
        wk = jnp.exp(g - m_new[..., None])
        C_new = decay[..., None, None] * C + jnp.einsum("bhl,bhld,bhle->bhde", wk, kj, vj)
        n_new = decay[..., None] * n + jnp.einsum("bhl,bhld->bhd", wk, kj)
        return (C_new, n_new, m_new), h

    init = (jnp.zeros((B, H, d, d), jnp.float32), jnp.zeros((B, H, d), jnp.float32), jnp.zeros((B, H), jnp.float32))
    _, hs = lax.scan(step, init, (qc, kc, vc, a, A, li))
    return hs.transpose(1, 0, 3, 2, 4).reshape(B, S, H, d).astype(v.dtype)

def peer_ffn(h, w_pq, sub_keys, u_exp, v_exp):
    B, S, D = h.shape
    T = B * S
    hb = h.reshape(T // PEER_BLOCK, PEER_BLOCK, D)

    def block(xb):
        q = (xb @ w_pq).reshape(PEER_BLOCK, PEER_HEADS, 2, D_KEY // 2)
        s = jnp.einsum("thpd,hpnd->thpn", q, sub_keys).astype(jnp.float32)
        s_top, i_top = lax.top_k(s, PEER_TOPK)
        cand = (s_top[:, :, 0, :, None] + s_top[:, :, 1, None, :]).reshape(PEER_BLOCK, PEER_HEADS, PEER_TOPK * PEER_TOPK)
        best, ci = lax.top_k(cand, PEER_TOPK)
        i1 = jnp.take_along_axis(i_top[:, :, 0, :], ci // PEER_TOPK, axis=-1)
        i2 = jnp.take_along_axis(i_top[:, :, 1, :], ci % PEER_TOPK, axis=-1)
        e = i1 * N_KEYS + i2
        gate = jax.nn.softmax(best, axis=-1)
        u = u_exp[e]
        v = v_exp[e]
        act = jax.nn.gelu(jnp.einsum("thkd,td->thk", u, xb))
        return jnp.einsum("thk,thkd->td", (gate * act).astype(xb.dtype), v)

    return lax.map(block, hb).reshape(B, S, D)

def second_inputs(seed: int = 0) -> dict:
    key = jax.random.key(seed)
    ks = jax.random.split(key, 24)
    nrm = lambda k, shape, s: jax.random.normal(k, shape, jnp.float32) * s
    L = DEPTH_2
    return {
        "x": nrm(ks[0], (BATCH, SEQ, D_MODEL), 1.0),
        "c": nrm(ks[1], (BATCH, D_MODEL), 1.0),
        "w_ada": nrm(ks[2], (L, D_MODEL, 6 * D_MODEL), 0.5 * D_MODEL ** -0.5),
        "b_ada": nrm(ks[3], (L, 6 * D_MODEL), 0.02),
        "norm1_g": 1.0 + nrm(ks[4], (L, D_MODEL), 0.02),
        "w_in": nrm(ks[5], (L, D_MODEL, IN_COLS), D_MODEL ** -0.5),
        "conv_w": nrm(ks[6], (L, CONV_K, 2 * B_WIDTH), CONV_K ** -0.5),
        "conv_b": nrm(ks[7], (L, 2 * B_WIDTH), 0.02),
        "b_igate": nrm(ks[8], (L, B_HEADS), 0.1),
        "b_fgate": jnp.linspace(3.0, 6.0, B_HEADS)[None, :] + nrm(ks[9], (L, B_HEADS), 0.1),
        "rel_bias": nrm(ks[10], (L, A_HEADS, 2 * REL_CLIP + 1), 0.1),
        "mlstm_norm_g": 1.0 + nrm(ks[11], (L, B_WIDTH), 0.02),
        "w_branch_a": nrm(ks[12], (L, A_WIDTH, D_MODEL), A_WIDTH ** -0.5),
        "w_branch_b": nrm(ks[13], (L, B_WIDTH, D_MODEL), B_WIDTH ** -0.5),
        "w_out": nrm(ks[14], (L, D_MODEL, D_MODEL), D_MODEL ** -0.5),
        "norm2_g": 1.0 + nrm(ks[15], (L, D_MODEL), 0.02),
        "w_peer_q": nrm(ks[16], (L, D_MODEL, PEER_HEADS * D_KEY), D_MODEL ** -0.5),
        "peer_sub_keys": nrm(ks[17], (L, PEER_HEADS, 2, N_KEYS, D_KEY // 2), (D_KEY // 2) ** -0.5),
        "peer_u": nrm(ks[18], (L, N_EXPERTS, D_MODEL), D_MODEL ** -0.5),
        "peer_v": nrm(ks[19], (L, N_EXPERTS, D_MODEL), 0.5),
        "final_g": 1.0 + nrm(ks[20], (D_MODEL,), 0.02),
    }

def second_block(x, c, w_ada, b_ada, norm1_g, w_in, conv_w, conv_b, b_igate, b_fgate, rel_bias, mlstm_norm_g,
              w_branch_a, w_branch_b, w_out, norm2_g, w_peer_q, peer_sub_keys, peer_u, peer_v, final_g):
    B, S, _ = x.shape
    split_at = [int(s) for s in np.cumsum(IN_SIZES)[:-1]]
    for l in range(DEPTH_2):
        mod = jax.nn.silu(c) @ w_ada[l] + b_ada[l]
        sh1, sc1, gt1, sh2, sc2, gt2 = jnp.split(mod, 6, axis=-1)

        h = modulate(rmsnorm(x, norm1_g[l]), sh1, sc1)
        proj = h @ w_in[l]
        qa, ka, va, qkb, vb, ob, ib, fb, ga, gb = jnp.split(proj, split_at, axis=-1)
        qkb = jax.nn.silu(causal_depthwise_conv(qkb, conv_w[l], conv_b[l]))
        qb, kb = jnp.split(qkb, 2, axis=-1)
        heads_a = lambda t: t.reshape(B, S, A_HEADS, A_HEAD_DIM)
        heads_b = lambda t: t.reshape(B, S, B_HEADS, B_HEAD_DIM)
        y_a = chunk_band_attention(heads_a(qa), heads_a(ka), heads_a(va), rel_bias[l])
        hb = mlstm_chunkwise(heads_b(qb), heads_b(kb), heads_b(vb), ib + b_igate[l], fb + b_fgate[l])
        hb = rmsnorm(hb, mlstm_norm_g[l].reshape(B_HEADS, B_HEAD_DIM)).reshape(B, S, B_WIDTH)
        y_b = jax.nn.sigmoid(ob) * hb
        y = jax.nn.sigmoid(ga) * (y_a @ w_branch_a[l]) + jax.nn.sigmoid(gb) * (y_b @ w_branch_b[l])
        x = x + gt1[:, None, :] * (y @ w_out[l])

        h2 = modulate(rmsnorm(x, norm2_g[l]), sh2, sc2)
        x = x + gt2[:, None, :] * peer_ffn(h2, w_peer_q[l], peer_sub_keys[l], peer_u[l], peer_v[l])
    return rmsnorm(x, final_g)


def setup_inputs(seed=0):
    out = dict(first_inputs(seed))
    for name, value in second_inputs(seed + 1).items():
        if name != "x":
            out[name + "_2"] = value
    return out


def reference(
    x, positions, conv_norm_g, conv_w_in, conv_w, conv_w_out, conv_ffn_norm_g, conv_ffn_w13,
    conv_ffn_w2, kv_norm_g, w_dkv, kv_latent_norm_g, w_ukv, mla_norm_g, mla_w_dq, mla_q_norm_g,
    mla_w_uq, mla_w_o, mla_ffn_norm_g, mla_ffn_w13, mla_ffn_w2, final_norm_g, c_2, w_ada_2,
    b_ada_2, norm1_g_2, w_in_2, conv_w_2, conv_b_2, b_igate_2, b_fgate_2, rel_bias_2,
    mlstm_norm_g_2, w_branch_a_2, w_branch_b_2, w_out_2, norm2_g_2, w_peer_q_2, peer_sub_keys_2,
    peer_u_2, peer_v_2, final_g_2,
):
    x = first_block(
        x, positions, conv_norm_g, conv_w_in, conv_w, conv_w_out, conv_ffn_norm_g, conv_ffn_w13,
        conv_ffn_w2, kv_norm_g, w_dkv, kv_latent_norm_g, w_ukv, mla_norm_g, mla_w_dq,
        mla_q_norm_g, mla_w_uq, mla_w_o, mla_ffn_norm_g, mla_ffn_w13, mla_ffn_w2, final_norm_g,
    )
    return second_block(
        x, c_2, w_ada_2, b_ada_2, norm1_g_2, w_in_2, conv_w_2, conv_b_2, b_igate_2, b_fgate_2,
        rel_bias_2, mlstm_norm_g_2, w_branch_a_2, w_branch_b_2, w_out_2, norm2_g_2, w_peer_q_2,
        peer_sub_keys_2, peer_u_2, peer_v_2, final_g_2,
    )


_drawn_inputs = setup_inputs


def setup_inputs(seed=0):
    import zlib

    import numpy as np

    out = dict(_drawn_inputs(seed))
    spreads = {}
    factors = {'conv_ffn_norm_g': 5.12,
     'kv_norm_g': 8.0,
     'kv_latent_norm_g': 8.0,
     'mla_norm_g': 8.0,
     'mla_q_norm_g': 8.0,
     'mla_ffn_norm_g': 5.635,
     'b_ada_2': 3.042,
     'norm1_g_2': 8.0,
     'conv_b_2': 200.0,
     'b_igate_2': 64.0,
     'rel_bias_2': 8.0,
     'mlstm_norm_g_2': 29.341,
     'norm2_g_2': 21.28,
     'final_g_2': 21.281}
    for name, (base, spread) in spreads.items():
        noise = np.random.default_rng([zlib.crc32(name.encode()), seed]).standard_normal(out[name].shape)
        drawn = base * np.exp(spread * noise) if base else spread * noise
        out[name] = __import__('jax').numpy.asarray(drawn.astype(out[name].dtype))
    for name, factor in factors.items():
        out[name] = (out[name] * factor).astype(out[name].dtype)
    return out
```

```python
from contextlib import ExitStack

import numpy as np

import concourse.bass as bass
from concourse import mybir

ALU = mybir.AluOpType
ACT = mybir.ActivationFunctionType
F32 = mybir.dt.float32
F32R = mybir.dt.float32r
U32 = mybir.dt.uint32
I32 = mybir.dt.int32
AX = mybir.AxisListType.X

P = 128
T = 256
TB = T // P
D = 1024
DC = D // P
FF = 2816
FT = FF // P
HEADS = 8
NOPE, ROPE = 128, 64
KVR, QR = 256, 384
KC, QC = KVR // P, QR // P
EPS = 1e-6
MLA_SCALE = float(NOPE + ROPE) ** -0.5
CW = 3
CK = 4
AH, AHD = 8, 64
BH, BD = 4, 128
CHUNK, CLIP = 64, 128
PH, NK, TOPK = 8, 128, 16
NEG = -1e30
LOWEST = -3e38
ROUND = 12582912.0
TWO_PI_PARTS = (6.28125, 1.935303211212158203125e-3, 3.9683743166540886e-09)
PI_BELOW = 3.1415925

RING = 3
LEAD = 2

STAGES = [("conv_in", 3 * DC), ("conv_out", DC), ("ffn1", 3 * FT), ("latent", 7), ("uq", 6), ("ukv", 4),
          ("attn_out", DC), ("ffn2", 3 * FT), ("proj", 45), ("branch", DC), ("mix_out", DC),
          ("peer_q", 2 * PH), ("peer", 2 * NK)]
FIRST = {}
BLOCKS = 0
for _name, _count in STAGES:
    FIRST[_name] = BLOCKS
    BLOCKS += _count

NORMS = [("conv", DC, 1), ("ffn1", DC, 1), ("mla", DC, 2), ("qlat", QC, 1), ("kvlat", KC, 1), ("ffn2", DC, 1),
         ("final", DC, 0), ("mix", DC, 1), ("peer", DC, 1), ("final2", DC, 0)]
NORM_NO = {n: i for i, (n, _, _) in enumerate(NORMS)}

GAIN = {}
GAINS = 0
for _name, _count in [("conv", DC), ("ffn1", DC), ("kv", DC), ("mla", DC), ("kvlat", KC), ("qlat", QC), ("ffn2", DC),
                      ("final", DC), ("norm1", DC), ("norm2", DC), ("final2", DC), ("mlstm", BH), ("c", DC),
                      ("b_ada", 6 * DC), ("conv_w", CW * DC), ("conv2_w", CK * 2 * BH), ("conv2_b", 2 * BH),
                      ("inv_freq", 1)]:
    GAIN[_name] = GAINS
    GAINS += _count


def block_no(const, trip=None, per_trip=1):
    return (const, trip, per_trip)


def number(block):
    const, trip, per_trip = block
    return const if trip is None else const + trip * (RING * per_trip)


def lap(block):
    const, trip, per_trip = block
    return const // RING if trip is None else const // RING + trip * per_trip


def after(block, k):
    return (block[0] + k,) + block[1:]


def wait(eng, sem, value):
    if isinstance(value, int) and value <= 0:
        return
    eng.wait_ge(sem, value)



CONST = {}
CONSTS = 0
for _name, _count in [("ident", P), ("iota", P), ("mask", 3 * P), ("ones", P), ("upto", P), ("past0", P + 1),
                      ("past1", 2 * P + 1)]:
    CONST[_name] = (CONSTS, CONSTS + _count)
    CONSTS += _count


def build(nc, stream, ada, gains, consts, positions, x_in, band_bias, gate_bias, sub_keys, out):
    with ExitStack() as ctx:
        place = [(nc.sbuf_base + 63) // 64 * 64]

        def sem(name):
            return ctx.enter_context(nc.semaphore(name))

        def sb(name, shape, dt=F32):
            t = nc.alloc_sbuf_tensor_at(name, shape, dt, offset=place[0])
            place[0] += (int(np.prod(shape[1:])) * 4 + 31) // 32 * 32
            assert place[0] <= nc.sbuf_usable_end, (name, place[0])
            return t

        h = sb("h", [P, DC, T])
        xh = sb("xh", [P, DC, T], F32R)
        xl = sb("xl", [P, DC, T], F32R)
        raw = sb("raw", [P, RING, 1024])
        wh = sb("wh", [P, RING, 1024], F32R)
        wl = sb("wl", [P, RING, 1024], F32R)
        gv = sb("gv", [P, GAINS])
        mod = sb("mod", [P, 6 * DC])
        modg = sb("modg", [P, 2, DC])
        cst = sb("cst", [P, CONSTS])
        cols = sb("cols", [P, 4])
        csilu = sb("csilu", [P, DC])
        sd = sb("sd", [P, T])
        rs = sb("rs", [P, T])
        i_t = sb("i_t", [P, 3, T])
        peer_at = place[0]
        act = sb("act", [P, T])
        w32 = sb("w32", [P, T])
        ph = sb("ph", [P, RING, T], F32R)
        pl = sb("pl", [P, RING, T], F32R)
        arena = (place[0] + 63) // 64 * 64
        place[0] = peer_at
        hot = sb("hot", [P, 2, 2, 4, P])
        place[0] = max(arena, place[0])
        gates = sb("gates", [P, T, NK])

        place[0] = arena
        yh = sb("yh", [P, DC, T], F32R)
        yl = sb("yl", [P, DC, T], F32R)
        sq = sb("sq", [P, DC, T])
        ada_acc = sb("ada_acc", [P, 6, D])
        ada_w = sb("ada_w", [P, 2, D])
        ada_p = sb("ada_p", [P, D])
        shared = place[0]
        place[0] = arena + 2 * 8192
        sc = sb("sc", [P, 2, T])
        pr = sb("pr", [P, 2, T])
        pt = sb("pt", [P, 2, 3 * P])
        stat = sb("stat", [P, 4, 2 * AH])

        place[0] = shared
        z = sb("z", [P, T + CW - 1])
        gc = sb("gc", [P, T])
        cv = sb("cv", [P, 3, T])
        sg = sb("sg", [P, T])
        hid = sb("hid", [P, T])
        hidh = sb("hidh", [P, T], F32R)
        hidl = sb("hidl", [P, T], F32R)
        pos_i = sb("pos_i", [P, T], I32)
        ang = sb("ang", [P, 8, T])
        lat = sb("lat", [P, KC + QC, T])
        lath = sb("lath", [P, KC + QC, T], F32R)
        latl = sb("latl", [P, KC + QC, T], F32R)
        kpe = sb("kpe", [P, 2, T])
        qn = sb("qn", [P, HEADS, T])
        qpe = sb("qpe", [P, 2, 2, T])
        kn = sb("kn", [P, HEADS, T])
        vm = sb("vm", [P, TB, HEADS, NOPE])
        rt = sb("rt", [P, 2, 2 * T])
        place[0] = shared
        ga = sb("ga", [P, DC, T])
        gb = sb("gb", [P, DC, T])
        ob = sb("ob", [P, BH, T])
        qk = sb("qk", [P, 2 * BH, T])
        vb = sb("vb", [P, TB, BH, BD])
        va = sb("va", [P, TB, 4, P])
        qa = sb("qa", [P, 4, T])
        ka = sb("ka", [P, 4, T])
        gt = sb("gt", [P, TB, 2 * BH])
        gw = sb("gw", [P, TB, 3, BH])
        u = sb("u", [P, T + CK - 1])
        uc = sb("uc", [P, CK, T])
        rr = sb("rr", [P, TB, 2 * P + 1])
        dm = sb("dm", [P, 2 * P + 1])
        sv = sb("sv", [P, T])
        st = sb("st", [P, 3 * P])
        hb = sb("hb", [P, TB, BH, BD])
        ms = sb("ms", [P, 10, 2 * BH])
        place[0] = arena + 3 * 8192
        bias = sb("bias", [P, AH, 3 * P])
        sk = sb("sk", [P, 2 * PH, NK])
        gbias = sb("gbias", [P, 2 * BH])
        place[0] = arena
        qp = sb("qp", [P, 2 * PH, T])
        place[0] = shared
        s2 = sb("s2", [P, NK])
        val = sb("val", [P, 2 * PH, TOPK])
        idx = sb("idx", [P, 2 * PH, TOPK], U32)
        idxf = sb("idxf", [P, 2 * PH, TOPK])
        cand = sb("cand", [P, PH, TOPK * TOPK])
        c2 = sb("c2", [P, TOPK * TOPK])
        best = sb("best", [P, PH, TOPK])
        pick = sb("pick", [P, 3, PH, TOPK], U32)
        pickf = sb("pickf", [P, 2, PH, TOPK])
        eq = sb("eq", [P, PH, TOPK, TOPK])
        key = sb("key", [P, 3, PH, TOPK])
        soft = sb("soft", [P, 2, PH])

        wk = ctx.enter_context(nc.psum_tensor("wk", [P, 4, 512], F32))
        acc = ctx.enter_context(nc.psum_tensor("acc", [P, 4, 512], F32))

        def acc_tile(j):
            return acc[:, j // 2, (j % 2) * T:(j % 2 + 1) * T]

        raw_in = [sem(f"raw_in{i}") for i in range(RING)]
        hi_ready = sem("hi_ready")
        lo_ready = sem("lo_ready")
        block_used = sem("block_used")
        const_in = sem("const_in")
        band_in = sem("band_in")
        set_up = sem("set_up")
        squares = sem("squares")
        summed = sem("summed")
        rooted = sem("rooted")
        scaled = sem("scaled")
        normed_hi = sem("normed_hi")
        normed = sem("normed")
        gate_copied = sem("gate_copied")
        gated = sem("gated")
        conved = sem("conved")
        conved_hi = sem("conved_hi")
        conved_lo = sem("conved_lo")
        res_add = sem("res_add")
        silu_ready = sem("silu_ready")
        hid_ready = sem("hid_ready")
        hid_hi = sem("hid_hi")
        hid_lo = sem("hid_lo")
        lat_read = sem("lat_read")
        uq_read = sem("uq_read")
        ukv_read = sem("ukv_read")
        angles = sem("angles")
        trig = sem("trig")
        scored = sem("scored")
        masked = sem("masked")
        expd = sem("expd")
        probs = sem("probs")
        turned = sem("turned")
        pt_ready = sem("pt_ready")
        mixed = sem("mixed")
        mixed_hi = sem("mixed_hi")
        mixed_lo = sem("mixed_lo")
        ada_in = [sem("ada_in0"), sem("ada_in1")]
        csilu_ready = sem("csilu_ready")
        ada_scaled = sem("ada_scaled")
        ada_added = sem("ada_added")
        ada_done = sem("ada_done")
        mod_summed = sem("mod_summed")
        mod_ready = sem("mod_ready")
        proj_dve = sem("proj_dve")
        proj_act = sem("proj_act")
        conv2 = sem("conv2")
        silu2 = sem("silu2")
        gate_exp = sem("gate_exp")
        gates_ready = sem("gates_ready")
        decays = sem("decays")
        decay_sums = sem("decay_sums")
        decay_max = sem("decay_max")
        decay_exp = sem("decay_exp")
        weighted = sem("weighted")
        w_turned = sem("w_turned")
        st_ready = sem("st_ready")
        m_mixed = sem("m_mixed")
        m_out = sem("m_out")
        m_sq = sem("m_sq")
        m_root = sem("m_root")
        m_normed = sem("m_normed")
        m_turned = sem("m_turned")
        m_gated = sem("m_gated")
        m_hi = sem("m_hi")
        m_lo = sem("m_lo")
        branch_sum = sem("branch_sum")
        branch_hi = sem("branch_hi")
        branch_lo = sem("branch_lo")
        qp_ready = sem("qp_ready")
        key_scored = sem("key_scored")
        key_read = sem("key_read")
        best_sub = sem("best_sub")
        best_exp = sem("best_exp")
        keys_ready = sem("keys_ready")
        keys_turned = sem("keys_turned")
        i_ready = sem("i_ready")
        hot_ready = sem("hot_ready")
        hot_used = sem("hot_used")
        gates_kept = sem("gates_kept")
        act_ready = sem("act_ready")
        w_ready = sem("w_ready")
        w_hi = sem("w_hi")
        w_lo = sem("w_lo")
        conv_step = sem("conv_step")
        step = sem("step")
        act_step = sem("act_step")
        out_sent = sem("out_sent")

        def const(name):
            a, b = CONST[name]
            return cst[:, a:b]

        def gain(name, k=0):
            return gv[:, GAIN[name] + k:GAIN[name] + k + 1]

        def squares_before(name):
            return sum(n for _, n, _ in NORMS[:NORM_NO[name]])

        def scaled_before(name):
            return sum(n * max(k, 1) for _, n, k in NORMS[:NORM_NO[name]])

        def normed_before(name):
            return sum(n * k for _, n, k in NORMS[:NORM_NO[name]])

        added = {name: i * DC for i, name in enumerate(["conv_out", "ffn1", "attn_out", "ffn2", "mix_out", "peer"])}

        def attention_base(kind):
            return 0 if kind == "latent" else HEADS

        block = ctx.enter_context(nc.Block())
        CONST_LOADS = 4

        @block.sync
        def _(sp):
            for n in range(RING):
                sp.dma_start(raw[:, n], stream[n]).then_inc(raw_in[n], 16)
            with sp.Fori(1, BLOCKS // RING) as i:
                for k in range(RING):
                    sp.wait_ge(lo_ready, i * RING + (k - RING + 1))
                    sp.dma_start(raw[:, k], stream[bass.ds(i * RING + k, 1)].rearrange("a p n -> (a p) n")
                                 ).then_inc(raw_in[k], 16)
            for n in range(BLOCKS // RING * RING, BLOCKS):
                sp.wait_ge(lo_ready, n - RING + 1)
                sp.dma_start(raw[:, n % RING], stream[n]).then_inc(raw_in[n % RING], 16)
            sp.wait_ge(scaled, scaled_before("final2") + DC)
            sp.dma_start(out, sq[:]).then_inc(out_sent, 16)
            sp.wait_ge(out_sent, 16)

        @block.gpsimd
        def _(pool):
            pool.wait_ge(csilu_ready, 1)

            def load(n):
                part, k = divmod(n, DC)
                pool.dma_start(ada_w[:, n % 2], ada[k * P:(k + 1) * P, part * D:(part + 1) * D]).then_inc(ada_in[n % 2], 16)

            load(0)
            load(1)
            for n in range(6 * DC):
                part, k = divmod(n, DC)
                pool.wait_ge(ada_in[n % 2], (n // 2 + 1) * 16)
                if k == 0:
                    pool.tensor_scalar(ada_acc[:, part], ada_w[:, n % 2], csilu[:, k:k + 1], None, ALU.mult
                                       ).then_inc(ada_scaled, 1)
                    pool.wait_ge(ada_scaled, n + 1)
                else:
                    wait(pool, ada_added, part * (DC - 1) + k - 1)
                    pool.tensor_scalar(ada_p[:], ada_w[:, n % 2], csilu[:, k:k + 1], None, ALU.mult
                                       ).then_inc(ada_scaled, 1)
                    pool.wait_ge(ada_scaled, n + 1)
                    pool.tensor_tensor(ada_acc[:, part], ada_acc[:, part], ada_p[:], ALU.add).then_inc(ada_added, 1)
                if n + 2 < 6 * DC:
                    load(n + 2)
            pool.wait_ge(ada_added, 6 * (DC - 1))
            pool.wait_ge(mod_summed, 1)
            pool.dma_start(bias[:], band_bias).then_inc(band_in, 16)
            pool.dma_start(sk[:], sub_keys).then_inc(band_in, 16)
            pool.dma_start(gbias[:], gate_bias).then_inc(band_in, 16)

        @block.tensor
        def _(pe):
            def three(out_ap, a_hi, a_lo, b_hi, b_lo, start, stop, skip=False):
                pe.matmul(out_ap, a_hi, b_hi, start=start, stop=False, skip_group_check=skip)
                pe.matmul(out_ap, a_hi, b_lo, start=False, stop=False, skip_group_check=skip)
                return pe.matmul(out_ap, a_lo, b_hi, start=False, stop=stop, skip_group_check=skip)

            def ready(blk):
                pe.wait_ge(lo_ready, number(blk) + 1)

            def piece(w, blk, lo, hi):
                return w[:, blk[0] % RING, lo:hi]

            def features(blk, bank, ah, al, first_wait=None):
                ready(blk)
                for c in range(DC):
                    if first_wait is not None:
                        pe.wait_ge(normed, first_wait + c + 1)
                    mm = three(wk[:, bank, 0:T], piece(wh, blk, c * P, c * P + P), piece(wl, blk, c * P, c * P + P),
                               ah[:, c], al[:, c], c == 0, c == DC - 1)
                mm.then_inc(block_used, 1)

            def tokens(blk, bank, ah, al, n, first_wait=None):
                ready(blk)
                if first_wait is not None:
                    pe.wait_ge(normed, first_wait + DC)
                for b in range(TB):
                    for c in range(DC):
                        mm = three(wk[:, bank, b * P:b * P + n], ah[:, c, b * P:(b + 1) * P], al[:, c, b * P:(b + 1) * P],
                                   piece(wh, blk, c * P, c * P + n), piece(wl, blk, c * P, c * P + n), c == 0, c == DC - 1)
                mm.then_inc(block_used, 1)

            def norm_sums(name):
                n = NORMS[NORM_NO[name]][1]
                base = squares_before(name)
                for c in range(n):
                    pe.wait_ge(squares, base + c + 1)
                    mm = pe.matmul(wk[:, 3, 0:T], const("ones"), sq[:, c], start=c == 0, stop=c == n - 1)
                mm.then_inc(summed, 1)

            pe.wait_ge(const_in, 16 * CONST_LOADS)
            norm_sums("conv")

            def conv_tile(c, blk, first):
                wait(pe, gate_copied, c)
                features(blk, 0, xh, xl, normed_before("conv") if first else None)
                wait(pe, gated, c)
                features(after(blk, 1), 1, xh, xl)
                wait(pe, conved, c)
                features(after(blk, 2), 2, xh, xl)

            conv_tile(0, block_no(0), True)
            with pe.Fori(1, DC) as c:
                conv_tile(c, block_no(0, c), False)

            def add_out(stage, ah, al, done, count):
                for c in range(DC):
                    blk = block_no(FIRST[stage] + c)
                    if c == 0:
                        pe.wait_ge(done, count)
                    wait(pe, res_add, added[stage] + c - 2 if c >= RING else 0)
                    features(blk, blk[0] % RING, ah, al)

            add_out("conv_out", yh, yl, conved_lo, DC)

            def ffn(stage, norm, turn):
                first = FIRST[stage]
                base = turn * FT

                def w2(blk, j, start, stop):
                    ready(blk)
                    pe.wait_ge(hid_lo, base + j + 1)
                    for o in range(DC):
                        mm = three(acc_tile(o), piece(wh, blk, o * P, o * P + P), piece(wl, blk, o * P, o * P + P),
                                   hidh[:], hidl[:], start and o % 2 == 0, stop, skip=True)
                    mm.then_inc(block_used, 1)

                b0 = first % RING
                norm_sums(norm)
                features(block_no(first), b0, xh, xl, normed_before(norm))
                features(block_no(first + 1), (b0 + 1) % RING, xh, xl)

                def triple(j, blk, start):
                    pe.wait_ge(silu_ready, base + j)
                    features(blk, b0, xh, xl)
                    pe.wait_ge(hid_ready, base + j)
                    features(after(blk, 1), (b0 + 1) % RING, xh, xl)
                    w2(after(blk, 2), j - 1, start, False)

                triple(1, block_no(first + 2), True)
                with pe.Fori(2, FT) as j:
                    triple(j, block_no(first - 1, j), False)
                w2(block_no(first + 3 * FT - 1), FT - 1, False, True)

            ffn("ffn1", "ffn1", 0)

            norm_sums("mla")
            base = normed_before("mla")
            for k in range(7):
                blk = block_no(FIRST["latent"] + k)
                wait(pe, lat_read, k - 2)
                if k == 0:
                    features(blk, blk[0] % RING, xh, xl, base)
                elif k < 4:
                    features(blk, blk[0] % RING, xh, xl)
                elif k == 4:
                    features(blk, blk[0] % RING, yh, yl, base + DC)
                else:
                    features(blk, blk[0] % RING, yh, yl)
            norm_sums("qlat")
            norm_sums("kvlat")

            pe.wait_ge(normed, normed_before("qlat") + QC)
            for k in range(6):
                blk = block_no(FIRST["uq"] + k)
                wait(pe, uq_read, k - 2)
                ready(blk)
                for t in range(2):
                    for c in range(QC):
                        at = (t * QC + c) * P
                        mm = three(wk[:, k % RING, t * T:(t + 1) * T], piece(wh, blk, at, at + P), piece(wl, blk, at, at + P),
                                   lath[:, KC + c], latl[:, KC + c], c == 0, c == QC - 1)
                mm.then_inc(block_used, 1)
            pe.wait_ge(normed, normed_before("kvlat") + KC)
            pe.wait_ge(uq_read, 6)
            for k in range(4):
                blk = block_no(FIRST["ukv"] + k)
                wait(pe, ukv_read, k - 1)
                ready(blk)
                b = 2 * (k % 2)
                if k < 2:
                    for t in range(4):
                        for c in range(KC):
                            at = c * 512 + t * P
                            mm = three(wk[:, b + t // 2, (t % 2) * T:(t % 2 + 1) * T], piece(wh, blk, at, at + P),
                                       piece(wl, blk, at, at + P), lath[:, c], latl[:, c], c == 0, c == KC - 1)
                else:
                    for t in range(TB):
                        for c in range(KC):
                            mm = three(wk[:, b + t], lath[:, c, t * P:(t + 1) * P], latl[:, c, t * P:(t + 1) * P],
                                       piece(wh, blk, c * 512, c * 512 + 512), piece(wl, blk, c * 512, c * 512 + 512),
                                       c == 0, c == KC - 1)
                mm.then_inc(block_used, 1)

            def attention(kind):
                h0 = attention_base(kind)

                def scores(i):
                    for b in range(TB):
                        n = (b + 1) * P
                        unit = TB * (h0 + i) + b
                        wait(pe, masked, unit - 3)
                        bank = wk[:, unit % 4, 0:n]
                        if kind == "latent":
                            r = 32 * (i % 4)
                            pe.matmul(bank, qn[:, i, b * P:(b + 1) * P], kn[:, i, 0:n], start=True, stop=False)
                            for s in range(2):
                                mm = pe.matmul(bank, qpe[r:r + 32, s, i // 4, b * P:(b + 1) * P], kpe[r:r + 32, s, 0:n],
                                               start=False, stop=s == 1, tile_position=(r, 0))
                        else:
                            r = AHD * (i % 2)
                            mm = pe.matmul(bank, qa[r:r + AHD, i // 2, b * P:(b + 1) * P], ka[r:r + AHD, i // 2, 0:n],
                                           start=True, stop=True)
                        mm.then_inc(scored, 1)

                def turn(i):
                    n = h0 + i
                    wait(pe, pt_ready, n - 1)
                    for b in range(TB):
                        pe.wait_ge(probs, TB * n + b + 1)
                        for k in range(b + 1):
                            at = (b + k) * P
                            mm = pe.transpose(acc[:, n % 2, at:at + P], pr[:, b, k * P:(k + 1) * P], const("ident"))
                    mm.then_inc(turned, 1)

                def mix(i):
                    n = h0 + i
                    pe.wait_ge(pt_ready, n + 1)
                    if kind == "latent":
                        wait(pe, mixed_lo, i - 1)
                        o = acc[:, 2 + n % 2, 0:T]
                        pe.matmul(o, vm[:, 0, i], pt[:, n % 2, 0:T], start=True, stop=False, skip_group_check=True)
                        pe.matmul(acc[:, 2 + n % 2, P:T], vm[:, 1, i], pt[:, n % 2, T:3 * P], start=False, stop=True,
                                  skip_group_check=True).then_inc(mixed, 1)
                    else:
                        r = AHD * (i % 2)
                        bank = 2 + (i // 2) % 2
                        wait(pe, mixed_lo, HEADS + i // 2 - 1 if i >= 4 else 0)
                        for t in range(TB):
                            mm = pe.matmul(acc[r:r + AHD, bank, t * P:T], va[:, t, i // 2, r:r + AHD],
                                           pt[:, n % 2, 2 * t * P:2 * t * P + T - t * P],
                                           start=t == 0, stop=t == 1, skip_group_check=True)
                        mm.then_inc(mixed, 1)

                count = HEADS if kind == "latent" else AH
                scores(0)
                for i in range(count):
                    if i + 1 < count:
                        scores(i + 1)
                    turn(i)
                    if i >= 1:
                        mix(i - 1)
                mix(count - 1)

            pe.wait_ge(ukv_read, 4)
            pe.wait_ge(trig, 3)
            attention("latent")
            add_out("attn_out", yh, yl, mixed_lo, HEADS)
            ffn("ffn2", "ffn2", 1)
            norm_sums("final")

            pe.wait_ge(ada_added, 6 * (DC - 1))
            for j in range(6 * DC):
                mm = pe.matmul(wk[:, 0, j:j + 1], ada_acc[:, j // DC, (j % DC) * P:(j % DC + 1) * P], const("ones")[:, 0:1],
                               start=True, stop=True)
            mm.then_inc(mod_summed, 1)
            norm_sums("mix")
            pe.wait_ge(mod_ready, 1)
            base = normed_before("mix")
            for k in range(45):
                blk = block_no(FIRST["proj"] + k)
                if k - RING >= 9:
                    pe.wait_ge(proj_act, k - RING - 8)
                elif k >= RING:
                    pe.wait_ge(proj_dve, k - RING + 1)
                bank = blk[0] % RING
                if k == 0:
                    tokens(blk, bank, xh, xl, 2 * BH, base)
                elif 9 <= k < 17:
                    tokens(blk, bank, xh, xl, P)
                else:
                    features(blk, bank, xh, xl)

            pe.wait_ge(proj_act, 36)
            pe.wait_ge(silu2, 2 * BH)
            for i in range(BH):
                pe.wait_ge(decays, i + 1)
                for b in range(TB):
                    unit = TB * i + b
                    wait(pe, weighted, unit)
                    n = (b + 1) * P
                    if b == 0:
                        pe.matmul(wk[:, 0, 0:P + 1], const("upto"), rr[:, 0, 0:P + 1], start=True, stop=True)
                    else:
                        pe.matmul(wk[:, 0, 0:T + 1], const("upto"), rr[:, 1], start=True, stop=False, skip_group_check=True)
                        pe.matmul(wk[:, 0, 0:P + 1], const("ones"), rr[:, 0, 0:P + 1], start=False, stop=True,
                                  skip_group_check=True)
                    pe.matmul(wk[:, 1, 0:n], qk[:, i, b * P:n], qk[:, BH + i, 0:n], start=True, stop=True
                              ).then_inc(decay_sums, 1)
                    pe.wait_ge(weighted, unit + 1)
                    for k in range(b + 1):
                        mm = pe.transpose(wk[:, 2, k * P:(k + 1) * P], sv[:, k * P:(k + 1) * P], const("ident"))
                    mm.then_inc(w_turned, 1)
                    pe.wait_ge(st_ready, unit + 1)
                    wait(pe, m_out, unit)
                    for k in range(b + 1):
                        mm = pe.matmul(wk[:, 3, 0:P], st[:, k * P:(k + 1) * P], vb[:, k, i], start=k == 0, stop=k == b)
                    mm.then_inc(m_mixed, 1)
            pe.wait_ge(m_normed, 1)
            for i in range(BH):
                wait(pe, m_gated, i - 1)
                for b in range(TB):
                    mm = pe.transpose(wk[:, 2 * (i % 2), b * P:(b + 1) * P], hb[:, b, i], const("ident"))
                mm.then_inc(m_turned, 1)

            pe.wait_ge(m_gated, BH)
            attention("band")
            pe.wait_ge(mixed_lo, HEADS + AH // 2)
            pe.wait_ge(m_lo, BH)
            for k in range(DC):
                blk = block_no(FIRST["branch"] + k)
                ready(blk)
                wait(pe, branch_sum, k - 1)
                for s in range(2):
                    for c in range(4):
                        at = (4 * s + c) * P
                        mm = three(wk[:, 2 * (k % 2) + s, 0:T], piece(wh, blk, at, at + P), piece(wl, blk, at, at + P),
                                   yh[:, 4 * s + c], yl[:, 4 * s + c], c == 0, c == 3)
                mm.then_inc(block_used, 1)
            add_out("mix_out", xh, xl, branch_lo, DC)

            norm_sums("peer")
            base = normed_before("peer")
            for k in range(2 * PH):
                blk = block_no(FIRST["peer_q"] + k)
                wait(pe, qp_ready, k - 2)
                features(blk, blk[0] % RING, xh, xl, base if k == 0 else None)
            pe.wait_ge(qp_ready, 2 * PH)
            pe.wait_ge(band_in, 48)
            for b in range(TB):
                for g in range(4):
                    n = 4 * b + g
                    wait(pe, key_read, n - 3)
                    for j in range(4):
                        mm = pe.matmul(wk[:, n % 4, j * P:(j + 1) * P], qp[:, 4 * g + j, b * P:(b + 1) * P], sk[:, 4 * g + j],
                                       start=True, stop=True)
                    mm.then_inc(key_scored, 1)
            for b in range(TB):
                pe.wait_ge(keys_ready, b + 1)
                for s in range(3):
                    mm = pe.transpose(acc[:, b, s * P:(s + 1) * P], key[:, s].rearrange("p h k -> p (h k)"), const("ident"))
                mm.then_inc(keys_turned, 1)
            def gate_group(g, par, first):
                pe.wait_ge(hot_ready, g + 1)
                wait(pe, gates_kept, g - 1 if not first else 0)
                for j in range(4):
                    mm = pe.matmul(wk[:, par, j * P:(j + 1) * P], hot[:, par, 1, j], hot[:, par, 0, j], start=True, stop=True)
                mm.then_inc(hot_used, 1)

            gate_group(0, 0, True)
            gate_group(1, 1, True)
            with pe.Fori(1, T // 8) as i:
                for par in range(2):
                    gate_group(i * 2 + par, par, False)
            p0 = FIRST["peer"]

            def experts_in(blk, bank):
                features(blk, bank, xh, xl)

            def experts_out(blk, i, k, start, stop):
                ready(blk)
                pe.wait_ge(w_lo, i + 1)
                for o in range(DC):
                    mm = three(acc_tile(o), piece(wh, blk, o * P, o * P + P), piece(wl, blk, o * P, o * P + P),
                               ph[:, k], pl[:, k], start and o % 2 == 0, stop, skip=True)
                mm.then_inc(block_used, 1)

            pe.wait_ge(gates_kept, T // 4)
            experts_in(block_no(p0), 0)

            def pair(i, k, blk, start):
                wait(pe, act_ready, i)
                experts_in(blk, (k + 1) % RING)
                experts_out(after(blk, 1), i, k, start, False)

            pair(0, 0, block_no(p0 + 1), True)
            with pe.Fori(0, (NK - 2) // RING) as t:
                for k in range(RING):
                    pair(t * RING + (1 + k), (1 + k) % RING, block_no(p0 + 3 + 2 * k, t, 2), False)
            experts_out(block_no(p0 + 2 * NK - 1), NK - 1, (NK - 1) % RING, False, True)
            norm_sums("final2")

        @block.scalar
        def _(sc_e):
            def hi(blk):
                n = number(blk)
                sc_e.wait_ge(raw_in[blk[0] % RING], (lap(blk) + 1) * 16)
                wait(sc_e, block_used, n - (RING - 1))
                nc.scalar.activation(wh[:, blk[0] % RING], raw[:, blk[0] % RING], ACT.Copy).then_inc(hi_ready, 1)

            def ahead(blk):
                if blk[1] is None and blk[0] + LEAD >= BLOCKS:
                    return
                hi(after(blk, LEAD))

            def used(blk):
                sc_e.wait_ge(block_used, number(blk) + 1)

            def norm(name, src, src_sem=None, src_base=0, splits=(), sources=None):
                n = NORMS[NORM_NO[name]][1]
                sc0 = scaled_before(name)
                wait(sc_e, normed, normed_before(name))
                for c in range(n):
                    if src_sem is not None:
                        sc_e.wait_ge(src_sem, src_base + c + 1)
                    nc.scalar.activation(sq[:, c], src[:, c], ACT.Square).then_inc(squares, 1)
                sc_e.wait_ge(summed, NORM_NO[name] + 1)
                nc.scalar.activation(sd[:], wk[:, 3, 0:T], ACT.Sqrt, bias=cols[:, 0:1], scale=1.0 / (n * P)
                                     ).then_inc(rooted, 1)
                for s, (dst, off, b) in enumerate(splits):
                    for c in range(n):
                        sc_e.wait_ge(scaled, sc0 + s * n + c + 1)
                        if b is None:
                            ins = nc.scalar.activation(dst[:, off + c], sq[:, c], ACT.Copy)
                        else:
                            ins = nc.scalar.activation(dst[:, off + c], sq[:, c], ACT.Identity,
                                                       bias=mod[:, b * DC + c:b * DC + c + 1])
                        ins.then_inc(normed_hi, 1)

            sc_e.dma_start(h[:], x_in).then_inc(const_in, 16)
            sc_e.dma_start(gv[:], gains).then_inc(const_in, 16)
            sc_e.dma_start(cst[:], consts).then_inc(const_in, 16)
            sc_e.dma_start(pos_i[:], positions.partition_broadcast(P)).then_inc(const_in, 16)
            sc_e.wait_ge(const_in, 16 * CONST_LOADS)
            nc.scalar.activation(csilu[:], gv[:, GAIN["c"]:GAIN["c"] + DC], ACT.Silu).then_inc(csilu_ready, 1)
            sc_e.wait_ge(angles, 1)
            nc.scalar.activation(ang[:, 7], ang[:, 3], ACT.Sin).then_inc(trig, 1)
            nc.scalar.activation(ang[:, 6], ang[:, 4], ACT.Sin, bias=cols[:, 1:2], scale=-1.0).then_inc(trig, 1)

            hi(block_no(0))
            hi(block_no(1))
            norm("conv", h, splits=[(xh, 0, None)])

            def conv_tile(c, blk):
                ahead(blk)
                used(blk)
                wait(sc_e, gated, c)
                nc.scalar.activation(gc[:], wk[:, 0, 0:T], ACT.Copy).then_inc(gate_copied, 1)
                ahead(after(blk, 1))
                ahead(after(blk, 2))
                sc_e.wait_ge(conved, c + 1)
                dst = yh[:, c] if isinstance(c, int) else yh[:, bass.ds(c, 1)].rearrange("p a t -> p (a t)")
                nc.scalar.activation(dst, cv[:, 2], ACT.Copy).then_inc(conved_hi, 1)

            conv_tile(0, block_no(0))
            with sc_e.Fori(1, DC) as c:
                conv_tile(c, block_no(0, c))
            for c in range(DC):
                ahead(block_no(FIRST["conv_out"] + c))

            def ffn(stage, norm_name, turn, res):
                first = FIRST[stage]
                base = turn * FT
                b0 = first % RING
                norm(norm_name, h, res_add, res, splits=[(xh, 0, None)])

                def silu(blk, j):
                    used(blk)
                    wait(sc_e, hid_ready, base + j)
                    nc.scalar.activation(sg[:], wk[:, b0, 0:T], ACT.Silu).then_inc(silu_ready, 1)

                def split_hid(j, used_before):
                    sc_e.wait_ge(hid_ready, base + j + 1)
                    sc_e.wait_ge(block_used, used_before)
                    nc.scalar.activation(hidh[:], hid[:], ACT.Copy).then_inc(hid_hi, 1)

                ahead(block_no(first))
                silu(block_no(first), 0)
                ahead(block_no(first + 1))

                def triple(j, blk):
                    ahead(blk)
                    split_hid(j - 1, number(blk))
                    silu(blk, j)
                    ahead(after(blk, 1))
                    ahead(after(blk, 2))

                triple(1, block_no(first + 2))
                with sc_e.Fori(2, FT) as j:
                    triple(j, block_no(first - 1, j))
                last = block_no(first + 3 * FT - 1)
                split_hid(FT - 1, number(last))
                ahead(last)

            ffn("ffn1", "ffn1", 0, 0)
            norm("mla", h, res_add, DC, splits=[(xh, 0, None), (yh, 0, None)])
            for k in range(7):
                ahead(block_no(FIRST["latent"] + k))
            norm("qlat", lat[:, KC:], lat_read, 4, splits=[(lath, KC, None)])
            norm("kvlat", lat, splits=[(lath, 0, None)])
            for k in range(6):
                ahead(block_no(FIRST["uq"] + k))
            for k in range(4):
                ahead(block_no(FIRST["ukv"] + k))

            def attention(kind):
                h0 = attention_base(kind)
                for i in range(HEADS + 2):
                    if i < HEADS:
                        for b in range(TB):
                            unit = TB * (h0 + i) + b
                            sc_e.wait_ge(masked, unit + 1)
                            wait(sc_e, turned, h0 + i)
                            nc.scalar.activation(pr[:, b, 0:(b + 1) * P], sc[:, b, 0:(b + 1) * P], ACT.Exp,
                                                 bias=stat[:, 0, TB * i + b:TB * i + b + 1],
                                                 accum_out=stat[:, 1, TB * i + b:TB * i + b + 1]).then_inc(expd, 1)
                    if 1 <= i <= HEADS:
                        n = h0 + i - 1
                        sc_e.wait_ge(turned, n + 1)
                        wait(sc_e, mixed, n - 1)
                        nc.scalar.activation(pt[:, n % 2], acc[:, n % 2, 0:3 * P], ACT.Copy).then_inc(pt_ready, 1)
                    if i >= 2:
                        j = i - 2
                        if kind == "latent":
                            sc_e.wait_ge(mixed, j + 1)
                            nc.scalar.activation(yh[:, j], acc[:, 2 + j % 2, 0:T], ACT.Copy).then_inc(mixed_hi, 1)
                        elif j % 2 == 1:
                            sc_e.wait_ge(mixed, h0 + j + 1)
                            nc.scalar.activation(yh[:, j // 2], acc[:, 2 + (j // 2) % 2, 0:T], ACT.Copy
                                                 ).then_inc(mixed_hi, 1)

            attention("latent")
            for c in range(DC):
                ahead(block_no(FIRST["attn_out"] + c))
            ffn("ffn2", "ffn2", 1, 2 * DC)
            norm("final", h, res_add, 3 * DC)
            norm("mix", h, scaled, scaled_before("final"), splits=[(xh, 0, 0)])

            for k in range(45):
                blk = block_no(FIRST["proj"] + k)
                ahead(blk)
                if k == 0:
                    continue
                if k < 9:
                    sc_e.wait_ge(conv2, k)
                    nc.scalar.activation(qk[:, k - 1], uc[:, CK - 1], ACT.Silu).then_inc(silu2, 1)
                    continue
                used(blk)
                src = wk[:, blk[0] % RING, 0:T]
                by_token = src.rearrange("p (b n) -> p b n", b=TB)
                if k < 13:
                    ins = nc.scalar.activation(vb[:, :, k - 9], by_token, ACT.Copy)
                elif k < 17:
                    ins = nc.scalar.activation(va[:, :, k - 13], by_token, ACT.Copy)
                elif k < 21:
                    ins = nc.scalar.activation(qa[:, k - 17], src, ACT.Copy)
                elif k < 25:
                    ins = nc.scalar.activation(ka[:, k - 21], src, ACT.Copy)
                elif k < 29:
                    ins = nc.scalar.activation(ob[:, k - 25], src, ACT.Sigmoid)
                else:
                    c = k - 29
                    ins = nc.scalar.activation((ga if c < DC else gb)[:, c % DC], src, ACT.Sigmoid)
                ins.then_inc(proj_act, 1)
            sc_e.wait_ge(gates_ready, 1)
            nc.scalar.activation(gw[:, :, 1], gw[:, :, 0], ACT.Exp, scale=-1.0).then_inc(gate_exp, 1)
            sc_e.wait_ge(gate_exp, 1)
            nc.scalar.activation(gw[:, :, 2], gw[:, :, 1], ACT.Ln, bias=cols[:, 3:4]).then_inc(gate_exp, 1)
            for i in range(BH):
                for b in range(TB):
                    unit = TB * i + b
                    n = (b + 1) * P
                    sc_e.wait_ge(decay_max, unit + 1)
                    nc.scalar.activation(dm[:, 1:n + 1], dm[:, 1:n + 1], ACT.Exp, bias=ms[:, 0, unit:unit + 1]
                                         ).then_inc(decay_exp, 1)
                    nc.scalar.activation(ms[:, 1, unit:unit + 1], ms[:, 0, unit:unit + 1], ACT.Exp).then_inc(decay_exp, 1)
                    sc_e.wait_ge(w_turned, unit + 1)
                    wait(sc_e, m_mixed, unit)
                    nc.scalar.activation(st[:, 0:n], wk[:, 2, 0:n], ACT.Copy).then_inc(st_ready, 1)
                    sc_e.wait_ge(m_out, unit + 1)
                    nc.scalar.activation(uc[:, 3, 0:P], hb[:, b, i], ACT.Square, accum_out=ms[:, 4, unit:unit + 1]
                                         ).then_inc(m_sq, 1)
            sc_e.wait_ge(m_sq, TB * BH)
            nc.scalar.activation(ms[:, 5], ms[:, 4], ACT.Sqrt, bias=cols[:, 0:1], scale=1.0 / BD).then_inc(m_root, 1)
            for i in range(BH):
                sc_e.wait_ge(m_gated, i + 1)
                nc.scalar.activation(yh[:, 4 + i], uc[:, i % 2], ACT.Copy).then_inc(m_hi, 1)
            attention("band")
            for k in range(DC):
                ahead(block_no(FIRST["branch"] + k))
                sc_e.wait_ge(branch_sum, k + 1)
                nc.scalar.activation(xh[:, k], uc[:, 2], ACT.Copy).then_inc(branch_hi, 1)
            for c in range(DC):
                ahead(block_no(FIRST["mix_out"] + c))
            norm("peer", h, res_add, 4 * DC, splits=[(xh, 0, 3)])
            for k in range(2 * PH):
                blk = block_no(FIRST["peer_q"] + k)
                ahead(blk)
                used(blk)
                nc.scalar.activation(qp[:, k], wk[:, blk[0] % RING, 0:T], ACT.Copy).then_inc(qp_ready, 1)
            for b in range(TB):
                sc_e.wait_ge(best_sub, b + 1)
                nc.scalar.activation(key[:, 2], best[:], ACT.Exp).then_inc(best_exp, 1)
            for b in range(TB):
                sc_e.wait_ge(keys_turned, b + 1)
                nc.scalar.activation(i_t[:, :, b * P:(b + 1) * P], acc[:, b, 0:3 * P].rearrange("p (s t) -> p s t", s=3),
                                     ACT.Copy).then_inc(i_ready, 1)

            def gate_group(g, par):
                sc_e.wait_ge(hot_used, g + 1)
                tok = gates[:, bass.ds(g * 4, 4)].rearrange("p t k -> p (t k)")
                nc.scalar.activation(tok, wk[:, par], ACT.Copy).then_inc(gates_kept, 1)

            with sc_e.Fori(0, T // 8) as i:
                for par in range(2):
                    gate_group(i * 2 + par, par)

            p0 = FIRST["peer"]

            def activate(blk, i, bank):
                used(blk)
                wait(sc_e, w_ready, i)
                nc.scalar.activation(act[:], wk[:, bank, 0:T], ACT.Gelu_apprx_tanh).then_inc(act_ready, 1)

            ahead(block_no(p0))
            activate(block_no(p0), 0, 0)

            def pair(i, k, blk):
                sc_e.wait_ge(w_ready, i + 1)
                wait(sc_e, block_used, number(blk) - 4)
                nc.scalar.activation(ph[:, k], w32[:], ACT.Copy).then_inc(w_hi, 1)
                ahead(blk)
                activate(blk, i + 1, (k + 1) % RING)
                ahead(after(blk, 1))

            pair(0, 0, block_no(p0 + 1))
            with sc_e.Fori(0, (NK - 2) // RING - 1) as t:
                for k in range(RING):
                    pair(t * RING + (1 + k), (1 + k) % RING, block_no(p0 + 3 + 2 * k, t, 2))
            for i in range(NK - 1 - RING, NK - 1):
                pair(i, i % RING, block_no(p0 + 1 + 2 * i))
            sc_e.wait_ge(w_ready, NK)
            nc.scalar.activation(ph[:, (NK - 1) % RING], w32[:], ACT.Copy).then_inc(w_hi, 1)
            norm("final2", h, res_add, 5 * DC)

        @block.vector
        def _(dve):
            v = nc.vector
            done = [0]

            def chain(ins):
                done[0] += 1
                ins.then_inc(step, 1)
                dve.wait_ge(step, done[0])

            def lo(blk):
                s = blk[0] % RING
                dve.wait_ge(hi_ready, number(blk) + 1)
                v.tensor_tensor(wl[:, s], raw[:, s], wh[:, s].bitcast(F32), ALU.subtract).then_inc(lo_ready, 1)

            def ahead(blk):
                if blk[1] is None and blk[0] + LEAD >= BLOCKS:
                    return
                lo(after(blk, LEAD))

            def used(blk):
                dve.wait_ge(block_used, number(blk) + 1)

            def norm(name, src, splits=(), dst=None):
                n = NORMS[NORM_NO[name]][1]
                sc0, hi0 = scaled_before(name), normed_before(name)
                dve.wait_ge(rooted, NORM_NO[name] + 1)
                wait(dve, scaled, sc0)
                wait(dve, normed, hi0)
                chain(v.reciprocal(rs[:], sd[:]))

                def scale(g, c, to):
                    v.scalar_tensor_tensor(out=to, in0=src[:, c], scalar=g(c), in1=rs[:], op0=ALU.mult,
                                           op1=ALU.mult).then_inc(scaled, 1)

                if dst is not None:
                    for c in range(n):
                        scale(dst[0], c, dst[1][:, c])
                    return
                for s, (g, th, tl, off, shift) in enumerate(splits):
                    def rest(c):
                        dve.wait_ge(normed_hi, hi0 + s * n + c + 1)
                        a, b = sq[:, c], th[:, off + c].bitcast(F32)
                        if shift is None:
                            ins = v.tensor_tensor(tl[:, off + c], a, b, ALU.subtract)
                        else:
                            ins = v.scalar_tensor_tensor(out=tl[:, off + c], in0=a, in1=b, op0=ALU.add, op1=ALU.subtract,
                                                         scalar=mod[:, shift * DC + c:shift * DC + c + 1])
                        ins.then_inc(normed, 1)

                    for c in range(n):
                        if s > 0:
                            dve.wait_ge(normed, hi0 + (s - 1) * n + c + 1)
                        scale(g, c, sq[:, c])
                        if c >= 1:
                            rest(c - 1)
                    rest(n - 1)

            def gain_of(name):
                return lambda c: gain(name, c)

            def columns(t, base=0):
                return lambda c: t[:, base + c:base + c + 1]

            v.memset(cols[:, 0:1], EPS).then_inc(set_up, 1)
            v.memset(cols[:, 1:2], float(np.pi / 2)).then_inc(set_up, 1)
            v.memset(cols[:, 2:3], 0.0).then_inc(set_up, 1)
            v.memset(cols[:, 3:4], 1.0).then_inc(set_up, 1)
            v.memset(z[:, 0:CW - 1], 0.0).then_inc(set_up, 1)
            dve.wait_ge(set_up, 5)
            dve.wait_ge(const_in, 16 * CONST_LOADS)
            chain(v.tensor_copy(ang[:, 0], pos_i[:]))
            chain(v.tensor_scalar(ang[:, 1], ang[:, 0], gain("inv_freq"), None, ALU.mult))
            chain(v.tensor_scalar(ang[:, 2], ang[:, 1], float(1 / (2 * np.pi)), ROUND, ALU.mult, ALU.add))
            chain(v.tensor_scalar(ang[:, 2], ang[:, 2], -ROUND, None, ALU.add))
            for k, part in enumerate(TWO_PI_PARTS):
                chain(v.scalar_tensor_tensor(out=ang[:, 1], in0=ang[:, 2], scalar=-part, in1=ang[:, 1],
                                             op0=ALU.mult, op1=ALU.add))
            chain(v.tensor_scalar(ang[:, 3], ang[:, 1], PI_BELOW, -PI_BELOW, ALU.min, ALU.max))
            v.scalar_tensor_tensor(out=ang[:, 4], in0=ang[:, 3], scalar=-1.0, in1=ang[:, 3], op0=ALU.mult, op1=ALU.max
                                   ).then_inc(angles, 1)

            lo(block_no(0))
            lo(block_no(1))
            norm("conv", h, splits=[(gain_of("conv"), xh, xl, 0, None)])

            def conv_tile(c, blk):
                def at(t, k=0, width=1):
                    return t[:, bass.ds(c * width + k, 1)] if not isinstance(c, int) else \
                        t[:, c * width + k:c * width + k + 1]

                w0 = GAIN["conv_w"]
                taps = gv[:, w0:w0 + CW * DC]
                base = c * (CW + 1)
                ahead(blk)
                used(after(blk, 1))
                dve.wait_ge(gate_copied, c + 1)
                wait(dve, conv_step, c * CW)
                wait(dve, conved_lo, c)
                v.tensor_tensor(z[:, CW - 1:], gc[:], wk[:, 1, 0:T], ALU.mult).then_inc(gated, 1)
                ahead(after(blk, 1))
                dve.wait_ge(gated, c + 1)
                v.tensor_scalar(cv[:, 0], z[:, 0:T], at(taps, 0, CW), None, ALU.mult).then_inc(conv_step, 1)
                dve.wait_ge(conv_step, c * CW + 1)
                v.scalar_tensor_tensor(out=cv[:, 1], in0=z[:, 1:T + 1], scalar=at(taps, 1, CW), in1=cv[:, 0],
                                       op0=ALU.mult, op1=ALU.add).then_inc(conv_step, 1)
                dve.wait_ge(conv_step, c * CW + 2)
                v.scalar_tensor_tensor(out=cv[:, 0], in0=z[:, 2:T + 2], scalar=at(taps, 2, CW), in1=cv[:, 1],
                                       op0=ALU.mult, op1=ALU.add).then_inc(conv_step, 1)
                ahead(after(blk, 2))
                dve.wait_ge(conv_step, c * CW + 3)
                used(after(blk, 2))
                v.tensor_tensor(cv[:, 2], cv[:, 0], wk[:, 2, 0:T], ALU.mult).then_inc(conved, 1)
                dve.wait_ge(conved_hi, c + 1)
                tile = (lambda t: t[:, c]) if isinstance(c, int) else \
                    (lambda t: t[:, bass.ds(c, 1)].rearrange("p a t -> p (a t)"))
                v.tensor_tensor(tile(yl), cv[:, 2], tile(yh).bitcast(F32), ALU.subtract).then_inc(conved_lo, 1)

            conv_tile(0, block_no(0))
            with dve.Fori(1, DC) as c:
                conv_tile(c, block_no(0, c))

            def add_out(stage, factor=None):
                for c in range(DC):
                    blk = block_no(FIRST[stage] + c)
                    ahead(blk)
                    used(blk)
                    src = wk[:, blk[0] % RING, 0:T]
                    if factor is None:
                        ins = v.tensor_tensor(h[:, c], h[:, c], src, ALU.add)
                    else:
                        ins = v.scalar_tensor_tensor(out=h[:, c], in0=src, scalar=factor(c), in1=h[:, c], op0=ALU.mult,
                                                     op1=ALU.add)
                    ins.then_inc(res_add, 1)

            add_out("conv_out")

            def ffn(stage, norm_name, turn):
                first = FIRST[stage]
                base = turn * FT
                b0 = first % RING
                norm(norm_name, h, splits=[(gain_of(norm_name), xh, xl, 0, None)])

                def product(blk, j):
                    used(blk)
                    dve.wait_ge(silu_ready, base + j + 1)
                    wait(dve, hid_lo, base + j)
                    v.tensor_tensor(hid[:], sg[:], wk[:, (b0 + 1) % RING, 0:T], ALU.mult).then_inc(hid_ready, 1)

                def rest(j):
                    dve.wait_ge(hid_hi, base + j + 1)
                    v.tensor_tensor(hidl[:], hid[:], hidh[:].bitcast(F32), ALU.subtract).then_inc(hid_lo, 1)

                ahead(block_no(first))
                ahead(block_no(first + 1))
                product(block_no(first + 1), 0)

                def triple(j, blk):
                    ahead(blk)
                    rest(j - 1)
                    ahead(after(blk, 1))
                    product(after(blk, 1), j)
                    ahead(after(blk, 2))

                triple(1, block_no(first + 2))
                with dve.Fori(2, FT) as j:
                    triple(j, block_no(first - 1, j))
                last = block_no(first + 3 * FT - 1)
                rest(FT - 1)
                ahead(last)
                used(last)
                for c in range(DC):
                    v.tensor_tensor(h[:, c], h[:, c], acc_tile(c), ALU.add).then_inc(res_add, 1)

            ffn("ffn1", "ffn1", 0)
            norm("mla", h, splits=[(gain_of("kv"), xh, xl, 0, None), (gain_of("mla"), yh, yl, 0, None)])
            dve.wait_ge(trig, 2)
            for k in range(7):
                blk = block_no(FIRST["latent"] + k)
                ahead(blk)
                used(blk)
                b = blk[0] % RING
                if k < 2:
                    v.tensor_copy(lat[:, k], wk[:, b, 0:T]).then_inc(lat_read, 1)
                elif k == 3:
                    x1, x2 = wk[:, (b - 1) % RING, 0:T], wk[:, b, 0:T]
                    cos, sin = ang[:, 6], ang[:, 7]
                    v.tensor_tensor(rt[:, 0, 0:T], x2, sin, ALU.mult).then_inc(step, 1)
                    v.tensor_tensor(rt[:, 0, T:2 * T], x2, cos, ALU.mult).then_inc(step, 1)
                    v.tensor_tensor(rt[:, 1, 0:T], x1, cos, ALU.mult).then_inc(step, 1)
                    done[0] += 3
                    chain(v.tensor_tensor(rt[:, 1, T:2 * T], x1, sin, ALU.mult))
                    v.tensor_tensor(kpe[:, 0], rt[:, 1, 0:T], rt[:, 0, 0:T], ALU.subtract).then_inc(lat_read, 1)
                    v.tensor_tensor(kpe[:, 1], rt[:, 1, T:2 * T], rt[:, 0, T:2 * T], ALU.add).then_inc(lat_read, 1)
                elif k > 3:
                    v.tensor_copy(lat[:, KC + k - 4], wk[:, b, 0:T]).then_inc(lat_read, 1)
            norm("qlat", lat[:, KC:], splits=[(gain_of("qlat"), lath, latl, KC, None)])
            norm("kvlat", lat, splits=[(gain_of("kvlat"), lath, latl, 0, None)])
            for k in range(6):
                blk = block_no(FIRST["uq"] + k)
                ahead(blk)
                used(blk)
                b = k % RING
                if k < 4:
                    v.tensor_copy(qn[:, 2 * k:2 * k + 2], wk[:, b].rearrange("p (a t) -> p a t", a=2)).then_inc(uq_read, 1)
                elif k == 5:
                    x1 = wk[:, (b - 1) % RING].rearrange("p (a t) -> p a t", a=2)
                    x2 = wk[:, b].rearrange("p (a t) -> p a t", a=2)
                    dve.wait_ge(lat_read, 7)
                    for s in range(2):
                        cos, sin = ang[:, 6], ang[:, 7]
                        v.tensor_tensor(rt[:, 0, 0:T], x2[:, s], sin, ALU.mult).then_inc(step, 1)
                        v.tensor_tensor(rt[:, 0, T:2 * T], x2[:, s], cos, ALU.mult).then_inc(step, 1)
                        v.tensor_tensor(rt[:, 1, 0:T], x1[:, s], cos, ALU.mult).then_inc(step, 1)
                        done[0] += 3
                        chain(v.tensor_tensor(rt[:, 1, T:2 * T], x1[:, s], sin, ALU.mult))
                        v.tensor_tensor(qpe[:, 0, s], rt[:, 1, 0:T], rt[:, 0, 0:T], ALU.subtract).then_inc(step, 1)
                        done[0] += 1
                        ins = v.tensor_tensor(qpe[:, 1, s], rt[:, 1, T:2 * T], rt[:, 0, T:2 * T], ALU.add)
                        chain(ins)
                    v.engine_nop().then_inc(uq_read, 2)
            for k in range(4):
                blk = block_no(FIRST["ukv"] + k)
                ahead(blk)
                used(blk)
                b = 2 * (k % 2)
                if k < 2:
                    v.tensor_copy(kn[:, 4 * k:4 * k + 4].rearrange("p a t -> p (a t)"),
                                  wk[:, b:b + 2].rearrange("p a t -> p (a t)")).then_inc(ukv_read, 1)
                else:
                    a = 4 * (k - 2)
                    v.tensor_copy(vm[:, :, a:a + 4].rearrange("p b a d -> p b (a d)"), wk[:, b:b + 2]).then_inc(ukv_read, 1)
            v.engine_nop().then_inc(trig, 1)

            def attention(kind):
                h0 = attention_base(kind)

                def mask(i, b):
                    n = (b + 1) * P
                    unit = TB * (h0 + i) + b
                    dve.wait_ge(scored, unit + 1)
                    wait(dve, expd, unit - 1)
                    if kind == "latent":
                        m, scale = const("mask")[:, b * P:b * P + n], MLA_SCALE
                    else:
                        m, scale = bias[:, i, b * P:b * P + n], AHD ** -0.5
                    chain(v.scalar_tensor_tensor(out=sc[:, b, 0:n], in0=wk[:, unit % 4, 0:n], scalar=scale, in1=m,
                                                 op0=ALU.mult, op1=ALU.add))
                    s = TB * i + b
                    v.tensor_reduce(stat[:, 0, s:s + 1], sc[:, b, 0:n], AX, ALU.max, negate=True).then_inc(masked, 1)

                def divide(i, b):
                    n = (b + 1) * P
                    s = TB * i + b
                    dve.wait_ge(expd, TB * (h0 + i) + b + 1)
                    chain(v.reciprocal(stat[:, 2, s:s + 1], stat[:, 1, s:s + 1]))
                    v.tensor_scalar(pr[:, b, 0:n], pr[:, b, 0:n], stat[:, 2, s:s + 1], None, ALU.mult).then_inc(probs, 1)

                for i in range(HEADS + 2):
                    if i < HEADS:
                        mask(i, 0)
                        mask(i, 1)
                        divide(i, 0)
                        divide(i, 1)
                    if i >= 2:
                        j = i - 2
                        if kind == "latent":
                            dve.wait_ge(mixed_hi, j + 1)
                            v.tensor_tensor(yl[:, j], acc[:, 2 + j % 2, 0:T], yh[:, j].bitcast(F32), ALU.subtract
                                            ).then_inc(mixed_lo, 1)
                        elif j % 2 == 1:
                            dve.wait_ge(mixed_hi, HEADS + j // 2 + 1)
                            v.tensor_tensor(yl[:, j // 2], acc[:, 2 + (j // 2) % 2, 0:T], yh[:, j // 2].bitcast(F32),
                                            ALU.subtract).then_inc(mixed_lo, 1)

            attention("latent")
            add_out("attn_out")
            ffn("ffn2", "ffn2", 1)
            norm("final", h, dst=(gain_of("final"), h))

            dve.wait_ge(mod_summed, 1)
            chain(v.tensor_tensor(mod[:], wk[:, 0, 0:6 * DC], gv[:, GAIN["b_ada"]:GAIN["b_ada"] + 6 * DC], ALU.add))
            for s, name in enumerate(["norm1", "norm2"]):
                part = mod[:, (3 * s + 1) * DC:(3 * s + 2) * DC]
                chain(v.scalar_tensor_tensor(out=modg[:, s], in0=part, scalar=1.0,
                                             in1=gv[:, GAIN[name]:GAIN[name] + DC], op0=ALU.add, op1=ALU.mult))
            v.memset(u[:, 0:CK - 1], 0.0).then_inc(mod_ready, 1)
            norm("mix", h, splits=[(columns(modg[:, 0]), xh, xl, 0, 0)])
            for k in range(45):
                blk = block_no(FIRST["proj"] + k)
                ahead(blk)
                if k == 0:
                    dve.wait_ge(band_in, 48)
                    used(blk)
                    for b in range(TB):
                        ins = v.tensor_tensor(gt[:, b], wk[:, blk[0] % RING, b * P:b * P + 2 * BH], gbias[:], ALU.add)
                        if b == 0:
                            ins.then_inc(step, 1)
                            done[0] += 1
                    ins.then_inc(proj_dve, 1)
                elif k < 9:
                    used(blk)
                    c = k - 1
                    w0 = GAIN["conv2_w"] + CK * c
                    wait(dve, conv2, k - 1)
                    v.tensor_copy(u[:, CK - 1:], wk[:, blk[0] % RING, 0:T]).then_inc(proj_dve, 1)
                    dve.wait_ge(proj_dve, k + 1)
                    wait(dve, silu2, k - 1)
                    chain(v.tensor_scalar(uc[:, 0], u[:, 0:T], gv[:, w0:w0 + 1], gain("conv2_b", c), ALU.mult, ALU.add))
                    for t in range(1, CK):
                        ins = v.scalar_tensor_tensor(out=uc[:, t], in0=u[:, t:t + T], scalar=gv[:, w0 + t:w0 + t + 1],
                                                     in1=uc[:, t - 1], op0=ALU.mult, op1=ALU.add)
                        if t < CK - 1:
                            chain(ins)
                        else:
                            ins.then_inc(conv2, 1)
            dve.wait_ge(proj_dve, 1)
            v.scalar_tensor_tensor(out=gw[:, :, 0], in0=gt[:, :, BH:], scalar=-1.0, in1=gt[:, :, BH:], op0=ALU.mult,
                                   op1=ALU.max).then_inc(gates_ready, 1)
            dve.wait_ge(gate_exp, 2)
            for b in range(TB):
                chain(v.scalar_tensor_tensor(out=gt[:, b, BH:], in0=gt[:, b, BH:], scalar=0.0, in1=gw[:, b, 2],
                                             op0=ALU.min, op1=ALU.subtract))
            ident, past = const("ident"), (const("past0"), const("past1"))
            chain(v.memset(rr[:], 0.0))
            for i in range(BH):
                wait(dve, decay_sums, TB * i)
                for b in range(TB):
                    n = (b + 1) * P
                    chain(v.tensor_scalar(rr[:, b, 0:n + 1], past[b], gt[:, b, BH + i:BH + i + 1], None, ALU.mult))
                    ins = v.scalar_tensor_tensor(out=rr[:, b, b * P + 1:n + 1], in0=ident, scalar=gt[:, b, i:i + 1],
                                                 in1=rr[:, b, b * P + 1:n + 1], op0=ALU.mult, op1=ALU.add)
                    if b == 0:
                        chain(ins)
                    else:
                        ins.then_inc(decays, 1)
                for b in range(TB):
                    unit = TB * i + b
                    n = (b + 1) * P
                    col = lambda r: ms[:, r, unit:unit + 1]
                    dve.wait_ge(decay_sums, unit + 1)
                    v.tensor_copy(dm[:, 0:1], wk[:, 0, 0:1]).then_inc(step, 1)
                    done[0] += 1
                    chain(v.tensor_tensor(dm[:, 1:n + 1], wk[:, 0, 1:n + 1], const("mask")[:, b * P:b * P + n], ALU.add))
                    v.tensor_reduce(col(0), dm[:, 0:n + 1], AX, ALU.max, negate=True).then_inc(decay_max, 1)
                    dve.wait_ge(decay_exp, 2 * unit + 2)
                    v.scalar_tensor_tensor(out=sv[:, 0:n], in0=wk[:, 1, 0:n], scalar=BD ** -0.5, in1=dm[:, 1:n + 1],
                                           op0=ALU.mult, op1=ALU.mult, accum_out=col(2)).then_inc(weighted, 1)
                    dve.wait_ge(weighted, unit + 1)
                    chain(v.scalar_tensor_tensor(out=col(3), in0=col(2), scalar=-1.0, in1=col(2), op0=ALU.mult, op1=ALU.max))
                    chain(v.tensor_scalar(col(3), col(3), col(1), None, ALU.max))
                    chain(v.reciprocal(col(6), col(3)))
                    dve.wait_ge(m_mixed, unit + 1)
                    v.tensor_scalar(hb[:, b, i], wk[:, 3, 0:P], col(6), None, ALU.mult).then_inc(m_out, 1)
            dve.wait_ge(m_root, 1)
            chain(v.reciprocal(ms[:, 7], ms[:, 5]))
            for i in range(BH):
                for b in range(TB):
                    unit = TB * i + b
                    chain(v.tensor_scalar(hb[:, b, i], hb[:, b, i], ms[:, 7, unit:unit + 1], None, ALU.mult))
            v.engine_nop().then_inc(m_normed, 1)
            for i in range(BH):
                dve.wait_ge(m_turned, i + 1)
                wait(dve, m_lo, i - 1)
                wait(dve, m_hi, i - 1)
                v.scalar_tensor_tensor(out=uc[:, i % 2], in0=wk[:, 2 * (i % 2), 0:T], scalar=gain("mlstm", i), in1=ob[:, i],
                                       op0=ALU.mult, op1=ALU.mult).then_inc(m_gated, 1)
                dve.wait_ge(m_hi, i + 1)
                v.tensor_tensor(yl[:, 4 + i], uc[:, i % 2], yh[:, 4 + i].bitcast(F32), ALU.subtract).then_inc(m_lo, 1)
            attention("band")
            for k in range(DC):
                blk = block_no(FIRST["branch"] + k)
                ahead(blk)
                used(blk)
                b = 2 * (k % 2)
                v.tensor_tensor(uc[:, 0], ga[:, k], wk[:, b, 0:T], ALU.mult).then_inc(step, 1)
                done[0] += 1
                chain(v.tensor_tensor(uc[:, 1], gb[:, k], wk[:, b + 1, 0:T], ALU.mult))
                wait(dve, branch_lo, k)
                v.tensor_tensor(uc[:, 2], uc[:, 0], uc[:, 1], ALU.add).then_inc(branch_sum, 1)
                dve.wait_ge(branch_hi, k + 1)
                v.tensor_tensor(xl[:, k], uc[:, 2], xh[:, k].bitcast(F32), ALU.subtract).then_inc(branch_lo, 1)
            add_out("mix_out", columns(mod, 2 * DC))
            norm("peer", h, splits=[(columns(modg[:, 1]), xh, xl, 0, 3)])
            for k in range(2 * PH):
                ahead(block_no(FIRST["peer_q"] + k))

            def top16(values, spare, out_v, out_i, last_sem=None):
                chain(v.max(out_v[:, 0:8], values))
                v.max_index(out_i[:, 0:8], out_v[:, 0:8], values).then_inc(step, 1)
                done[0] += 1
                chain(v.match_replace(spare, out_v[:, 0:8], values, LOWEST))
                chain(v.max(out_v[:, 8:16], spare))
                ins = v.max_index(out_i[:, 8:16], out_v[:, 8:16], spare)
                if last_sem is None:
                    chain(ins)
                else:
                    ins.then_inc(last_sem, 1)

            iota16 = const("iota")[:, 0:TOPK]

            def spread(ap, dims):
                for d in range(3):
                    if d not in dims:
                        ap = ap.unsqueeze(d + 1)
                return ap.to_broadcast([P, PH, TOPK, TOPK])

            for b in range(TB):
                for g in range(4):
                    n = 4 * b + g
                    dve.wait_ge(key_scored, n + 1)
                    for j in range(4):
                        s = 4 * g + j
                        top16(wk[:, n % 4, j * P:(j + 1) * P], s2[:], val[:, s], idx[:, s])
                    v.engine_nop().then_inc(key_read, 1)
                chain(v.tensor_copy(idxf[:], idx[:]))
                sides = val[:].rearrange("p (h s) k -> p h s k", s=2)
                chain(v.tensor_tensor(cand[:].rearrange("p h (a b) -> p h a b", a=TOPK), spread(sides[:, :, 0], (0, 1)),
                                      spread(sides[:, :, 1], (0, 2)), ALU.add))
                wait(dve, keys_turned, b)
                for i in range(PH):
                    top16(cand[:, i], c2[:], best[:, i], pick[:, 0, i])
                v.tensor_single_scalar(pick[:, 1], pick[:, 0], 4, ALU.logical_shift_right).then_inc(step, 1)
                done[0] += 1
                chain(v.tensor_single_scalar(pick[:, 2], pick[:, 0], TOPK - 1, ALU.bitwise_and))
                chain(v.tensor_copy(pickf[:], pick[:, 1:3]))
                ids = idxf[:].rearrange("p (h s) k -> p h s k", s=2)
                for s in range(2):
                    chain(v.tensor_tensor(eq[:], spread(pickf[:, s], (0, 1)), spread(iota16, (2,)), ALU.is_equal))
                    chain(v.tensor_tensor(eq[:], eq[:], spread(ids[:, :, s], (0, 2)), ALU.mult))
                    chain(v.tensor_reduce(key[:, s], eq[:], AX, ALU.add))
                chain(v.tensor_copy(soft[:, 0], best[:, :, 0]))
                v.tensor_tensor(best[:], best[:], soft[:, 0].unsqueeze(2).to_broadcast([P, PH, TOPK]), ALU.subtract
                                ).then_inc(best_sub, 1)
                dve.wait_ge(best_exp, b + 1)
                chain(v.tensor_reduce(soft[:, 0], key[:, 2], AX, ALU.add))
                chain(v.reciprocal(soft[:, 1], soft[:, 0]))
                v.tensor_tensor(key[:, 2], key[:, 2], soft[:, 1].unsqueeze(2).to_broadcast([P, PH, TOPK]), ALU.mult
                                ).then_inc(keys_ready, 1)
            dve.wait_ge(i_ready, TB)

            def one_hot(g, par, first):
                wait(dve, hot_used, g - 1 if not first else 0)
                for j in range(4):
                    def column(s):
                        return i_t[:, s, bass.ds(g * 4 + j, 1)]
                    v.tensor_scalar(hot[:, par, 0, j], const("iota"), column(0), column(2), ALU.is_equal, ALU.mult)
                    ins = v.tensor_scalar(hot[:, par, 1, j], const("iota"), column(1), None, ALU.is_equal)
                ins.then_inc(hot_ready, 1)

            one_hot(0, 0, True)
            one_hot(1, 1, True)
            with dve.Fori(1, T // 8) as i:
                for par in range(2):
                    one_hot(i * 2 + par, par, False)

            p0 = FIRST["peer"]
            dve.wait_ge(gates_kept, T // 4)

            def weigh(i):
                dve.wait_ge(act_ready, i + 1)
                wait(dve, w_lo, i)
                wait(dve, w_hi, i)
                g = gates[:, :, bass.ds(i, 1)].rearrange("p t a -> p (t a)")
                v.tensor_tensor(w32[:], act[:], g, ALU.mult).then_inc(w_ready, 1)

            def rest(i, k):
                dve.wait_ge(w_hi, i + 1)
                v.tensor_tensor(pl[:, k], w32[:], ph[:, k].bitcast(F32), ALU.subtract).then_inc(w_lo, 1)

            ahead(block_no(p0))
            weigh(0)

            def pair(i, k, blk):
                rest(i, k)
                ahead(blk)
                weigh(i + 1)
                ahead(after(blk, 1))

            pair(0, 0, block_no(p0 + 1))
            with dve.Fori(0, (NK - 2) // RING - 1) as t:
                for k in range(RING):
                    pair(t * RING + (1 + k), (1 + k) % RING, block_no(p0 + 3 + 2 * k, t, 2))
            for i in range(NK - 1 - RING, NK - 1):
                pair(i, i % RING, block_no(p0 + 1 + 2 * i))
            rest(NK - 1, (NK - 1) % RING)
            used(block_no(BLOCKS - 1))
            for c in range(DC):
                v.scalar_tensor_tensor(out=h[:, c], in0=acc_tile(c), scalar=mod[:, 5 * DC + c:5 * DC + c + 1], in1=h[:, c],
                                       op0=ALU.mult, op1=ALU.add).then_inc(res_add, 1)
            norm("final2", h, dst=(gain_of("final2"), sq))


def pieces(w):
    k, n = w.shape
    return w.reshape(k // P, P, n // P, P).transpose(2, 1, 0, 3).reshape(n // P, P, (k // P) * P)


def padded(w, width):
    return np.concatenate([w, np.zeros(w.shape[:2] + (width - w.shape[2],), np.float32)], axis=2)


def kernel(x, positions, conv_norm_g, conv_w_in, conv_w, conv_w_out, conv_ffn_norm_g, conv_ffn_w13, conv_ffn_w2,
           kv_norm_g, w_dkv, kv_latent_norm_g, w_ukv, mla_norm_g, mla_w_dq, mla_q_norm_g, mla_w_uq, mla_w_o,
           mla_ffn_norm_g, mla_ffn_w13, mla_ffn_w2, final_norm_g, c_2, w_ada_2, b_ada_2, norm1_g_2, w_in_2, conv_w_2,
           conv_b_2, b_igate_2, b_fgate_2, rel_bias_2, mlstm_norm_g_2, w_branch_a_2, w_branch_b_2, w_out_2, norm2_g_2,
           w_peer_q_2, peer_sub_keys_2, peer_u_2, peer_v_2, final_g_2):
    import concourse.bacc as bacc
    from concourse.bass_utils import run_bass_kernel_spmd

    f = np.asarray
    blocks = []

    w = pieces(f(conv_w_in)[0]).reshape(3, DC, P, 1024)
    blocks.append(w[[1, 2, 0]].transpose(1, 0, 2, 3).reshape(-1, P, 1024))
    blocks.append(pieces(f(conv_w_out)[0]))

    def ffn(w13, w2):
        gu = pieces(f(w13)[0]).reshape(2, FT, P, 1024)
        o = f(w2)[0].reshape(FT, P, D)
        order = [gu[0, 0], gu[1, 0]]
        for j in range(1, FT):
            order += [gu[0, j], gu[1, j], o[j - 1]]
        return np.stack(order + [o[FT - 1]])

    blocks.append(ffn(conv_ffn_w13, conv_ffn_w2))
    dkv = f(w_dkv)
    half = ROPE // 2
    x1, x2 = dkv[:, KVR:KVR + half], dkv[:, KVR + half:]
    blocks.append(pieces(np.concatenate([dkv[:, :KVR]] + [x1] * 4 + [x2] * 4 + [f(mla_w_dq)[0]], axis=1)))
    uq = f(mla_w_uq)[0].reshape(QR, HEADS, NOPE + ROPE)
    uq = np.concatenate([uq[:, :, :NOPE].reshape(QR, -1), uq[:, :, NOPE:NOPE + half].reshape(QR, -1),
                         uq[:, :, NOPE + half:].reshape(QR, -1)], axis=1)
    uq = pieces(uq).reshape(6, 2, P, QC * P).transpose(0, 2, 1, 3).reshape(6, P, 2 * QC * P)
    blocks.append(padded(uq, 1024))
    ukv = f(w_ukv).reshape(KC, P, HEADS, 2, NOPE)
    ukv = ukv.transpose(3, 2, 1, 0, 4).reshape(2, 2, 4, P, KC, NOPE)
    blocks.append(ukv.transpose(0, 1, 3, 4, 2, 5).reshape(4, P, 1024))
    blocks.append(pieces(f(mla_w_o)[0]))
    blocks.append(ffn(mla_ffn_w13, mla_ffn_w2))
    win = f(w_in_2)[0]
    sizes = [512, 512, 512, 1024, 512, 512, BH, BH, D, D]
    qa, ka, va, qkb, vb, ob, ib, fb, ga, gb = np.split(win, np.cumsum(sizes)[:-1], axis=1)
    gate = np.concatenate([ib, fb, np.zeros((D, P - 2 * BH), np.float32)], axis=1)
    blocks.append(pieces(np.concatenate([gate, qkb, vb, va, qa, ka, ob, ga, gb], axis=1)))
    blocks.append(np.concatenate([pieces(f(w_branch_a_2)[0]), pieces(f(w_branch_b_2)[0])], axis=2))
    blocks.append(pieces(f(w_out_2)[0]))
    blocks.append(pieces(f(w_peer_q_2)[0]))
    pu = f(peer_u_2)[0].reshape(NK, NK, DC, P).transpose(0, 3, 2, 1).reshape(NK, P, 1024)
    pv = f(peer_v_2)[0].reshape(NK, NK, D)
    pairs = np.stack([pu[1:], pv[:-1]], axis=1).reshape(-1, P, 1024)
    blocks += [pu[:1], pairs, pv[-1:]]
    stream = np.concatenate(blocks)
    del blocks, pu, pairs
    assert stream.shape == (BLOCKS, P, 1024)

    def column(a):
        return f(a).reshape(-1, P).T

    inv_freq = (np.float32(10000.0) ** (-np.arange(0, ROPE, 2, dtype=np.float32) / np.float32(ROPE))).astype(np.float32)
    gains = np.concatenate(
        [column(a) for a in (conv_norm_g, conv_ffn_norm_g, kv_norm_g, mla_norm_g, kv_latent_norm_g, mla_q_norm_g,
                             mla_ffn_norm_g, final_norm_g, norm1_g_2, norm2_g_2, final_g_2, mlstm_norm_g_2, c_2, b_ada_2)]
        + [f(conv_w)[0].reshape(CW, DC, P).transpose(2, 1, 0).reshape(P, -1),
           f(conv_w_2)[0].reshape(CK, 2 * BH, P).transpose(2, 1, 0).reshape(P, -1), column(conv_b_2),
           np.tile(inv_freq, 4)[:, None]], axis=1).astype(np.float32)

    i = np.arange(P)
    tri = np.where(i[None, :] <= i[:, None], 0.0, NEG)
    past = (i[None, :] < i[:, None]).astype(np.float32)
    one, zero = np.ones((P, 1)), np.zeros((P, P))
    consts = np.concatenate([np.eye(P), np.tile(i, (P, 1)), tri, zero, tri, np.ones((P, P)),
                             i[:, None] <= i[None, :], one, past, one, np.ones((P, P)), past], axis=1).astype(np.float32)

    q, k = np.arange(T)[:, None], np.arange(T)[None, :]
    rel = np.clip(q - k, -CLIP, CLIP) + CLIP
    band = f(rel_bias_2)[0][:, rel]
    band = np.where((k // CHUNK > q // CHUNK)[None], np.float32(NEG), band)
    band = np.concatenate([band[:, :P, :P], band[:, P:]], axis=2).transpose(1, 0, 2)
    gate_bias = np.tile(np.concatenate([f(b_igate_2)[0], f(b_fgate_2)[0]])[None], (P, 1))
    sub_keys = f(peer_sub_keys_2)[0].reshape(2 * PH, NK, P).transpose(2, 0, 1)
    x_in = f(x)[0].reshape(T, DC, P).transpose(2, 1, 0)

    arrays = {"stream": stream, "ada": f(w_ada_2)[0], "gains": gains, "consts": consts, "positions": f(positions),
              "x_in": x_in, "band_bias": band, "gate_bias": gate_bias, "sub_keys": sub_keys}
    arrays = {n: np.ascontiguousarray(a) for n, a in arrays.items()}
    nc = bacc.Bacc("TRN2", target_bir_lowering=False, num_devices=1)
    aps = {n: nc.dram_tensor(n, a.shape, mybir.dt.from_np(a.dtype), kind="ExternalInput").ap() for n, a in arrays.items()}
    aps["positions"] = aps["positions"][0]
    out = nc.dram_tensor("out", (P, DC, T), F32, kind="ExternalOutput").ap()
    build(nc, out=out, **aps)
    r = run_bass_kernel_spmd(nc, [arrays], core_ids=[0])
    return r.results[0]["out"].transpose(2, 1, 0).reshape(1, T, D)
```

```python
from contextlib import ExitStack

import numpy as np

import concourse.bass as bass
from concourse import mybir

ALU = mybir.AluOpType
ACT = mybir.ActivationFunctionType
F32 = mybir.dt.float32
F32R = mybir.dt.float32r
U32 = mybir.dt.uint32
I32 = mybir.dt.int32
AX = mybir.AxisListType.X

P = 128
T = 256
TB = T // P
D = 1024
DC = D // P
FF = 2816
FT = FF // P
HEADS = 8
NOPE, ROPE = 128, 64
KVR, QR = 256, 384
KC, QC = KVR // P, QR // P
EPS = 1e-6
MLA_SCALE = float(NOPE + ROPE) ** -0.5
CW = 3
CK = 4
AH, AHD = 8, 64
BH, BD = 4, 128
CHUNK, CLIP = 64, 128
PH, NK, TOPK = 8, 128, 16
NEG = -1e30
LOWEST = -3e38
ROUND = 12582912.0
TWO_PI_PARTS = (6.28125, 1.935303211212158203125e-3, 3.9683743166540886e-09)
PI_BELOW = 3.1415925

RING = 3
LEAD = 2

STAGES = [("conv_in", 3 * DC), ("conv_out", DC), ("ffn1", 3 * FT), ("latent", 7), ("uq", 6), ("ukv", 4),
          ("attn_out", DC), ("ffn2", 3 * FT), ("proj", 45), ("branch", DC), ("mix_out", DC),
          ("peer_q", 2 * PH), ("peer", 2 * NK)]
FIRST = {}
BLOCKS = 0
for _name, _count in STAGES:
    FIRST[_name] = BLOCKS
    BLOCKS += _count

NORMS = [("conv", DC, 1), ("ffn1", DC, 1), ("mla", DC, 2), ("qlat", QC, 1), ("kvlat", KC, 1), ("ffn2", DC, 1),
         ("final", DC, 0), ("mix", DC, 1), ("peer", DC, 1), ("final2", DC, 0)]
NORM_NO = {n: i for i, (n, _, _) in enumerate(NORMS)}

GAIN = {}
GAINS = 0
for _name, _count in [("conv", DC), ("ffn1", DC), ("kv", DC), ("mla", DC), ("kvlat", KC), ("qlat", QC), ("ffn2", DC),
                      ("final", DC), ("norm1", DC), ("norm2", DC), ("final2", DC), ("mlstm", BH), ("c", DC),
                      ("b_ada", 6 * DC), ("conv_w", CW * DC), ("conv2_w", CK * 2 * BH), ("conv2_b", 2 * BH),
                      ("inv_freq", 1)]:
    GAIN[_name] = GAINS
    GAINS += _count


def block_no(const, trip=None, per_trip=1):
    return (const, trip, per_trip)


def number(block):
    const, trip, per_trip = block
    return const if trip is None else const + trip * (RING * per_trip)


def lap(block):
    const, trip, per_trip = block
    return const // RING if trip is None else const // RING + trip * per_trip


def after(block, k):
    return (block[0] + k,) + block[1:]


def wait(eng, sem, value):
    if isinstance(value, int) and value <= 0:
        return
    eng.wait_ge(sem, value)



CONST = {}
CONSTS = 0
for _name, _count in [("ident", P), ("iota", P), ("mask", 3 * P), ("ones", P), ("upto", P), ("past0", P + 1),
                      ("past1", 2 * P + 1)]:
    CONST[_name] = (CONSTS, CONSTS + _count)
    CONSTS += _count


def build(nc, stream, ada, gains, consts, positions, x_in, band_bias, gate_bias, sub_keys, out):
    with ExitStack() as ctx:
        place = [(nc.sbuf_base + 63) // 64 * 64]

        def sem(name):
            return ctx.enter_context(nc.semaphore(name))

        def sb(name, shape, dt=F32):
            t = nc.alloc_sbuf_tensor_at(name, shape, dt, offset=place[0])
            place[0] += (int(np.prod(shape[1:])) * 4 + 31) // 32 * 32
            assert place[0] <= nc.sbuf_usable_end, (name, place[0])
            return t

        h = sb("h", [P, DC, T])
        xh = sb("xh", [P, DC, T], F32R)
        xl = sb("xl", [P, DC, T], F32R)
        raw = sb("raw", [P, RING, 1024])
        wh = sb("wh", [P, RING, 1024], F32R)
        wl = sb("wl", [P, RING, 1024], F32R)
        gv = sb("gv", [P, GAINS])
        mod = sb("mod", [P, 6 * DC])
        modg = sb("modg", [P, 2, DC])
        cst = sb("cst", [P, CONSTS])
        cols = sb("cols", [P, 4])
        csilu = sb("csilu", [P, DC])
        sd = sb("sd", [P, T])
        rs = sb("rs", [P, T])
        i_t = sb("i_t", [P, 3, T])
        peer_at = place[0]
        act = sb("act", [P, T])
        w32 = sb("w32", [P, T])
        ph = sb("ph", [P, RING, T], F32R)
        pl = sb("pl", [P, RING, T], F32R)
        arena = (place[0] + 63) // 64 * 64
        place[0] = peer_at
        hot = sb("hot", [P, 2, 2, 4, P])
        place[0] = max(arena, place[0])
        gates = sb("gates", [P, T, NK])

        place[0] = arena
        yh = sb("yh", [P, DC, T], F32R)
        yl = sb("yl", [P, DC, T], F32R)
        sq = sb("sq", [P, DC, T])
        ada_acc = sb("ada_acc", [P, 6, D])
        ada_w = sb("ada_w", [P, 2, D])
        ada_p = sb("ada_p", [P, D])
        shared = place[0]
        place[0] = arena + 2 * 8192
        sc = sb("sc", [P, 2, T])
        pr = sb("pr", [P, 2, T])
        pt = sb("pt", [P, 2, 3 * P])
        stat = sb("stat", [P, 4, 2 * AH])

        place[0] = shared
        z = sb("z", [P, T + CW - 1])
        gc = sb("gc", [P, T])
        cv = sb("cv", [P, 3, T])
        sg = sb("sg", [P, T])
        hid = sb("hid", [P, T])
        hidh = sb("hidh", [P, T], F32R)
        hidl = sb("hidl", [P, T], F32R)
        pos_i = sb("pos_i", [P, T], I32)
        ang = sb("ang", [P, 8, T])
        lat = sb("lat", [P, KC + QC, T])
        lath = sb("lath", [P, KC + QC, T], F32R)
        latl = sb("latl", [P, KC + QC, T], F32R)
        kpe = sb("kpe", [P, 2, T])
        qn = sb("qn", [P, HEADS, T])
        qpe = sb("qpe", [P, 2, 2, T])
        kn = sb("kn", [P, HEADS, T])
        vm = sb("vm", [P, TB, HEADS, NOPE])
        rt = sb("rt", [P, 2, 2 * T])
        place[0] = shared
        ga = sb("ga", [P, DC, T])
        gb = sb("gb", [P, DC, T])
        ob = sb("ob", [P, BH, T])
        qk = sb("qk", [P, 2 * BH, T])
        vb = sb("vb", [P, TB, BH, BD])
        va = sb("va", [P, TB, 4, P])
        qa = sb("qa", [P, 4, T])
        ka = sb("ka", [P, 4, T])
        gt = sb("gt", [P, TB, 2 * BH])
        gw = sb("gw", [P, TB, 3, BH])
        u = sb("u", [P, T + CK - 1])
        uc = sb("uc", [P, CK, T])
        rr = sb("rr", [P, TB, 2 * P + 1])
        dm = sb("dm", [P, 2 * P + 1])
        sv = sb("sv", [P, T])
        st = sb("st", [P, 3 * P])
        hb = sb("hb", [P, TB, BH, BD])
        ms = sb("ms", [P, 10, 2 * BH])
        place[0] = arena + 3 * 8192
        bias = sb("bias", [P, AH, 3 * P])
        sk = sb("sk", [P, 2 * PH, NK])
        gbias = sb("gbias", [P, 2 * BH])
        place[0] = arena
        qp = sb("qp", [P, 2 * PH, T])
        place[0] = shared
        s2 = sb("s2", [P, NK])
        val = sb("val", [P, 2 * PH, TOPK])
        idx = sb("idx", [P, 2 * PH, TOPK], U32)
        idxf = sb("idxf", [P, 2 * PH, TOPK])
        cand = sb("cand", [P, PH, TOPK * TOPK])
        c2 = sb("c2", [P, TOPK * TOPK])
        best = sb("best", [P, PH, TOPK])
        pick = sb("pick", [P, 3, PH, TOPK], U32)
        pickf = sb("pickf", [P, 2, PH, TOPK])
        eq = sb("eq", [P, PH, TOPK, TOPK])
        key = sb("key", [P, 3, PH, TOPK])
        soft = sb("soft", [P, 2, PH])

        wk = ctx.enter_context(nc.psum_tensor("wk", [P, 4, 512], F32))
        acc = ctx.enter_context(nc.psum_tensor("acc", [P, 4, 512], F32))

        def acc_tile(j):
            return acc[:, j // 2, (j % 2) * T:(j % 2 + 1) * T]

        raw_in = [sem(f"raw_in{i}") for i in range(RING)]
        hi_ready = sem("hi_ready")
        lo_ready = sem("lo_ready")
        block_used = sem("block_used")
        x_landed = [sem("x_landed0"), sem("x_landed1")]
        const_in = sem("const_in")
        band_in = sem("band_in")
        set_up = sem("set_up")
        squares = sem("squares")
        summed = sem("summed")
        rooted = sem("rooted")
        scaled = sem("scaled")
        normed_hi = sem("normed_hi")
        normed = sem("normed")
        gate_copied = sem("gate_copied")
        gated = sem("gated")
        conved = sem("conved")
        conved_hi = sem("conved_hi")
        conved_lo = sem("conved_lo")
        res_add = sem("res_add")
        silu_ready = sem("silu_ready")
        hid_ready = sem("hid_ready")
        hid_hi = sem("hid_hi")
        hid_lo = sem("hid_lo")
        lat_read = sem("lat_read")
        uq_read = sem("uq_read")
        ukv_read = sem("ukv_read")
        angles = sem("angles")
        trig = sem("trig")
        scored = sem("scored")
        masked = sem("masked")
        expd = sem("expd")
        probs = sem("probs")
        turned = sem("turned")
        pt_ready = sem("pt_ready")
        mixed = sem("mixed")
        mixed_hi = sem("mixed_hi")
        mixed_lo = sem("mixed_lo")
        ada_in = [sem("ada_in0"), sem("ada_in1")]
        csilu_ready = sem("csilu_ready")
        ada_scaled = sem("ada_scaled")
        ada_added = sem("ada_added")
        ada_done = sem("ada_done")
        mod_summed = sem("mod_summed")
        mod_ready = sem("mod_ready")
        proj_dve = sem("proj_dve")
        proj_act = sem("proj_act")
        sigmoids = sem("sigmoids")
        conv2 = sem("conv2")
        silu2 = sem("silu2")
        gate_exp = sem("gate_exp")
        gates_ready = sem("gates_ready")
        decays = sem("decays")
        decay_sums = sem("decay_sums")
        decay_max = sem("decay_max")
        decay_exp = sem("decay_exp")
        weighted = sem("weighted")
        w_turned = sem("w_turned")
        st_ready = sem("st_ready")
        m_mixed = sem("m_mixed")
        m_out = sem("m_out")
        m_sq = sem("m_sq")
        m_root = sem("m_root")
        m_normed = sem("m_normed")
        m_turned = sem("m_turned")
        m_gated = sem("m_gated")
        m_hi = sem("m_hi")
        m_lo = sem("m_lo")
        branch_sum = sem("branch_sum")
        branch_hi = sem("branch_hi")
        branch_lo = sem("branch_lo")
        qp_ready = sem("qp_ready")
        key_scored = sem("key_scored")
        key_read = sem("key_read")
        best_sub = sem("best_sub")
        best_exp = sem("best_exp")
        keys_ready = sem("keys_ready")
        keys_turned = sem("keys_turned")
        i_ready = sem("i_ready")
        hot_ready = sem("hot_ready")
        hot_used = sem("hot_used")
        gates_kept = sem("gates_kept")
        act_ready = sem("act_ready")
        w_ready = sem("w_ready")
        w_hi = sem("w_hi")
        w_lo = sem("w_lo")
        conv_step = sem("conv_step")
        step = sem("step")
        act_step = sem("act_step")
        out_sent = sem("out_sent")

        def const(name):
            a, b = CONST[name]
            return cst[:, a:b]

        def gain(name, k=0):
            return gv[:, GAIN[name] + k:GAIN[name] + k + 1]

        def squares_before(name):
            return sum(n for _, n, _ in NORMS[:NORM_NO[name]])

        def scaled_before(name):
            return sum(n * max(k, 1) for _, n, k in NORMS[:NORM_NO[name]])

        def normed_before(name):
            return sum(n * k for _, n, k in NORMS[:NORM_NO[name]])

        added = {name: i * DC for i, name in enumerate(["conv_out", "ffn1", "attn_out", "ffn2", "mix_out", "peer"])}

        def attention_base(kind):
            return 0 if kind == "latent" else HEADS

        block = ctx.enter_context(nc.Block())
        CONST_LOADS = 3

        @block.sync
        def _(sp):
            for half in range(2):
                sp.dma_start(h[:, half * 4:half * 4 + 4], x_in[:, half * 4:half * 4 + 4]).then_inc(x_landed[half], 16)
            for n in range(RING):
                sp.dma_start(raw[:, n], stream[n]).then_inc(raw_in[n], 16)
            with sp.Fori(1, BLOCKS // RING) as i:
                for k in range(RING):
                    sp.wait_ge(lo_ready, i * RING + (k - RING + 1))
                    sp.dma_start(raw[:, k], stream[bass.ds(i * RING + k, 1)].rearrange("a p n -> (a p) n")
                                 ).then_inc(raw_in[k], 16)
            for n in range(BLOCKS // RING * RING, BLOCKS):
                sp.wait_ge(lo_ready, n - RING + 1)
                sp.dma_start(raw[:, n % RING], stream[n]).then_inc(raw_in[n % RING], 16)
            sp.wait_ge(scaled, scaled_before("final2") + DC)
            sp.dma_start(out, sq[:]).then_inc(out_sent, 16)
            sp.wait_ge(out_sent, 16)

        @block.gpsimd
        def _(pool):
            pool.wait_ge(csilu_ready, 1)

            def load(n):
                part, k = divmod(n, DC)
                pool.dma_start(ada_w[:, n % 2], ada[k * P:(k + 1) * P, part * D:(part + 1) * D]).then_inc(ada_in[n % 2], 16)

            def load_next(n):
                if n + 2 < 6 * DC:
                    load(n + 2)

            load(0)
            load(1)
            for n in range(6 * DC):
                part, k = divmod(n, DC)
                pool.wait_ge(ada_in[n % 2], (n // 2 + 1) * 16)
                if k == 0:
                    pool.tensor_scalar(ada_acc[:, part], ada_w[:, n % 2], csilu[:, k:k + 1], None, ALU.mult
                                       ).then_inc(ada_scaled, 1)
                    pool.wait_ge(ada_scaled, n + 1)
                    load_next(n)
                else:
                    wait(pool, ada_added, part * (DC - 1) + k - 1)
                    pool.tensor_scalar(ada_p[:], ada_w[:, n % 2], csilu[:, k:k + 1], None, ALU.mult
                                       ).then_inc(ada_scaled, 1)
                    pool.wait_ge(ada_scaled, n + 1)
                    load_next(n)
                    pool.tensor_tensor(ada_acc[:, part], ada_acc[:, part], ada_p[:], ALU.add).then_inc(ada_added, 1)
            pool.wait_ge(ada_added, 6 * (DC - 1))
            pool.wait_ge(mod_summed, 1)
            pool.dma_start(bias[:], band_bias).then_inc(band_in, 16)
            pool.dma_start(sk[:], sub_keys).then_inc(band_in, 16)
            pool.dma_start(gbias[:], gate_bias).then_inc(band_in, 16)

        @block.tensor
        def _(pe):
            def three(out_ap, a_hi, a_lo, b_hi, b_lo, start, stop, skip=False):
                pe.matmul(out_ap, a_hi, b_hi, start=start, stop=False, skip_group_check=skip)
                pe.matmul(out_ap, a_hi, b_lo, start=False, stop=False, skip_group_check=skip)
                return pe.matmul(out_ap, a_lo, b_hi, start=False, stop=stop, skip_group_check=skip)

            def ready(blk):
                pe.wait_ge(lo_ready, number(blk) + 1)

            def piece(w, blk, lo, hi):
                return w[:, blk[0] % RING, lo:hi]

            def features(blk, bank, ah, al, first_wait=None):
                ready(blk)
                for c in range(DC):
                    if first_wait is not None:
                        pe.wait_ge(normed, first_wait + c + 1)
                    mm = three(wk[:, bank, 0:T], piece(wh, blk, c * P, c * P + P), piece(wl, blk, c * P, c * P + P),
                               ah[:, c], al[:, c], c == 0, c == DC - 1)
                mm.then_inc(block_used, 1)

            def tokens(blk, bank, ah, al, n, first_wait=None):
                ready(blk)
                if first_wait is not None:
                    pe.wait_ge(normed, first_wait + DC)
                for b in range(TB):
                    for c in range(DC):
                        mm = three(wk[:, bank, b * P:b * P + n], ah[:, c, b * P:(b + 1) * P], al[:, c, b * P:(b + 1) * P],
                                   piece(wh, blk, c * P, c * P + n), piece(wl, blk, c * P, c * P + n), c == 0, c == DC - 1)
                mm.then_inc(block_used, 1)

            def norm_sum(name, c):
                if c == 0:
                    wait(pe, rooted, NORM_NO[name])
                    if name == "ffn2":
                        pe.wait_ge(mod_ready, 1)
                pe.wait_ge(squares, squares_before(name) + c + 1)
                n = NORMS[NORM_NO[name]][1]
                mm = pe.matmul(wk[:, 3, 0:T], const("ones"), sq[:, c], start=c == 0, stop=c == n - 1)
                if c == n - 1:
                    mm.then_inc(summed, 1)

            def norm_sums(name, first=0):
                for c in range(first, NORMS[NORM_NO[name]][1]):
                    norm_sum(name, c)

            pe.wait_ge(const_in, 16 * CONST_LOADS)
            norm_sums("conv")

            def conv_tile(c, blk, first):
                wait(pe, gate_copied, c)
                features(blk, 0, xh, xl, normed_before("conv") if first else None)
                wait(pe, gated, c)
                features(after(blk, 1), 1, xh, xl)
                wait(pe, conved, c)
                features(after(blk, 2), 2, xh, xl)

            conv_tile(0, block_no(0), True)
            with pe.Fori(1, DC) as c:
                conv_tile(c, block_no(0, c), False)

            def add_out(stage, ah, al, done, count, norm):
                for c in range(DC):
                    blk = block_no(FIRST[stage] + c)
                    if c == 0:
                        pe.wait_ge(done, count)
                    wait(pe, res_add, added[stage] + c - 2 if c >= RING else 0)
                    features(blk, blk[0] % RING, ah, al)
                    if c >= 2:
                        norm_sum(norm, c - 2)
                norm_sums(norm, DC - 2)

            add_out("conv_out", yh, yl, conved_lo, DC, "ffn1")

            def ffn(stage, norm, turn):
                first = FIRST[stage]
                base = turn * FT

                def w2(blk, j, start, stop):
                    ready(blk)
                    pe.wait_ge(hid_lo, base + j + 1)
                    for o in range(DC):
                        mm = three(acc_tile(o), piece(wh, blk, o * P, o * P + P), piece(wl, blk, o * P, o * P + P),
                                   hidh[:], hidl[:], start and o % 2 == 0, stop, skip=True)
                    mm.then_inc(block_used, 1)

                b0 = first % RING
                features(block_no(first), b0, xh, xl, normed_before(norm))
                features(block_no(first + 1), (b0 + 1) % RING, xh, xl)

                def triple(j, blk, start):
                    pe.wait_ge(silu_ready, base + j)
                    features(blk, b0, xh, xl)
                    pe.wait_ge(hid_ready, base + j)
                    features(after(blk, 1), (b0 + 1) % RING, xh, xl)
                    w2(after(blk, 2), j - 1, start, False)

                triple(1, block_no(first + 2), True)
                with pe.Fori(2, FT) as j:
                    triple(j, block_no(first - 1, j), False)
                w2(block_no(first + 3 * FT - 1), FT - 1, False, True)

            ffn("ffn1", "ffn1", 0)

            norm_sums("mla")
            base = normed_before("mla")
            for k in range(7):
                blk = block_no(FIRST["latent"] + k)
                wait(pe, lat_read, k - 2)
                if k == 0:
                    features(blk, blk[0] % RING, xh, xl, base)
                elif k < 4:
                    features(blk, blk[0] % RING, xh, xl)
                elif k == 4:
                    features(blk, blk[0] % RING, yh, yl, base + DC)
                else:
                    features(blk, blk[0] % RING, yh, yl)
            norm_sums("qlat")
            norm_sums("kvlat")

            pe.wait_ge(normed, normed_before("qlat") + QC)
            for k in range(6):
                blk = block_no(FIRST["uq"] + k)
                wait(pe, uq_read, k - 2)
                ready(blk)
                for t in range(2):
                    for c in range(QC):
                        at = (t * QC + c) * P
                        mm = three(wk[:, k % RING, t * T:(t + 1) * T], piece(wh, blk, at, at + P), piece(wl, blk, at, at + P),
                                   lath[:, KC + c], latl[:, KC + c], c == 0, c == QC - 1)
                mm.then_inc(block_used, 1)
            pe.wait_ge(normed, normed_before("kvlat") + KC)
            pe.wait_ge(uq_read, 6)
            for k in range(4):
                blk = block_no(FIRST["ukv"] + k)
                wait(pe, ukv_read, k - 1)
                ready(blk)
                b = 2 * (k % 2)
                if k < 2:
                    for t in range(4):
                        for c in range(KC):
                            at = c * 512 + t * P
                            mm = three(wk[:, b + t // 2, (t % 2) * T:(t % 2 + 1) * T], piece(wh, blk, at, at + P),
                                       piece(wl, blk, at, at + P), lath[:, c], latl[:, c], c == 0, c == KC - 1)
                else:
                    for t in range(TB):
                        for c in range(KC):
                            mm = three(wk[:, b + t], lath[:, c, t * P:(t + 1) * P], latl[:, c, t * P:(t + 1) * P],
                                       piece(wh, blk, c * 512, c * 512 + 512), piece(wl, blk, c * 512, c * 512 + 512),
                                       c == 0, c == KC - 1)
                mm.then_inc(block_used, 1)

            def attention(kind, beside):
                h0 = attention_base(kind)

                def scores(i):
                    if kind == "band":
                        pe.wait_ge(masked, TB * (h0 + i))
                        r = AHD * (i % 2)
                        for b in range(TB):
                            mm = pe.matmul(wk[:, 3, b * P:b * P + (b + 1) * P], qa[r:r + AHD, i // 2, b * P:(b + 1) * P],
                                           ka[r:r + AHD, i // 2, 0:(b + 1) * P], start=True, stop=True)
                        mm.then_inc(scored, TB)
                        return
                    for b in range(TB):
                        n = (b + 1) * P
                        unit = TB * (h0 + i) + b
                        wait(pe, masked, unit - 2)
                        bank = wk[:, unit % 3, 0:n]
                        r = 32 * (i % 4)
                        pe.matmul(bank, qn[:, i, b * P:(b + 1) * P], kn[:, i, 0:n], start=True, stop=False)
                        for s in range(2):
                            mm = pe.matmul(bank, qpe[r:r + 32, s, i // 4, b * P:(b + 1) * P], kpe[r:r + 32, s, 0:n],
                                           start=False, stop=s == 1, tile_position=(r, 0))
                        mm.then_inc(scored, 1)

                def turn(i):
                    n = h0 + i
                    wait(pe, pt_ready, n - 1)
                    for b in range(TB):
                        pe.wait_ge(probs, TB * n + b + 1)
                        for k in range(b + 1):
                            at = (b + k) * P
                            mm = pe.transpose(acc[:, n % 2, at:at + P], pr[:, b, k * P:(k + 1) * P], const("ident"))
                    mm.then_inc(turned, 1)

                def mix(i):
                    n = h0 + i
                    pe.wait_ge(pt_ready, n + 1)
                    if kind == "latent":
                        wait(pe, mixed_lo, i - 1)
                        o = acc[:, 2 + n % 2, 0:T]
                        pe.matmul(o, vm[:, 0, i], pt[:, n % 2, 0:T], start=True, stop=False, skip_group_check=True)
                        pe.matmul(acc[:, 2 + n % 2, P:T], vm[:, 1, i], pt[:, n % 2, T:3 * P], start=False, stop=True,
                                  skip_group_check=True).then_inc(mixed, 1)
                    else:
                        r = AHD * (i % 2)
                        bank = 2 + (i // 2) % 2
                        wait(pe, mixed_lo, HEADS + i // 2 - 1 if i >= 4 else 0)
                        for t in range(TB):
                            mm = pe.matmul(acc[r:r + AHD, bank, t * P:T], va[:, t, i // 2, r:r + AHD],
                                           pt[:, n % 2, 2 * t * P:2 * t * P + T - t * P],
                                           start=t == 0, stop=t == 1, skip_group_check=True)
                        mm.then_inc(mixed, 1)

                scores(0)
                for i in range(HEADS):
                    if kind == "band":
                        beside(i, 0)
                    if i + 1 < HEADS:
                        scores(i + 1)
                    turn(i)
                    if kind == "band":
                        beside(i, 1)
                    else:
                        beside(i)
                    if i >= 1:
                        mix(i - 1)
                mix(HEADS - 1)

            pe.wait_ge(ukv_read, 4)
            pe.wait_ge(trig, 3)
            pe.wait_ge(ada_added, 6 * (DC - 1))

            def mod_sums(i):
                for j in range(6 * i, 6 * i + 6):
                    mm = pe.matmul(wk[:, 3, j:j + 1], ada_acc[:, j // DC, (j % DC) * P:(j % DC + 1) * P],
                                   const("ones")[:, 0:1], start=True, stop=True)
                if i == HEADS - 1:
                    mm.then_inc(mod_summed, 1)

            attention("latent", mod_sums)
            add_out("attn_out", yh, yl, mixed_lo, HEADS, "ffn2")
            ffn("ffn2", "ffn2", 1)
            norm_sums("final")

            norm_sums("mix")
            pe.wait_ge(mod_ready, 1)
            base = normed_before("mix")
            def proj(k):
                blk = block_no(FIRST["proj"] + k)
                bank = blk[0] % RING
                if k == 0:
                    tokens(blk, bank, xh, xl, 2 * BH, base)
                elif 9 <= k < 17:
                    s = (k - 9) % 4
                    ready(blk)
                    if k == 9:
                        pe.wait_ge(proj_dve, 9)
                    elif s == 0:
                        pe.wait_ge(proj_act, 1)
                    for b in range(TB):
                        for c in range(2):
                            mm = three(wk[:, b], xh[:, 2 * s + c, b * P:(b + 1) * P], xl[:, 2 * s + c, b * P:(b + 1) * P],
                                       piece(wh, blk, c * 512, c * 512 + 512), piece(wl, blk, c * 512, c * 512 + 512),
                                       s == 0 and c == 0, s == 3 and c == 1)
                    mm.then_inc(block_used, 1)
                else:
                    if 17 <= k < 20:
                        pe.wait_ge(proj_act, 2)
                    elif k >= 20:
                        pe.wait_ge(proj_act, k - 17)
                    elif k > RING:
                        pe.wait_ge(proj_dve, k - RING + 1)
                    features(blk, bank, xh, xl)

            for k in range(13):
                proj(k)

            pe.wait_ge(silu2, 2 * BH)

            def m_scores(unit):
                i, b = divmod(unit, TB)
                n = (b + 1) * P
                pe.wait_ge(decays, i + 1)
                if b == 0:
                    pe.matmul(acc[:, 0, 0:P + 1], const("upto"), rr[:, 0, 0:P + 1], start=True, stop=True)
                else:
                    pe.matmul(acc[:, 0, 0:T + 1], const("upto"), rr[:, 1], start=True, stop=False, skip_group_check=True)
                    pe.matmul(acc[:, 0, 0:P + 1], const("ones"), rr[:, 0, 0:P + 1], start=False, stop=True,
                              skip_group_check=True)
                pe.matmul(acc[:, 1, 0:n], qk[:, i, b * P:n], qk[:, BH + i, 0:n], start=True, stop=True
                          ).then_inc(decay_sums, 1)

            m_scores(0)
            for unit in range(TB * BH):
                i, b = divmod(unit, TB)
                proj(13 + 2 * unit)
                pe.wait_ge(weighted, unit + 1)
                for k in range(b + 1):
                    mm = pe.transpose(acc[:, 2, k * P:(k + 1) * P], sv[:, k * P:(k + 1) * P], const("ident"))
                mm.then_inc(w_turned, 1)
                if unit + 1 < TB * BH:
                    m_scores(unit + 1)
                proj(14 + 2 * unit)
                if unit == 0:
                    pe.wait_ge(proj_act, 1)
                pe.wait_ge(st_ready, unit + 1)
                wait(pe, m_out, unit)
                for k in range(b + 1):
                    mm = pe.matmul(acc[:, 3, 0:P], st[:, k * P:(k + 1) * P], vb[:, k, i], start=k == 0, stop=k == b)
                mm.then_inc(m_mixed, 1)
            proj(29)
            pe.wait_ge(m_normed, 1)
            for i in range(BH):
                wait(pe, m_gated, i - 1)
                for b in range(TB):
                    mm = pe.transpose(acc[:, i % 2, b * P:(b + 1) * P], hb[:, b, i], const("ident"))
                mm.then_inc(m_turned, 1)

            pe.wait_ge(m_gated, BH)

            def two_more(i, half):
                if 30 + 2 * i + half < 45:
                    proj(30 + 2 * i + half)

            attention("band", two_more)
            pe.wait_ge(mixed_lo, HEADS + AH // 2)
            pe.wait_ge(m_lo, BH)
            pe.wait_ge(proj_act, 30)
            for k in range(DC):
                blk = block_no(FIRST["branch"] + k)
                ready(blk)
                wait(pe, branch_sum, k - 1)
                for s in range(2):
                    for c in range(4):
                        at = (4 * s + c) * P
                        mm = three(wk[:, 2 * (k % 2) + s, 0:T], piece(wh, blk, at, at + P), piece(wl, blk, at, at + P),
                                   yh[:, 4 * s + c], yl[:, 4 * s + c], c == 0, c == 3)
                mm.then_inc(block_used, 1)
            add_out("mix_out", xh, xl, branch_lo, DC, "peer")

            base = normed_before("peer")
            for k in range(2 * PH):
                blk = block_no(FIRST["peer_q"] + k)
                wait(pe, qp_ready, k - 2)
                features(blk, blk[0] % RING, xh, xl, base if k == 0 else None)
            pe.wait_ge(qp_ready, 2 * PH)
            pe.wait_ge(band_in, 48)
            for b in range(TB):
                for g in range(4):
                    n = 4 * b + g
                    wait(pe, key_read, n - 3)
                    for j in range(4):
                        mm = pe.matmul(wk[:, n % 4, j * P:(j + 1) * P], qp[:, 4 * g + j, b * P:(b + 1) * P], sk[:, 4 * g + j],
                                       start=True, stop=True)
                    mm.then_inc(key_scored, 1)
            for b in range(TB):
                pe.wait_ge(keys_ready, b + 1)
                for s in range(3):
                    mm = pe.transpose(acc[:, b, s * P:(s + 1) * P], key[:, s].rearrange("p h k -> p (h k)"), const("ident"))
                mm.then_inc(keys_turned, 1)
            def gate_group(g, par, first):
                pe.wait_ge(hot_ready, g + 1)
                wait(pe, gates_kept, g - 1 if not first else 0)
                for j in range(4):
                    mm = pe.matmul(wk[:, par, j * P:(j + 1) * P], hot[:, par, 1, j], hot[:, par, 0, j], start=True, stop=True)
                mm.then_inc(hot_used, 1)

            gate_group(0, 0, True)
            gate_group(1, 1, True)
            with pe.Fori(1, T // 8) as i:
                for par in range(2):
                    gate_group(i * 2 + par, par, False)
            p0 = FIRST["peer"]

            def experts_in(blk, bank):
                features(blk, bank, xh, xl)

            def experts_out(blk, i, k, start, stop):
                ready(blk)
                pe.wait_ge(w_lo, i + 1)
                for o in range(DC):
                    mm = three(acc_tile(o), piece(wh, blk, o * P, o * P + P), piece(wl, blk, o * P, o * P + P),
                               ph[:, k], pl[:, k], start and o % 2 == 0, stop, skip=True)
                mm.then_inc(block_used, 1)

            pe.wait_ge(gates_kept, T // 4)
            experts_in(block_no(p0), 0)

            def pair(i, k, blk, start):
                wait(pe, act_ready, i)
                experts_in(blk, (k + 1) % RING)
                experts_out(after(blk, 1), i, k, start, False)

            pair(0, 0, block_no(p0 + 1), True)
            with pe.Fori(0, (NK - 2) // RING) as t:
                for k in range(RING):
                    pair(t * RING + (1 + k), (1 + k) % RING, block_no(p0 + 3 + 2 * k, t, 2), False)
            experts_out(block_no(p0 + 2 * NK - 1), NK - 1, (NK - 1) % RING, False, True)
            norm_sums("final2")

        @block.scalar
        def _(sc_e):
            def hi(blk):
                n = number(blk)
                sc_e.wait_ge(raw_in[blk[0] % RING], (lap(blk) + 1) * 16)
                wait(sc_e, block_used, n - (RING - 1))
                nc.scalar.activation(wh[:, blk[0] % RING], raw[:, blk[0] % RING], ACT.Copy).then_inc(hi_ready, 1)

            def ahead(blk):
                if blk[1] is None and blk[0] + LEAD >= BLOCKS:
                    return
                hi(after(blk, LEAD))

            def used(blk):
                sc_e.wait_ge(block_used, number(blk) + 1)

            def square(name, c, src, src_sem=None, src_base=0):
                if c == 0:
                    wait(sc_e, normed, normed_before(name))
                if src_sem is not None:
                    sc_e.wait_ge(src_sem, src_base + c + 1)
                nc.scalar.activation(sq[:, c], src[:, c], ACT.Square).then_inc(squares, 1)

            def norm(name, src, src_sem=None, src_base=0, splits=(), first=0):
                n = NORMS[NORM_NO[name]][1]
                sc0 = scaled_before(name)
                nc.scalar.preload_act_table(ACT.Sqrt)
                for c in range(first, n):
                    square(name, c, src, src_sem, src_base)
                sc_e.wait_ge(summed, NORM_NO[name] + 1)
                nc.scalar.activation(sd[:], wk[:, 3, 0:T], ACT.Sqrt, bias=cols[:, 0:1], scale=1.0 / (n * P)
                                     ).then_inc(rooted, 1)
                for s, (dst, off, b) in enumerate(splits):
                    for c in range(n):
                        sc_e.wait_ge(scaled, sc0 + s * n + c + 1)
                        if b is None:
                            ins = nc.scalar.activation(dst[:, off + c], sq[:, c], ACT.Copy)
                        else:
                            ins = nc.scalar.activation(dst[:, off + c], sq[:, c], ACT.Identity,
                                                       bias=mod[:, b * DC + c:b * DC + c + 1])
                        ins.then_inc(normed_hi, 1)

            sc_e.dma_start(gv[:], gains).then_inc(const_in, 16)
            sc_e.dma_start(cst[:], consts).then_inc(const_in, 16)
            sc_e.dma_start(pos_i[:], positions.partition_broadcast(P)).then_inc(const_in, 16)
            sc_e.wait_ge(const_in, 16 * CONST_LOADS)
            hi(block_no(0))
            sc_e.wait_ge(set_up, 5)
            for c in range(DC):
                sc_e.wait_ge(x_landed[c // 4], 16)
                square("conv", c, h)
            hi(block_no(1))
            norm("conv", h, splits=[(xh, 0, None)], first=DC)

            nc.scalar.activation(csilu[:], gv[:, GAIN["c"]:GAIN["c"] + DC], ACT.Silu).then_inc(csilu_ready, 1)
            sc_e.wait_ge(angles, 1)
            nc.scalar.activation(ang[:, 7], ang[:, 3], ACT.Sin).then_inc(trig, 1)
            nc.scalar.activation(ang[:, 6], ang[:, 4], ACT.Sin, bias=cols[:, 1:2], scale=-1.0).then_inc(trig, 1)


            def conv_tile(c, blk):
                ahead(blk)
                used(blk)
                wait(sc_e, gated, c)
                nc.scalar.activation(gc[:], wk[:, 0, 0:T], ACT.Copy).then_inc(gate_copied, 1)
                ahead(after(blk, 1))
                ahead(after(blk, 2))
                sc_e.wait_ge(conved, c + 1)
                dst = yh[:, c] if isinstance(c, int) else yh[:, bass.ds(c, 1)].rearrange("p a t -> p (a t)")
                nc.scalar.activation(dst, cv[:, 2], ACT.Copy).then_inc(conved_hi, 1)

            conv_tile(0, block_no(0))
            with sc_e.Fori(1, DC) as c:
                conv_tile(c, block_no(0, c))

            def add_out(stage, norm_name):
                for c in range(DC):
                    ahead(block_no(FIRST[stage] + c))
                    if c >= 1:
                        square(norm_name, c - 1, h, res_add, added[stage])

            add_out("conv_out", "ffn1")

            def ffn(stage, norm_name, turn, res):
                first = FIRST[stage]
                base = turn * FT
                b0 = first % RING
                norm(norm_name, h, res_add, res, splits=[(xh, 0, None)], first=DC - 1)

                def silu(blk, j):
                    used(blk)
                    wait(sc_e, hid_ready, base + j)
                    nc.scalar.activation(sg[:], wk[:, b0, 0:T], ACT.Silu).then_inc(silu_ready, 1)

                def split_hid(j, used_before):
                    sc_e.wait_ge(hid_ready, base + j + 1)
                    sc_e.wait_ge(block_used, used_before)
                    nc.scalar.activation(hidh[:], hid[:], ACT.Copy).then_inc(hid_hi, 1)

                ahead(block_no(first))
                silu(block_no(first), 0)
                ahead(block_no(first + 1))

                def triple(j, blk):
                    ahead(blk)
                    split_hid(j - 1, number(blk))
                    silu(blk, j)
                    ahead(after(blk, 1))
                    ahead(after(blk, 2))

                triple(1, block_no(first + 2))
                with sc_e.Fori(2, FT) as j:
                    triple(j, block_no(first - 1, j))
                last = block_no(first + 3 * FT - 1)
                split_hid(FT - 1, number(last))
                ahead(last)

            ffn("ffn1", "ffn1", 0, 0)
            norm("mla", h, res_add, DC, splits=[(xh, 0, None), (yh, 0, None)])
            for k in range(7):
                ahead(block_no(FIRST["latent"] + k))
            norm("qlat", lat[:, KC:], lat_read, 4, splits=[(lath, KC, None)])
            norm("kvlat", lat, splits=[(lath, 0, None)])
            for k in range(6):
                ahead(block_no(FIRST["uq"] + k))
            for k in range(4):
                ahead(block_no(FIRST["ukv"] + k))

            def attention(kind, beside=None):
                h0 = attention_base(kind)

                def exps(i):
                    for b in range(TB):
                        sc_e.wait_ge(masked, TB * (h0 + i) + b + 1)
                        wait(sc_e, turned, h0 + i)
                        nc.scalar.activation(pr[:, b, 0:(b + 1) * P], sc[:, b, 0:(b + 1) * P], ACT.Exp,
                                             bias=stat[:, 0, TB * i + b:TB * i + b + 1],
                                             accum_out=stat[:, 1, TB * i + b:TB * i + b + 1]).then_inc(expd, 1)

                def keep_hi(j):
                    if kind == "latent":
                        sc_e.wait_ge(mixed, j + 1)
                        nc.scalar.activation(yh[:, j], acc[:, 2 + j % 2, 0:T], ACT.Copy).then_inc(mixed_hi, 1)
                    elif j % 2 == 1:
                        sc_e.wait_ge(mixed, h0 + j + 1)
                        nc.scalar.activation(yh[:, j // 2], acc[:, 2 + (j // 2) % 2, 0:T], ACT.Copy).then_inc(mixed_hi, 1)

                exps(0)
                for i in range(HEADS):
                    if beside:
                        beside(i, 0)
                    n = h0 + i
                    sc_e.wait_ge(turned, n + 1)
                    wait(sc_e, mixed, n - 1)
                    nc.scalar.activation(pt[:, n % 2], acc[:, n % 2, 0:3 * P], ACT.Copy).then_inc(pt_ready, 1)
                    if i + 1 < HEADS:
                        exps(i + 1)
                    if beside:
                        beside(i, 1)
                    if i >= 1:
                        keep_hi(i - 1)
                keep_hi(HEADS - 1)

            attention("latent")
            add_out("attn_out", "ffn2")
            ffn("ffn2", "ffn2", 1, 2 * DC)
            norm("final", h, res_add, 3 * DC)
            norm("mix", h, scaled, scaled_before("final"), splits=[(xh, 0, 0)])

            def proj(k):
                blk = block_no(FIRST["proj"] + k)
                ahead(blk)
                if k == 0 or 9 <= k < 17 and k % 4 != 0:
                    return
                if k < 9:
                    sc_e.wait_ge(conv2, k)
                    nc.scalar.activation(qk[:, k - 1], uc[:, CK - 1], ACT.Silu).then_inc(silu2, 1)
                    return
                used(blk)
                src = wk[:, blk[0] % RING, 0:T]
                if k in (12, 16):
                    dst = vb[:].rearrange("p b h d -> p b (h d)") if k == 12 else va[:].rearrange("p b h d -> p b (h d)")
                    nc.scalar.activation(dst, wk[:, 0:2], ACT.Copy).then_inc(proj_act, 1)
                elif k < 25:
                    dst = qa[:, k - 17] if k < 21 else ka[:, k - 21]
                    nc.scalar.activation(dst, src, ACT.Copy).then_inc(proj_act, 1)
                else:
                    dst = ob[:, k - 25] if k < 29 else (ga if k < 37 else gb)[:, (k - 29) % DC]
                    nc.scalar.activation(dst, src, ACT.Tanh, scale=0.5).then_inc(proj_act, 1)
                    sc_e.wait_ge(proj_act, k - 14)
                    nc.scalar.activation(dst, dst, ACT.Copy, scale=0.5, bias=0.5).then_inc(sigmoids, 1)

            for k in range(11):
                proj(k)
            sc_e.wait_ge(gates_ready, 1)
            nc.scalar.activation(gw[:, :, 1], gw[:, :, 0], ACT.Exp, scale=-1.0).then_inc(gate_exp, 1)
            sc_e.wait_ge(gate_exp, 1)
            nc.scalar.activation(gw[:, :, 2], gw[:, :, 1], ACT.Ln, bias=cols[:, 3:4]).then_inc(gate_exp, 1)
            proj(11)
            proj(12)

            def m_exps(unit):
                n = (unit % TB + 1) * P
                sc_e.wait_ge(decay_max, unit + 1)
                nc.scalar.activation(dm[:, 1:n + 1], dm[:, 1:n + 1], ACT.Exp, bias=ms[:, 0, unit:unit + 1]
                                     ).then_inc(decay_exp, 1)
                nc.scalar.activation(ms[:, 1, unit:unit + 1], ms[:, 0, unit:unit + 1], ACT.Exp).then_inc(decay_exp, 1)

            m_exps(0)
            for unit in range(TB * BH):
                i, b = divmod(unit, TB)
                n = (b + 1) * P
                proj(13 + 2 * unit)
                sc_e.wait_ge(w_turned, unit + 1)
                wait(sc_e, m_mixed, unit)
                nc.scalar.activation(st[:, 0:n], acc[:, 2, 0:n], ACT.Copy).then_inc(st_ready, 1)
                proj(14 + 2 * unit)
                if unit + 1 < TB * BH:
                    m_exps(unit + 1)
                sc_e.wait_ge(m_out, unit + 1)
                nc.scalar.activation(uc[:, 3, 0:P], hb[:, b, i], ACT.Square, accum_out=ms[:, 4, unit:unit + 1]
                                     ).then_inc(m_sq, 1)
            sc_e.wait_ge(m_sq, TB * BH)
            nc.scalar.activation(ms[:, 5], ms[:, 4], ACT.Sqrt, bias=cols[:, 0:1], scale=1.0 / BD).then_inc(m_root, 1)
            proj(29)
            for i in range(BH):
                sc_e.wait_ge(m_gated, i + 1)
                nc.scalar.activation(yh[:, 4 + i], uc[:, i % 2], ACT.Copy).then_inc(m_hi, 1)
            attention("band", lambda i, half: proj(30 + 2 * i + half) if 30 + 2 * i + half < 45 else None)
            for k in range(DC):
                ahead(block_no(FIRST["branch"] + k))
                sc_e.wait_ge(branch_sum, k + 1)
                nc.scalar.activation(xh[:, k], uc[:, 2], ACT.Copy).then_inc(branch_hi, 1)
            add_out("mix_out", "peer")
            norm("peer", h, res_add, 4 * DC, splits=[(xh, 0, 3)], first=DC - 1)
            for k in range(2 * PH):
                blk = block_no(FIRST["peer_q"] + k)
                ahead(blk)
                used(blk)
                nc.scalar.activation(qp[:, k], wk[:, blk[0] % RING, 0:T], ACT.Copy).then_inc(qp_ready, 1)
            for b in range(TB):
                sc_e.wait_ge(best_sub, b + 1)
                nc.scalar.activation(key[:, 2], best[:], ACT.Exp).then_inc(best_exp, 1)
            for b in range(TB):
                sc_e.wait_ge(keys_turned, b + 1)
                nc.scalar.activation(i_t[:, :, b * P:(b + 1) * P], acc[:, b, 0:3 * P].rearrange("p (s t) -> p s t", s=3),
                                     ACT.Copy).then_inc(i_ready, 1)

            def gate_group(g, par):
                sc_e.wait_ge(hot_used, g + 1)
                tok = gates[:, bass.ds(g * 4, 4)].rearrange("p t k -> p (t k)")
                nc.scalar.activation(tok, wk[:, par], ACT.Copy).then_inc(gates_kept, 1)

            with sc_e.Fori(0, T // 8) as i:
                for par in range(2):
                    gate_group(i * 2 + par, par)

            p0 = FIRST["peer"]

            def activate(blk, i, bank):
                used(blk)
                wait(sc_e, w_ready, i)
                nc.scalar.activation(act[:], wk[:, bank, 0:T], ACT.Gelu_apprx_tanh).then_inc(act_ready, 1)

            ahead(block_no(p0))
            activate(block_no(p0), 0, 0)

            def pair(i, k, blk):
                sc_e.wait_ge(w_ready, i + 1)
                wait(sc_e, block_used, number(blk) - 4)
                nc.scalar.activation(ph[:, k], w32[:], ACT.Copy).then_inc(w_hi, 1)
                ahead(blk)
                activate(blk, i + 1, (k + 1) % RING)
                ahead(after(blk, 1))

            pair(0, 0, block_no(p0 + 1))
            with sc_e.Fori(0, (NK - 2) // RING - 1) as t:
                for k in range(RING):
                    pair(t * RING + (1 + k), (1 + k) % RING, block_no(p0 + 3 + 2 * k, t, 2))
            for i in range(NK - 1 - RING, NK - 1):
                pair(i, i % RING, block_no(p0 + 1 + 2 * i))
            sc_e.wait_ge(w_ready, NK)
            nc.scalar.activation(ph[:, (NK - 1) % RING], w32[:], ACT.Copy).then_inc(w_hi, 1)
            norm("final2", h, res_add, 5 * DC)

        @block.vector
        def _(dve):
            v = nc.vector
            done = [0]

            def chain(ins):
                done[0] += 1
                ins.then_inc(step, 1)
                dve.wait_ge(step, done[0])

            def lo(blk):
                s = blk[0] % RING
                dve.wait_ge(hi_ready, number(blk) + 1)
                v.tensor_tensor(wl[:, s], raw[:, s], wh[:, s].bitcast(F32), ALU.subtract).then_inc(lo_ready, 1)

            def ahead(blk):
                if blk[1] is None and blk[0] + LEAD >= BLOCKS:
                    return
                lo(after(blk, LEAD))

            def used(blk):
                dve.wait_ge(block_used, number(blk) + 1)

            def norm(name, src, splits=(), dst=None):
                n = NORMS[NORM_NO[name]][1]
                sc0, hi0 = scaled_before(name), normed_before(name)
                dve.wait_ge(rooted, NORM_NO[name] + 1)
                wait(dve, scaled, sc0)
                wait(dve, normed, hi0)
                chain(v.reciprocal(rs[:], sd[:]))

                def scale(g, c, to):
                    v.scalar_tensor_tensor(out=to, in0=src[:, c], scalar=g(c), in1=rs[:], op0=ALU.mult,
                                           op1=ALU.mult).then_inc(scaled, 1)

                if dst is not None:
                    for c in range(n):
                        scale(dst[0], c, dst[1][:, c])
                    return
                for s, (g, th, tl, off, shift) in enumerate(splits):
                    def rest(c):
                        dve.wait_ge(normed_hi, hi0 + s * n + c + 1)
                        a, b = sq[:, c], th[:, off + c].bitcast(F32)
                        if shift is None:
                            ins = v.tensor_tensor(tl[:, off + c], a, b, ALU.subtract)
                        else:
                            ins = v.scalar_tensor_tensor(out=tl[:, off + c], in0=a, in1=b, op0=ALU.add, op1=ALU.subtract,
                                                         scalar=mod[:, shift * DC + c:shift * DC + c + 1])
                        ins.then_inc(normed, 1)

                    for c in range(n):
                        if s > 0:
                            dve.wait_ge(normed, hi0 + (s - 1) * n + c + 1)
                        scale(g, c, sq[:, c])
                        if c >= 1:
                            rest(c - 1)
                    rest(n - 1)

            def gain_of(name):
                return lambda c: gain(name, c)

            def columns(t, base=0):
                return lambda c: t[:, base + c:base + c + 1]

            v.memset(cols[:, 0:1], EPS).then_inc(set_up, 1)
            v.memset(cols[:, 1:2], float(np.pi / 2)).then_inc(set_up, 1)
            v.memset(cols[:, 2:3], 0.0).then_inc(set_up, 1)
            v.memset(cols[:, 3:4], 1.0).then_inc(set_up, 1)
            v.memset(z[:, 0:CW - 1], 0.0).then_inc(set_up, 1)
            dve.wait_ge(set_up, 5)
            dve.wait_ge(const_in, 16 * CONST_LOADS)
            lo(block_no(0))
            lo(block_no(1))
            norm("conv", h, splits=[(gain_of("conv"), xh, xl, 0, None)])
            chain(v.tensor_copy(ang[:, 0], pos_i[:]))
            chain(v.tensor_scalar(ang[:, 1], ang[:, 0], gain("inv_freq"), None, ALU.mult))
            chain(v.tensor_scalar(ang[:, 2], ang[:, 1], float(1 / (2 * np.pi)), ROUND, ALU.mult, ALU.add))
            chain(v.tensor_scalar(ang[:, 2], ang[:, 2], -ROUND, None, ALU.add))
            for k, part in enumerate(TWO_PI_PARTS):
                chain(v.scalar_tensor_tensor(out=ang[:, 1], in0=ang[:, 2], scalar=-part, in1=ang[:, 1],
                                             op0=ALU.mult, op1=ALU.add))
            chain(v.tensor_scalar(ang[:, 3], ang[:, 1], PI_BELOW, -PI_BELOW, ALU.min, ALU.max))
            v.scalar_tensor_tensor(out=ang[:, 4], in0=ang[:, 3], scalar=-1.0, in1=ang[:, 3], op0=ALU.mult, op1=ALU.max
                                   ).then_inc(angles, 1)


            def conv_tile(c, blk):
                def at(t, k=0, width=1):
                    return t[:, bass.ds(c * width + k, 1)] if not isinstance(c, int) else \
                        t[:, c * width + k:c * width + k + 1]

                w0 = GAIN["conv_w"]
                taps = gv[:, w0:w0 + CW * DC]
                base = c * (CW + 1)
                ahead(blk)
                used(after(blk, 1))
                dve.wait_ge(gate_copied, c + 1)
                wait(dve, conv_step, c * CW)
                wait(dve, conved_lo, c)
                v.tensor_tensor(z[:, CW - 1:], gc[:], wk[:, 1, 0:T], ALU.mult).then_inc(gated, 1)
                ahead(after(blk, 1))
                dve.wait_ge(gated, c + 1)
                v.tensor_scalar(cv[:, 0], z[:, 0:T], at(taps, 0, CW), None, ALU.mult).then_inc(conv_step, 1)
                dve.wait_ge(conv_step, c * CW + 1)
                v.scalar_tensor_tensor(out=cv[:, 1], in0=z[:, 1:T + 1], scalar=at(taps, 1, CW), in1=cv[:, 0],
                                       op0=ALU.mult, op1=ALU.add).then_inc(conv_step, 1)
                dve.wait_ge(conv_step, c * CW + 2)
                v.scalar_tensor_tensor(out=cv[:, 0], in0=z[:, 2:T + 2], scalar=at(taps, 2, CW), in1=cv[:, 1],
                                       op0=ALU.mult, op1=ALU.add).then_inc(conv_step, 1)
                ahead(after(blk, 2))
                dve.wait_ge(conv_step, c * CW + 3)
                used(after(blk, 2))
                v.tensor_tensor(cv[:, 2], cv[:, 0], wk[:, 2, 0:T], ALU.mult).then_inc(conved, 1)
                dve.wait_ge(conved_hi, c + 1)
                tile = (lambda t: t[:, c]) if isinstance(c, int) else \
                    (lambda t: t[:, bass.ds(c, 1)].rearrange("p a t -> p (a t)"))
                v.tensor_tensor(tile(yl), cv[:, 2], tile(yh).bitcast(F32), ALU.subtract).then_inc(conved_lo, 1)

            conv_tile(0, block_no(0))
            with dve.Fori(1, DC) as c:
                conv_tile(c, block_no(0, c))

            def add_out(stage, factor=None):
                for c in range(DC):
                    blk = block_no(FIRST[stage] + c)
                    ahead(blk)
                    used(blk)
                    src = wk[:, blk[0] % RING, 0:T]
                    if factor is None:
                        ins = v.tensor_tensor(h[:, c], h[:, c], src, ALU.add)
                    else:
                        ins = v.scalar_tensor_tensor(out=h[:, c], in0=src, scalar=factor(c), in1=h[:, c], op0=ALU.mult,
                                                     op1=ALU.add)
                    ins.then_inc(res_add, 1)

            add_out("conv_out")

            def ffn(stage, norm_name, turn):
                first = FIRST[stage]
                base = turn * FT
                b0 = first % RING
                norm(norm_name, h, splits=[(gain_of(norm_name), xh, xl, 0, None)])

                def product(blk, j):
                    used(blk)
                    dve.wait_ge(silu_ready, base + j + 1)
                    wait(dve, hid_lo, base + j)
                    v.tensor_tensor(hid[:], sg[:], wk[:, (b0 + 1) % RING, 0:T], ALU.mult).then_inc(hid_ready, 1)

                def rest(j):
                    dve.wait_ge(hid_hi, base + j + 1)
                    v.tensor_tensor(hidl[:], hid[:], hidh[:].bitcast(F32), ALU.subtract).then_inc(hid_lo, 1)

                ahead(block_no(first))
                ahead(block_no(first + 1))
                product(block_no(first + 1), 0)

                def triple(j, blk):
                    ahead(blk)
                    rest(j - 1)
                    ahead(after(blk, 1))
                    product(after(blk, 1), j)
                    ahead(after(blk, 2))

                triple(1, block_no(first + 2))
                with dve.Fori(2, FT) as j:
                    triple(j, block_no(first - 1, j))
                last = block_no(first + 3 * FT - 1)
                rest(FT - 1)
                ahead(last)
                used(last)
                for c in range(DC):
                    v.tensor_tensor(h[:, c], h[:, c], acc_tile(c), ALU.add).then_inc(res_add, 1)

            ffn("ffn1", "ffn1", 0)
            norm("mla", h, splits=[(gain_of("kv"), xh, xl, 0, None), (gain_of("mla"), yh, yl, 0, None)])
            dve.wait_ge(trig, 2)
            for k in range(7):
                blk = block_no(FIRST["latent"] + k)
                ahead(blk)
                used(blk)
                b = blk[0] % RING
                if k < 2:
                    v.tensor_copy(lat[:, k], wk[:, b, 0:T]).then_inc(lat_read, 1)
                elif k == 3:
                    x1, x2 = wk[:, (b - 1) % RING, 0:T], wk[:, b, 0:T]
                    cos, sin = ang[:, 6], ang[:, 7]
                    v.tensor_tensor(rt[:, 0, 0:T], x2, sin, ALU.mult).then_inc(step, 1)
                    v.tensor_tensor(rt[:, 0, T:2 * T], x2, cos, ALU.mult).then_inc(step, 1)
                    v.tensor_tensor(rt[:, 1, 0:T], x1, cos, ALU.mult).then_inc(step, 1)
                    done[0] += 3
                    chain(v.tensor_tensor(rt[:, 1, T:2 * T], x1, sin, ALU.mult))
                    v.tensor_tensor(kpe[:, 0], rt[:, 1, 0:T], rt[:, 0, 0:T], ALU.subtract).then_inc(lat_read, 1)
                    v.tensor_tensor(kpe[:, 1], rt[:, 1, T:2 * T], rt[:, 0, T:2 * T], ALU.add).then_inc(lat_read, 1)
                elif k > 3:
                    v.tensor_copy(lat[:, KC + k - 4], wk[:, b, 0:T]).then_inc(lat_read, 1)
            norm("qlat", lat[:, KC:], splits=[(gain_of("qlat"), lath, latl, KC, None)])
            norm("kvlat", lat, splits=[(gain_of("kvlat"), lath, latl, 0, None)])
            for k in range(6):
                blk = block_no(FIRST["uq"] + k)
                ahead(blk)
                used(blk)
                b = k % RING
                if k < 4:
                    v.tensor_copy(qn[:, 2 * k:2 * k + 2], wk[:, b].rearrange("p (a t) -> p a t", a=2)).then_inc(uq_read, 1)
                elif k == 5:
                    x1 = wk[:, (b - 1) % RING].rearrange("p (a t) -> p a t", a=2)
                    x2 = wk[:, b].rearrange("p (a t) -> p a t", a=2)
                    dve.wait_ge(lat_read, 7)
                    for s in range(2):
                        cos, sin = ang[:, 6], ang[:, 7]
                        v.tensor_tensor(rt[:, 0, 0:T], x2[:, s], sin, ALU.mult).then_inc(step, 1)
                        v.tensor_tensor(rt[:, 0, T:2 * T], x2[:, s], cos, ALU.mult).then_inc(step, 1)
                        v.tensor_tensor(rt[:, 1, 0:T], x1[:, s], cos, ALU.mult).then_inc(step, 1)
                        done[0] += 3
                        chain(v.tensor_tensor(rt[:, 1, T:2 * T], x1[:, s], sin, ALU.mult))
                        v.tensor_tensor(qpe[:, 0, s], rt[:, 1, 0:T], rt[:, 0, 0:T], ALU.subtract).then_inc(step, 1)
                        done[0] += 1
                        ins = v.tensor_tensor(qpe[:, 1, s], rt[:, 1, T:2 * T], rt[:, 0, T:2 * T], ALU.add)
                        chain(ins)
                    v.engine_nop().then_inc(uq_read, 2)
            for k in range(4):
                blk = block_no(FIRST["ukv"] + k)
                ahead(blk)
                used(blk)
                b = 2 * (k % 2)
                if k < 2:
                    v.tensor_copy(kn[:, 4 * k:4 * k + 4].rearrange("p a t -> p (a t)"),
                                  wk[:, b:b + 2].rearrange("p a t -> p (a t)")).then_inc(ukv_read, 1)
                else:
                    a = 4 * (k - 2)
                    v.tensor_copy(vm[:, :, a:a + 4].rearrange("p b a d -> p b (a d)"), wk[:, b:b + 2]).then_inc(ukv_read, 1)
            v.engine_nop().then_inc(trig, 1)

            def attention(kind, beside=None):
                h0 = attention_base(kind)

                def mask(i, b):
                    n = (b + 1) * P
                    unit = TB * (h0 + i) + b
                    dve.wait_ge(scored, unit + 1)
                    wait(dve, expd, unit - 1)
                    if kind == "latent":
                        m, scale, src = const("mask")[:, b * P:b * P + n], MLA_SCALE, wk[:, unit % 3, 0:n]
                    else:
                        m, scale, src = bias[:, i, b * P:b * P + n], AHD ** -0.5, wk[:, 3, b * P:b * P + n]
                    chain(v.scalar_tensor_tensor(out=sc[:, b, 0:n], in0=src, scalar=scale, in1=m,
                                                 op0=ALU.mult, op1=ALU.add))
                    s = TB * i + b
                    v.tensor_reduce(stat[:, 0, s:s + 1], sc[:, b, 0:n], AX, ALU.max, negate=True).then_inc(masked, 1)

                def divide(i, b):
                    n = (b + 1) * P
                    s = TB * i + b
                    dve.wait_ge(expd, TB * (h0 + i) + b + 1)
                    chain(v.reciprocal(stat[:, 2, s:s + 1], stat[:, 1, s:s + 1]))
                    v.tensor_scalar(pr[:, b, 0:n], pr[:, b, 0:n], stat[:, 2, s:s + 1], None, ALU.mult).then_inc(probs, 1)

                def softmax(i):
                    mask(i, 0)
                    mask(i, 1)
                    divide(i, 0)
                    divide(i, 1)

                softmax(0)
                for i in range(HEADS + 1):
                    if beside and i < HEADS:
                        beside(i, 0)
                    if i + 1 < HEADS:
                        softmax(i + 1)
                    if beside and i < HEADS:
                        beside(i, 1)
                    if i >= 1:
                        j = i - 1
                        if kind == "latent":
                            dve.wait_ge(mixed_hi, j + 1)
                            v.tensor_tensor(yl[:, j], acc[:, 2 + j % 2, 0:T], yh[:, j].bitcast(F32), ALU.subtract
                                            ).then_inc(mixed_lo, 1)
                        elif j % 2 == 1:
                            dve.wait_ge(mixed_hi, HEADS + j // 2 + 1)
                            v.tensor_tensor(yl[:, j // 2], acc[:, 2 + (j // 2) % 2, 0:T], yh[:, j // 2].bitcast(F32),
                                            ALU.subtract).then_inc(mixed_lo, 1)

            attention("latent")
            dve.wait_ge(mod_summed, 1)
            chain(v.tensor_tensor(mod[:], wk[:, 3, 0:6 * DC], gv[:, GAIN["b_ada"]:GAIN["b_ada"] + 6 * DC], ALU.add))
            for s, name in enumerate(["norm1", "norm2"]):
                part = mod[:, (3 * s + 1) * DC:(3 * s + 2) * DC]
                chain(v.scalar_tensor_tensor(out=modg[:, s], in0=part, scalar=1.0,
                                             in1=gv[:, GAIN[name]:GAIN[name] + DC], op0=ALU.add, op1=ALU.mult))
            v.engine_nop().then_inc(mod_ready, 1)
            add_out("attn_out")
            ffn("ffn2", "ffn2", 1)
            norm("final", h, dst=(gain_of("final"), h))
            chain(v.memset(u[:, 0:CK - 1], 0.0))

            norm("mix", h, splits=[(columns(modg[:, 0]), xh, xl, 0, 0)])
            def proj(k):
                blk = block_no(FIRST["proj"] + k)
                ahead(blk)
                if k == 0:
                    dve.wait_ge(band_in, 48)
                    used(blk)
                    for b in range(TB):
                        ins = v.tensor_tensor(gt[:, b], wk[:, blk[0] % RING, b * P:b * P + 2 * BH], gbias[:], ALU.add)
                        if b == 0:
                            ins.then_inc(step, 1)
                            done[0] += 1
                    ins.then_inc(proj_dve, 1)
                elif k < 9:
                    used(blk)
                    c = k - 1
                    w0 = GAIN["conv2_w"] + CK * c
                    wait(dve, conv2, k - 1)
                    v.tensor_copy(u[:, CK - 1:], wk[:, blk[0] % RING, 0:T]).then_inc(proj_dve, 1)
                    dve.wait_ge(proj_dve, k + 1)
                    wait(dve, silu2, k - 1)
                    chain(v.tensor_scalar(uc[:, 0], u[:, 0:T], gv[:, w0:w0 + 1], gain("conv2_b", c), ALU.mult, ALU.add))
                    for t in range(1, CK):
                        ins = v.scalar_tensor_tensor(out=uc[:, t], in0=u[:, t:t + T], scalar=gv[:, w0 + t:w0 + t + 1],
                                                     in1=uc[:, t - 1], op0=ALU.mult, op1=ALU.add)
                        if t < CK - 1:
                            chain(ins)
                        else:
                            ins.then_inc(conv2, 1)
            for k in range(10):
                proj(k)
            dve.wait_ge(proj_dve, 1)
            v.scalar_tensor_tensor(out=gw[:, :, 0], in0=gt[:, :, BH:], scalar=-1.0, in1=gt[:, :, BH:], op0=ALU.mult,
                                   op1=ALU.max).then_inc(gates_ready, 1)
            proj(10)
            dve.wait_ge(gate_exp, 2)
            for b in range(TB):
                chain(v.scalar_tensor_tensor(out=gt[:, b, BH:], in0=gt[:, b, BH:], scalar=0.0, in1=gw[:, b, 2],
                                             op0=ALU.min, op1=ALU.subtract))
            ident, past = const("ident"), (const("past0"), const("past1"))
            chain(v.memset(rr[:], 0.0))

            def m_decays(i):
                wait(dve, decay_sums, TB * i)
                for b in range(TB):
                    n = (b + 1) * P
                    chain(v.tensor_scalar(rr[:, b, 0:n + 1], past[b], gt[:, b, BH + i:BH + i + 1], None, ALU.mult))
                    ins = v.scalar_tensor_tensor(out=rr[:, b, b * P + 1:n + 1], in0=ident, scalar=gt[:, b, i:i + 1],
                                                 in1=rr[:, b, b * P + 1:n + 1], op0=ALU.mult, op1=ALU.add)
                    if b == 0:
                        chain(ins)
                    else:
                        ins.then_inc(decays, 1)

            def m_weigh(unit):
                b = unit % TB
                n = (b + 1) * P
                col = lambda r: ms[:, r, unit:unit + 1]
                dve.wait_ge(decay_sums, unit + 1)
                v.tensor_copy(dm[:, 0:1], acc[:, 0, 0:1]).then_inc(step, 1)
                done[0] += 1
                chain(v.tensor_tensor(dm[:, 1:n + 1], acc[:, 0, 1:n + 1], const("mask")[:, b * P:b * P + n], ALU.add))
                v.tensor_reduce(col(0), dm[:, 0:n + 1], AX, ALU.max, negate=True).then_inc(decay_max, 1)
                dve.wait_ge(decay_exp, 2 * unit + 2)
                v.scalar_tensor_tensor(out=sv[:, 0:n], in0=acc[:, 1, 0:n], scalar=BD ** -0.5, in1=dm[:, 1:n + 1],
                                       op0=ALU.mult, op1=ALU.mult, accum_out=col(2)).then_inc(weighted, 1)
                dve.wait_ge(weighted, unit + 1)
                chain(v.scalar_tensor_tensor(out=col(3), in0=col(2), scalar=-1.0, in1=col(2), op0=ALU.mult, op1=ALU.max))
                chain(v.tensor_scalar(col(3), col(3), col(1), None, ALU.max))
                chain(v.reciprocal(col(6), col(3)))

            m_decays(0)
            proj(11)
            m_weigh(0)
            proj(12)
            for unit in range(TB * BH):
                i, b = divmod(unit, TB)
                if b == 1 and i + 1 < BH:
                    m_decays(i + 1)
                proj(13 + 2 * unit)
                proj(14 + 2 * unit)
                if unit + 1 < TB * BH:
                    dve.wait_ge(w_turned, unit + 1)
                    m_weigh(unit + 1)
                dve.wait_ge(m_mixed, unit + 1)
                v.tensor_scalar(hb[:, b, i], acc[:, 3, 0:P], ms[:, 6, unit:unit + 1], None, ALU.mult).then_inc(m_out, 1)
            dve.wait_ge(m_root, 1)
            chain(v.reciprocal(ms[:, 7], ms[:, 5]))
            for i in range(BH):
                for b in range(TB):
                    unit = TB * i + b
                    chain(v.tensor_scalar(hb[:, b, i], hb[:, b, i], ms[:, 7, unit:unit + 1], None, ALU.mult))
            v.engine_nop().then_inc(m_normed, 1)
            proj(29)
            dve.wait_ge(sigmoids, 4)
            for i in range(BH):
                dve.wait_ge(m_turned, i + 1)
                wait(dve, m_lo, i - 1)
                wait(dve, m_hi, i - 1)
                v.scalar_tensor_tensor(out=uc[:, i % 2], in0=acc[:, i % 2, 0:T], scalar=gain("mlstm", i), in1=ob[:, i],
                                       op0=ALU.mult, op1=ALU.mult).then_inc(m_gated, 1)
                dve.wait_ge(m_hi, i + 1)
                v.tensor_tensor(yl[:, 4 + i], uc[:, i % 2], yh[:, 4 + i].bitcast(F32), ALU.subtract).then_inc(m_lo, 1)
            attention("band", lambda i, half: proj(30 + 2 * i + half) if 30 + 2 * i + half < 45 else None)
            dve.wait_ge(sigmoids, 20)
            for k in range(DC):
                blk = block_no(FIRST["branch"] + k)
                ahead(blk)
                used(blk)
                b = 2 * (k % 2)
                v.tensor_tensor(uc[:, 0], ga[:, k], wk[:, b, 0:T], ALU.mult).then_inc(step, 1)
                done[0] += 1
                chain(v.tensor_tensor(uc[:, 1], gb[:, k], wk[:, b + 1, 0:T], ALU.mult))
                wait(dve, branch_lo, k)
                v.tensor_tensor(uc[:, 2], uc[:, 0], uc[:, 1], ALU.add).then_inc(branch_sum, 1)
                dve.wait_ge(branch_hi, k + 1)
                v.tensor_tensor(xl[:, k], uc[:, 2], xh[:, k].bitcast(F32), ALU.subtract).then_inc(branch_lo, 1)
            add_out("mix_out", columns(mod, 2 * DC))
            norm("peer", h, splits=[(columns(modg[:, 1]), xh, xl, 0, 3)])
            for k in range(2 * PH):
                ahead(block_no(FIRST["peer_q"] + k))

            def top16(values, spare, out_v, out_i, last_sem=None):
                chain(v.max(out_v[:, 0:8], values))
                v.max_index(out_i[:, 0:8], out_v[:, 0:8], values).then_inc(step, 1)
                done[0] += 1
                chain(v.match_replace(spare, out_v[:, 0:8], values, LOWEST))
                chain(v.max(out_v[:, 8:16], spare))
                ins = v.max_index(out_i[:, 8:16], out_v[:, 8:16], spare)
                if last_sem is None:
                    chain(ins)
                else:
                    ins.then_inc(last_sem, 1)

            iota16 = const("iota")[:, 0:TOPK]

            def spread(ap, dims):
                for d in range(3):
                    if d not in dims:
                        ap = ap.unsqueeze(d + 1)
                return ap.to_broadcast([P, PH, TOPK, TOPK])

            for b in range(TB):
                for g in range(4):
                    n = 4 * b + g
                    dve.wait_ge(key_scored, n + 1)
                    for j in range(4):
                        s = 4 * g + j
                        top16(wk[:, n % 4, j * P:(j + 1) * P], s2[:], val[:, s], idx[:, s])
                    v.engine_nop().then_inc(key_read, 1)
                chain(v.tensor_copy(idxf[:], idx[:]))
                sides = val[:].rearrange("p (h s) k -> p h s k", s=2)
                chain(v.tensor_tensor(cand[:].rearrange("p h (a b) -> p h a b", a=TOPK), spread(sides[:, :, 0], (0, 1)),
                                      spread(sides[:, :, 1], (0, 2)), ALU.add))
                wait(dve, keys_turned, b)
                for i in range(PH):
                    top16(cand[:, i], c2[:], best[:, i], pick[:, 0, i])
                v.tensor_single_scalar(pick[:, 1], pick[:, 0], 4, ALU.logical_shift_right).then_inc(step, 1)
                done[0] += 1
                chain(v.tensor_single_scalar(pick[:, 2], pick[:, 0], TOPK - 1, ALU.bitwise_and))
                chain(v.tensor_copy(pickf[:], pick[:, 1:3]))
                ids = idxf[:].rearrange("p (h s) k -> p h s k", s=2)
                for s in range(2):
                    chain(v.tensor_tensor(eq[:], spread(pickf[:, s], (0, 1)), spread(iota16, (2,)), ALU.is_equal))
                    chain(v.tensor_tensor(eq[:], eq[:], spread(ids[:, :, s], (0, 2)), ALU.mult))
                    chain(v.tensor_reduce(key[:, s], eq[:], AX, ALU.add))
                chain(v.tensor_copy(soft[:, 0], best[:, :, 0]))
                v.tensor_tensor(best[:], best[:], soft[:, 0].unsqueeze(2).to_broadcast([P, PH, TOPK]), ALU.subtract
                                ).then_inc(best_sub, 1)
                dve.wait_ge(best_exp, b + 1)
                chain(v.tensor_reduce(soft[:, 0], key[:, 2], AX, ALU.add))
                chain(v.reciprocal(soft[:, 1], soft[:, 0]))
                v.tensor_tensor(key[:, 2], key[:, 2], soft[:, 1].unsqueeze(2).to_broadcast([P, PH, TOPK]), ALU.mult
                                ).then_inc(keys_ready, 1)
            dve.wait_ge(i_ready, TB)

            def one_hot(g, par, first):
                wait(dve, hot_used, g - 1 if not first else 0)
                for j in range(4):
                    def column(s):
                        return i_t[:, s, bass.ds(g * 4 + j, 1)]
                    v.tensor_scalar(hot[:, par, 0, j], const("iota"), column(0), column(2), ALU.is_equal, ALU.mult)
                    ins = v.tensor_scalar(hot[:, par, 1, j], const("iota"), column(1), None, ALU.is_equal)
                ins.then_inc(hot_ready, 1)

            one_hot(0, 0, True)
            one_hot(1, 1, True)
            with dve.Fori(1, T // 8) as i:
                for par in range(2):
                    one_hot(i * 2 + par, par, False)

            p0 = FIRST["peer"]
            dve.wait_ge(gates_kept, T // 4)

            def weigh(i):
                dve.wait_ge(act_ready, i + 1)
                wait(dve, w_lo, i)
                wait(dve, w_hi, i)
                g = gates[:, :, bass.ds(i, 1)].rearrange("p t a -> p (t a)")
                v.tensor_tensor(w32[:], act[:], g, ALU.mult).then_inc(w_ready, 1)

            def rest(i, k):
                dve.wait_ge(w_hi, i + 1)
                v.tensor_tensor(pl[:, k], w32[:], ph[:, k].bitcast(F32), ALU.subtract).then_inc(w_lo, 1)

            ahead(block_no(p0))
            weigh(0)

            def pair(i, k, blk):
                rest(i, k)
                ahead(blk)
                weigh(i + 1)
                ahead(after(blk, 1))

            pair(0, 0, block_no(p0 + 1))
            with dve.Fori(0, (NK - 2) // RING - 1) as t:
                for k in range(RING):
                    pair(t * RING + (1 + k), (1 + k) % RING, block_no(p0 + 3 + 2 * k, t, 2))
            for i in range(NK - 1 - RING, NK - 1):
                pair(i, i % RING, block_no(p0 + 1 + 2 * i))
            rest(NK - 1, (NK - 1) % RING)
            used(block_no(BLOCKS - 1))
            for c in range(DC):
                v.scalar_tensor_tensor(out=h[:, c], in0=acc_tile(c), scalar=mod[:, 5 * DC + c:5 * DC + c + 1], in1=h[:, c],
                                       op0=ALU.mult, op1=ALU.add).then_inc(res_add, 1)
            norm("final2", h, dst=(gain_of("final2"), sq))


def pieces(w):
    k, n = w.shape
    return w.reshape(k // P, P, n // P, P).transpose(2, 1, 0, 3).reshape(n // P, P, (k // P) * P)


def padded(w, width):
    return np.concatenate([w, np.zeros(w.shape[:2] + (width - w.shape[2],), np.float32)], axis=2)


def kernel(x, positions, conv_norm_g, conv_w_in, conv_w, conv_w_out, conv_ffn_norm_g, conv_ffn_w13, conv_ffn_w2,
           kv_norm_g, w_dkv, kv_latent_norm_g, w_ukv, mla_norm_g, mla_w_dq, mla_q_norm_g, mla_w_uq, mla_w_o,
           mla_ffn_norm_g, mla_ffn_w13, mla_ffn_w2, final_norm_g, c_2, w_ada_2, b_ada_2, norm1_g_2, w_in_2, conv_w_2,
           conv_b_2, b_igate_2, b_fgate_2, rel_bias_2, mlstm_norm_g_2, w_branch_a_2, w_branch_b_2, w_out_2, norm2_g_2,
           w_peer_q_2, peer_sub_keys_2, peer_u_2, peer_v_2, final_g_2):
    import concourse.bacc as bacc
    from concourse.bass_utils import run_bass_kernel_spmd

    f = np.asarray
    blocks = []

    w = pieces(f(conv_w_in)[0]).reshape(3, DC, P, 1024)
    blocks.append(w[[1, 2, 0]].transpose(1, 0, 2, 3).reshape(-1, P, 1024))
    blocks.append(pieces(f(conv_w_out)[0]))

    def ffn(w13, w2):
        gu = pieces(f(w13)[0]).reshape(2, FT, P, 1024)
        o = f(w2)[0].reshape(FT, P, D)
        order = [gu[0, 0], gu[1, 0]]
        for j in range(1, FT):
            order += [gu[0, j], gu[1, j], o[j - 1]]
        return np.stack(order + [o[FT - 1]])

    blocks.append(ffn(conv_ffn_w13, conv_ffn_w2))
    dkv = f(w_dkv)
    half = ROPE // 2
    x1, x2 = dkv[:, KVR:KVR + half], dkv[:, KVR + half:]
    blocks.append(pieces(np.concatenate([dkv[:, :KVR]] + [x1] * 4 + [x2] * 4 + [f(mla_w_dq)[0]], axis=1)))
    uq = f(mla_w_uq)[0].reshape(QR, HEADS, NOPE + ROPE)
    uq = np.concatenate([uq[:, :, :NOPE].reshape(QR, -1), uq[:, :, NOPE:NOPE + half].reshape(QR, -1),
                         uq[:, :, NOPE + half:].reshape(QR, -1)], axis=1)
    uq = pieces(uq).reshape(6, 2, P, QC * P).transpose(0, 2, 1, 3).reshape(6, P, 2 * QC * P)
    blocks.append(padded(uq, 1024))
    ukv = f(w_ukv).reshape(KC, P, HEADS, 2, NOPE)
    ukv = ukv.transpose(3, 2, 1, 0, 4).reshape(2, 2, 4, P, KC, NOPE)
    blocks.append(ukv.transpose(0, 1, 3, 4, 2, 5).reshape(4, P, 1024))
    blocks.append(pieces(f(mla_w_o)[0]))
    blocks.append(ffn(mla_ffn_w13, mla_ffn_w2))
    win = f(w_in_2)[0]
    sizes = [512, 512, 512, 1024, 512, 512, BH, BH, D, D]
    qa, ka, va, qkb, vb, ob, ib, fb, ga, gb = np.split(win, np.cumsum(sizes)[:-1], axis=1)
    gate = np.concatenate([ib, fb, np.zeros((D, P - 2 * BH), np.float32)], axis=1)
    blocks.append(pieces(np.concatenate([gate, qkb], axis=1)))
    for v in (vb, va):
        blocks.append(v.reshape(4, 2, P, 512).transpose(0, 2, 1, 3).reshape(4, P, 1024))
    blocks.append(pieces(np.concatenate([qa, ka, ob, ga, gb], axis=1)))
    blocks.append(np.concatenate([pieces(f(w_branch_a_2)[0]), pieces(f(w_branch_b_2)[0])], axis=2))
    blocks.append(pieces(f(w_out_2)[0]))
    blocks.append(pieces(f(w_peer_q_2)[0]))
    pu = f(peer_u_2)[0].reshape(NK, NK, DC, P).transpose(0, 3, 2, 1).reshape(NK, P, 1024)
    pv = f(peer_v_2)[0].reshape(NK, NK, D)
    pairs = np.stack([pu[1:], pv[:-1]], axis=1).reshape(-1, P, 1024)
    blocks += [pu[:1], pairs, pv[-1:]]
    stream = np.concatenate(blocks)
    del blocks, pu, pairs
    assert stream.shape == (BLOCKS, P, 1024)

    def column(a):
        return f(a).reshape(-1, P).T

    inv_freq = (np.float32(10000.0) ** (-np.arange(0, ROPE, 2, dtype=np.float32) / np.float32(ROPE))).astype(np.float32)
    gains = np.concatenate(
        [column(a) for a in (conv_norm_g, conv_ffn_norm_g, kv_norm_g, mla_norm_g, kv_latent_norm_g, mla_q_norm_g,
                             mla_ffn_norm_g, final_norm_g, norm1_g_2, norm2_g_2, final_g_2, mlstm_norm_g_2, c_2, b_ada_2)]
        + [f(conv_w)[0].reshape(CW, DC, P).transpose(2, 1, 0).reshape(P, -1),
           f(conv_w_2)[0].reshape(CK, 2 * BH, P).transpose(2, 1, 0).reshape(P, -1), column(conv_b_2),
           np.tile(inv_freq, 4)[:, None]], axis=1).astype(np.float32)

    i = np.arange(P)
    tri = np.where(i[None, :] <= i[:, None], 0.0, NEG)
    past = (i[None, :] < i[:, None]).astype(np.float32)
    one, zero = np.ones((P, 1)), np.zeros((P, P))
    consts = np.concatenate([np.eye(P), np.tile(i, (P, 1)), tri, zero, tri, np.ones((P, P)),
                             i[:, None] <= i[None, :], one, past, one, np.ones((P, P)), past], axis=1).astype(np.float32)

    q, k = np.arange(T)[:, None], np.arange(T)[None, :]
    rel = np.clip(q - k, -CLIP, CLIP) + CLIP
    band = f(rel_bias_2)[0][:, rel]
    band = np.where((k // CHUNK > q // CHUNK)[None], np.float32(NEG), band)
    band = np.concatenate([band[:, :P, :P], band[:, P:]], axis=2).transpose(1, 0, 2)
    gate_bias = np.tile(np.concatenate([f(b_igate_2)[0], f(b_fgate_2)[0]])[None], (P, 1))
    sub_keys = f(peer_sub_keys_2)[0].reshape(2 * PH, NK, P).transpose(2, 0, 1)
    x_in = f(x)[0].reshape(T, DC, P).transpose(2, 1, 0)

    arrays = {"stream": stream, "ada": f(w_ada_2)[0], "gains": gains, "consts": consts, "positions": f(positions),
              "x_in": x_in, "band_bias": band, "gate_bias": gate_bias, "sub_keys": sub_keys}
    arrays = {n: np.ascontiguousarray(a) for n, a in arrays.items()}
    nc = bacc.Bacc("TRN2", target_bir_lowering=False, num_devices=1)
    aps = {n: nc.dram_tensor(n, a.shape, mybir.dt.from_np(a.dtype), kind="ExternalInput").ap() for n, a in arrays.items()}
    aps["positions"] = aps["positions"][0]
    out = nc.dram_tensor("out", (P, DC, T), F32, kind="ExternalOutput").ap()
    build(nc, out=out, **aps)
    r = run_bass_kernel_spmd(nc, [arrays], core_ids=[0])
    return r.results[0]["out"].transpose(2, 1, 0).reshape(1, T, D)
```

```python
from contextlib import ExitStack

import numpy as np

import concourse.bass as bass
from concourse import mybir

ALU = mybir.AluOpType
ACT = mybir.ActivationFunctionType
F32 = mybir.dt.float32
F32R = mybir.dt.float32r
U32 = mybir.dt.uint32
I32 = mybir.dt.int32
AX = mybir.AxisListType.X

P = 128
T = 256
TB = T // P
D = 1024
DC = D // P
FF = 2816
FT = FF // P
HEADS = 8
NOPE, ROPE = 128, 64
KVR, QR = 256, 384
KC, QC = KVR // P, QR // P
EPS = 1e-6
MLA_SCALE = float(NOPE + ROPE) ** -0.5
CW = 3
CK = 4
AH, AHD = 8, 64
BH, BD = 4, 128
CHUNK, CLIP = 64, 128
PH, NK, TOPK = 8, 128, 16
NEG = -1e30
LOWEST = -3e38
ROUND = 12582912.0
TWO_PI_PARTS = (6.28125, 1.935303211212158203125e-3, 3.9683743166540886e-09)
PI_BELOW = 3.1415925

RING = 3
LEAD = 2

STAGES = [("conv_in", 3 * DC), ("conv_out", DC), ("ffn1", 3 * FT), ("latent", 7), ("uq", 6), ("ukv", 4),
          ("attn_out", DC), ("ffn2", 3 * FT), ("proj", 45), ("branch", DC), ("mix_out", DC),
          ("peer_q", 2 * PH), ("peer", 2 * NK)]
FIRST = {}
BLOCKS = 0
for _name, _count in STAGES:
    FIRST[_name] = BLOCKS
    BLOCKS += _count

NORMS = [("conv", DC, 1), ("ffn1", DC, 1), ("mla", DC, 2), ("qlat", QC, 1), ("kvlat", KC, 1), ("ffn2", DC, 1),
         ("final", DC, 0), ("mix", DC, 1), ("peer", DC, 1), ("final2", DC, 0)]
NORM_NO = {n: i for i, (n, _, _) in enumerate(NORMS)}

GAIN = {}
GAINS = 0
for _name, _count in [("conv", DC), ("ffn1", DC), ("kv", DC), ("mla", DC), ("kvlat", KC), ("qlat", QC), ("ffn2", DC),
                      ("final", DC), ("norm1", DC), ("norm2", DC), ("final2", DC), ("mlstm", BH), ("c", DC),
                      ("b_ada", 6 * DC), ("conv_w", CW * DC), ("conv2_w", CK * 2 * BH), ("conv2_b", 2 * BH),
                      ("inv_freq", 1)]:
    GAIN[_name] = GAINS
    GAINS += _count


def block_no(const, trip=None, per_trip=1):
    return (const, trip, per_trip)


def number(block):
    const, trip, per_trip = block
    return const if trip is None else const + trip * (RING * per_trip)


def lap(block):
    const, trip, per_trip = block
    return const // RING if trip is None else const // RING + trip * per_trip


def after(block, k):
    return (block[0] + k,) + block[1:]


def wait(eng, sem, value):
    if isinstance(value, int) and value <= 0:
        return
    eng.wait_ge(sem, value)



GATE_TAIL = 4
GATE_TRIPS = (T // 4 - GATE_TAIL) // (2 * RING)
EARLY_CHOICE = 48
EARLY = EARLY_CHOICE + RING * GATE_TRIPS + RING
assert EARLY % RING == 0 and 2 * RING * GATE_TRIPS + GATE_TAIL == T // 4 and (NK - 2) % RING == 0


CONST = {}
CONSTS = 0
for _name, _count in [("ident", P), ("iota", P), ("ones", P), ("mask", 3 * P), ("upto", P), ("past0", P + 1),
                      ("past1", 2 * P + 1)]:
    CONST[_name] = (CONSTS, CONSTS + _count)
    CONSTS += _count


def build(nc, stream, ada, gains, consts, positions, x_in, band_bias, gate_bias, sub_keys, out, put_off):
    with ExitStack() as ctx:
        place = [(nc.sbuf_base + 63) // 64 * 64]

        def sem(name):
            return ctx.enter_context(nc.semaphore(name))

        def sb(name, shape, dt=F32):
            t = nc.alloc_sbuf_tensor_at(name, shape, dt, offset=place[0])
            place[0] += (int(np.prod(shape[1:])) * 4 + 31) // 32 * 32
            assert place[0] <= nc.sbuf_usable_end, (name, place[0])
            return t

        h = sb("h", [P, DC, T])
        xh = sb("xh", [P, DC, T], F32R)
        xl = sb("xl", [P, DC, T], F32R)
        raw = sb("raw", [P, RING, 1024])
        wh = sb("wh", [P, RING, 1024], F32R)
        wl = sb("wl", [P, RING, 1024], F32R)
        gv = sb("gv", [P, GAINS])
        mod = sb("mod", [P, 6 * DC])
        modg = sb("modg", [P, 2, DC])
        cst_at = place[0]
        cst = sb("cst", [P, CONSTS])
        cols = sb("cols", [P, 4])
        csilu = sb("csilu", [P, DC])
        sd = sb("sd", [P, T])
        rs = sb("rs", [P, T])
        i_t = sb("i_t", [P, 3, T])
        peer_at = place[0]
        w32 = sb("w32", [P, T])
        ph = sb("ph", [P, RING, T], F32R)
        pl = sb("pl", [P, RING, T], F32R)
        arena = (place[0] + 63) // 64 * 64
        place[0] = peer_at
        hot = sb("hot", [P, 2, 2, 4, P])
        place[0] = cst_at + CONST["mask"][0] * 4
        acts = sb("acts", [P, RING, T])
        assert place[0] <= cst_at + CONSTS * 4
        place[0] = max(arena, peer_at + 8 * P * 4 * 2)
        gates = sb("gates", [P, T, NK])

        place[0] = arena
        yh = sb("yh", [P, DC, T], F32R)
        yl = sb("yl", [P, DC, T], F32R)
        sq = sb("sq", [P, DC, T])
        ada_acc = sb("ada_acc", [P, 6, D])
        ada_w = sb("ada_w", [P, 2, D])
        ada_p = sb("ada_p", [P, D])
        shared = place[0]
        place[0] = arena + 2 * 8192
        sc = sb("sc", [P, 2, T])
        pr = sb("pr", [P, 2, T])
        pt = sb("pt", [P, 2, 3 * P])
        stat = sb("stat", [P, 4, 2 * AH])

        place[0] = shared
        z = sb("z", [P, T + CW - 1])
        gc = sb("gc", [P, T])
        cv = sb("cv", [P, 3, T])
        sg = sb("sg", [P, T])
        hid = sb("hid", [P, T])
        hidh = sb("hidh", [P, T], F32R)
        hidl = sb("hidl", [P, T], F32R)
        pos_i = sb("pos_i", [P, T], I32)
        ang = sb("ang", [P, 8, T])
        lat = sb("lat", [P, KC + QC, T])
        lath = sb("lath", [P, KC + QC, T], F32R)
        latl = sb("latl", [P, KC + QC, T], F32R)
        kpe = sb("kpe", [P, 2, T])
        qn = sb("qn", [P, HEADS, T])
        qpe = sb("qpe", [P, 2, 2, T])
        kn = sb("kn", [P, HEADS, T])
        vm = sb("vm", [P, TB, HEADS, NOPE])
        rt = sb("rt", [P, 2, 2 * T])
        place[0] = shared
        ga = sb("ga", [P, DC, T])
        gb = sb("gb", [P, DC, T])
        ob = sb("ob", [P, BH, T])
        qk = sb("qk", [P, 2 * BH, T])
        vb = sb("vb", [P, TB, BH, BD])
        va = sb("va", [P, TB, 4, P])
        qa = sb("qa", [P, 4, T])
        ka = sb("ka", [P, 4, T])
        gt = sb("gt", [P, TB, 2 * BH])
        gw = sb("gw", [P, TB, 3, BH])
        u = sb("u", [P, T + CK - 1])
        uc = sb("uc", [P, CK, T])
        rr = sb("rr", [P, TB, 2 * P + 1])
        dm = sb("dm", [P, 2 * P + 1])
        sv = sb("sv", [P, T])
        st = sb("st", [P, 3 * P])
        hb = sb("hb", [P, TB, BH, BD])
        ms = sb("ms", [P, 10, 2 * BH])
        place[0] = arena + 3 * 8192
        bias = sb("bias", [P, AH, 3 * P])
        sk = sb("sk", [P, 2 * PH, NK])
        gbias = sb("gbias", [P, 2 * BH])
        place[0] = arena
        qp = sb("qp", [P, 2 * PH, T])
        place[0] = shared
        s2 = sb("s2", [P, NK])
        val = sb("val", [P, 2 * PH, TOPK])
        idx = sb("idx", [P, 2 * PH, TOPK], U32)
        idxf = sb("idxf", [P, 2 * PH, TOPK])
        cand = sb("cand", [P, PH, TOPK * TOPK])
        c2 = sb("c2", [P, TOPK * TOPK])
        best = sb("best", [P, TB, PH, TOPK])
        pick = sb("pick", [P, 3, PH, TOPK], U32)
        pickf = sb("pickf", [P, 2, PH, TOPK])
        eq = sb("eq", [P, PH, TOPK, TOPK])
        key = sb("key", [P, TB, 3, PH, TOPK])
        soft = sb("soft", [P, TB, 2, PH])
        ks = sb("ks", [P, TB, 2 * PH, NK])

        wk = ctx.enter_context(nc.psum_tensor("wk", [P, 4, 512], F32))
        acc = ctx.enter_context(nc.psum_tensor("acc", [P, 4, 512], F32))

        def acc_tile(j):
            return acc[:, j // 2, (j % 2) * T:(j % 2 + 1) * T]

        raw_in = [sem(f"raw_in{i}") for i in range(RING)]
        hi_ready = sem("hi_ready")
        lo_ready = sem("lo_ready")
        block_used = sem("block_used")
        x_landed = [sem("x_landed0"), sem("x_landed1")]
        const_in = sem("const_in")
        band_in = sem("band_in")
        set_up = sem("set_up")
        squares = sem("squares")
        summed = sem("summed")
        rooted = sem("rooted")
        scaled = sem("scaled")
        normed_hi = sem("normed_hi")
        normed = sem("normed")
        gate_copied = sem("gate_copied")
        gated = sem("gated")
        conved = sem("conved")
        conved_hi = sem("conved_hi")
        conved_lo = sem("conved_lo")
        res_add = sem("res_add")
        silu_ready = sem("silu_ready")
        hid_ready = sem("hid_ready")
        hid_hi = sem("hid_hi")
        hid_lo = sem("hid_lo")
        lat_read = sem("lat_read")
        uq_read = sem("uq_read")
        ukv_read = sem("ukv_read")
        angles = sem("angles")
        trig = sem("trig")
        scored = sem("scored")
        masked = sem("masked")
        expd = sem("expd")
        probs = sem("probs")
        turned = sem("turned")
        pt_ready = sem("pt_ready")
        mixed = sem("mixed")
        mixed_hi = sem("mixed_hi")
        mixed_lo = sem("mixed_lo")
        ada_in = [sem("ada_in0"), sem("ada_in1")]
        csilu_ready = sem("csilu_ready")
        ada_scaled = sem("ada_scaled")
        ada_added = sem("ada_added")
        ada_done = sem("ada_done")
        mod_summed = sem("mod_summed")
        mod_ready = sem("mod_ready")
        proj_dve = sem("proj_dve")
        proj_act = sem("proj_act")
        sigmoids = sem("sigmoids")
        conv2 = sem("conv2")
        silu2 = sem("silu2")
        gate_exp = sem("gate_exp")
        gates_ready = sem("gates_ready")
        decays = sem("decays")
        decay_sums = sem("decay_sums")
        decay_max = sem("decay_max")
        decay_exp = sem("decay_exp")
        weighted = sem("weighted")
        w_turned = sem("w_turned")
        st_ready = sem("st_ready")
        m_mixed = sem("m_mixed")
        m_out = sem("m_out")
        m_sq = sem("m_sq")
        m_root = sem("m_root")
        m_normed = sem("m_normed")
        m_turned = sem("m_turned")
        m_gated = sem("m_gated")
        m_hi = sem("m_hi")
        m_lo = sem("m_lo")
        branch_sum = sem("branch_sum")
        branch_hi = sem("branch_hi")
        branch_lo = sem("branch_lo")
        qp_ready = sem("qp_ready")
        key_scored = sem("key_scored")
        key_read = sem("key_read")
        best_sub = sem("best_sub")
        best_exp = sem("best_exp")
        keys_ready = sem("keys_ready")
        keys_turned = sem("keys_turned")
        i_ready = sem("i_ready")
        hot_ready = sem("hot_ready")
        hot_used = sem("hot_used")
        gates_kept = sem("gates_kept")
        act_ready = sem("act_ready")
        act_sent = [sem(f"act_sent{i}") for i in range(RING)]
        act_back = [sem(f"act_back{i}") for i in range(RING)]
        w_ready = sem("w_ready")
        w_hi = sem("w_hi")
        w_lo = sem("w_lo")
        conv_step = sem("conv_step")
        step = sem("step")
        out_sent = sem("out_sent")

        def const(name):
            a, b = CONST[name]
            return cst[:, a:b]

        def gain(name, k=0):
            return gv[:, GAIN[name] + k:GAIN[name] + k + 1]

        def squares_before(name):
            return sum(n for _, n, _ in NORMS[:NORM_NO[name]])

        def scaled_before(name):
            return sum(n * max(k, 1) for _, n, k in NORMS[:NORM_NO[name]])

        def normed_before(name):
            return sum(n * k for _, n, k in NORMS[:NORM_NO[name]])

        added = {name: i * DC for i, name in enumerate(["conv_out", "ffn1", "attn_out", "ffn2", "mix_out", "peer"])}

        def attention_base(kind):
            return 0 if kind == "latent" else HEADS

        block = ctx.enter_context(nc.Block())
        CONST_LOADS = 3

        @block.sync
        def _(sp):
            for half in range(2):
                sp.dma_start(h[:, half * 4:half * 4 + 4], x_in[:, half * 4:half * 4 + 4]).then_inc(x_landed[half], 16)
            for n in range(RING):
                sp.dma_start(raw[:, n], stream[n]).then_inc(raw_in[n], 16)
            with sp.Fori(1, BLOCKS // RING) as i:
                for k in range(RING):
                    sp.wait_ge(lo_ready, i * RING + (k - RING + 1))
                    sp.dma_start(raw[:, k], stream[bass.ds(i * RING + k, 1)].rearrange("a p n -> (a p) n")
                                 ).then_inc(raw_in[k], 16)
            for n in range(BLOCKS // RING * RING, BLOCKS):
                sp.wait_ge(lo_ready, n - RING + 1)
                sp.dma_start(raw[:, n % RING], stream[n]).then_inc(raw_in[n % RING], 16)
            sp.wait_ge(scaled, scaled_before("final2") + DC)
            sp.dma_start(out, sq[:]).then_inc(out_sent, 16)
            sp.wait_ge(out_sent, 16)

        @block.gpsimd
        def _(pool):
            pool.wait_ge(csilu_ready, 1)

            def load(n):
                part, k = divmod(n, DC)
                pool.dma_start(ada_w[:, n % 2], ada[k * P:(k + 1) * P, part * D:(part + 1) * D]).then_inc(ada_in[n % 2], 16)

            def load_next(n):
                if n + 2 < 6 * DC:
                    load(n + 2)

            load(0)
            load(1)
            for n in range(6 * DC):
                part, k = divmod(n, DC)
                pool.wait_ge(ada_in[n % 2], (n // 2 + 1) * 16)
                if k == 0:
                    pool.tensor_scalar(ada_acc[:, part], ada_w[:, n % 2], csilu[:, k:k + 1], None, ALU.mult
                                       ).then_inc(ada_scaled, 1)
                    pool.wait_ge(ada_scaled, n + 1)
                    load_next(n)
                else:
                    wait(pool, ada_added, part * (DC - 1) + k - 1)
                    pool.tensor_scalar(ada_p[:], ada_w[:, n % 2], csilu[:, k:k + 1], None, ALU.mult
                                       ).then_inc(ada_scaled, 1)
                    pool.wait_ge(ada_scaled, n + 1)
                    load_next(n)
                    pool.tensor_tensor(ada_acc[:, part], ada_acc[:, part], ada_p[:], ALU.add).then_inc(ada_added, 1)
            pool.wait_ge(ada_added, 6 * (DC - 1))
            pool.wait_ge(mod_summed, 1)
            pool.dma_start(bias[:], band_bias).then_inc(band_in, 16)
            pool.dma_start(sk[:], sub_keys).then_inc(band_in, 16)
            pool.dma_start(gbias[:], gate_bias).then_inc(band_in, 16)

            p0 = FIRST["peer"]
            pool.wait_ge(lo_ready, p0 + LEAD)
            with pool.Fori(0, EARLY // RING) as t:
                for k in range(RING):
                    blk = block_no(p0 + LEAD + k, t)
                    s = blk[0] % RING
                    pool.wait_ge(hi_ready, number(blk) + 1)
                    pool.tensor_tensor(wl[:, s], raw[:, s], wh[:, s].bitcast(F32), ALU.subtract).then_inc(lo_ready, 1)
            for k in range(RING):
                pool.wait_ge(act_sent[k], 16 * (EARLY // RING - 1))
            with pool.Fori(0, EARLY // RING - 1) as t:
                for k in range(RING):
                    pool.wait_ge(w_ready, t * RING + (k + 1))
                    pool.dma_start(acts[:, k], put_off[bass.ds(t * RING + k, 1)].rearrange("a p n -> (a p) n")
                                   ).then_inc(act_back[k], 16)

        @block.tensor
        def _(pe):
            def three(out_ap, a_hi, a_lo, b_hi, b_lo, start, stop, skip=False):
                pe.matmul(out_ap, a_hi, b_hi, start=start, stop=False, skip_group_check=skip)
                pe.matmul(out_ap, a_hi, b_lo, start=False, stop=False, skip_group_check=skip)
                return pe.matmul(out_ap, a_lo, b_hi, start=False, stop=stop, skip_group_check=skip)

            def ready(blk):
                pe.wait_ge(lo_ready, number(blk) + 1)

            def piece(w, blk, lo, hi):
                return w[:, blk[0] % RING, lo:hi]

            def features(blk, bank, ah, al, first_wait=None):
                ready(blk)
                for c in range(DC):
                    if first_wait is not None:
                        pe.wait_ge(normed, first_wait + c + 1)
                    mm = three(wk[:, bank, 0:T], piece(wh, blk, c * P, c * P + P), piece(wl, blk, c * P, c * P + P),
                               ah[:, c], al[:, c], c == 0, c == DC - 1)
                mm.then_inc(block_used, 1)

            def tokens(blk, bank, ah, al, n, first_wait=None):
                ready(blk)
                for c in range(DC):
                    if first_wait is not None:
                        pe.wait_ge(normed, first_wait + c + 1)
                    for b in range(TB):
                        mm = three(wk[:, bank, b * P:b * P + n], ah[:, c, b * P:(b + 1) * P], al[:, c, b * P:(b + 1) * P],
                                   piece(wh, blk, c * P, c * P + n), piece(wl, blk, c * P, c * P + n),
                                   c == 0 and b == 0, c == DC - 1, skip=True)
                mm.then_inc(block_used, 1)

            def norm_sum(name, c):
                if c == 0:
                    wait(pe, rooted, NORM_NO[name])
                    if name == "ffn2":
                        pe.wait_ge(mod_ready, 1)
                pe.wait_ge(squares, squares_before(name) + c + 1)
                n = NORMS[NORM_NO[name]][1]
                mm = pe.matmul(wk[:, 3, 0:T], const("ones"), sq[:, c], start=c == 0, stop=c == n - 1)
                if c == n - 1:
                    mm.then_inc(summed, 1)

            def norm_sums(name, first=0):
                for c in range(first, NORMS[NORM_NO[name]][1]):
                    norm_sum(name, c)

            pe.wait_ge(const_in, 16 * CONST_LOADS)
            norm_sums("conv")

            def conv_tile(c, blk, first):
                wait(pe, gate_copied, c)
                features(blk, 0, xh, xl, normed_before("conv") if first else None)
                wait(pe, gated, c)
                features(after(blk, 1), 1, xh, xl)
                wait(pe, conved, c)
                features(after(blk, 2), 2, xh, xl)

            conv_tile(0, block_no(0), True)
            with pe.Fori(1, DC) as c:
                conv_tile(c, block_no(0, c), False)

            def add_out(stage, ah, al, done, count, norm):
                for c in range(DC):
                    blk = block_no(FIRST[stage] + c)
                    if c == 0:
                        pe.wait_ge(done, count)
                    wait(pe, res_add, added[stage] + c - 2 if c >= RING else 0)
                    features(blk, blk[0] % RING, ah, al)
                    if c >= 2:
                        norm_sum(norm, c - 2)
                norm_sums(norm, DC - 2)

            add_out("conv_out", yh, yl, conved_lo, DC, "ffn1")

            def ffn(stage, norm, turn):
                first = FIRST[stage]
                base = turn * FT

                def w2(blk, j, start, stop):
                    ready(blk)
                    pe.wait_ge(hid_lo, base + j + 1)
                    for o in range(DC):
                        mm = three(acc_tile(o), piece(wh, blk, o * P, o * P + P), piece(wl, blk, o * P, o * P + P),
                                   hidh[:], hidl[:], start and o % 2 == 0, stop, skip=True)
                    mm.then_inc(block_used, 1)

                b0 = first % RING
                features(block_no(first), b0, xh, xl, normed_before(norm))
                features(block_no(first + 1), (b0 + 1) % RING, xh, xl)

                def triple(j, blk, start):
                    pe.wait_ge(silu_ready, base + j)
                    features(blk, b0, xh, xl)
                    pe.wait_ge(hid_ready, base + j)
                    features(after(blk, 1), (b0 + 1) % RING, xh, xl)
                    w2(after(blk, 2), j - 1, start, False)

                triple(1, block_no(first + 2), True)
                with pe.Fori(2, FT) as j:
                    triple(j, block_no(first - 1, j), False)
                w2(block_no(first + 3 * FT - 1), FT - 1, False, True)

            ffn("ffn1", "ffn1", 0)

            norm_sums("mla")
            base = normed_before("mla")
            for k in range(7):
                blk = block_no(FIRST["latent"] + k)
                wait(pe, lat_read, k - 2)
                if k == 0:
                    features(blk, blk[0] % RING, xh, xl, base)
                elif k < 4:
                    features(blk, blk[0] % RING, xh, xl)
                elif k == 4:
                    features(blk, blk[0] % RING, yh, yl, base + DC)
                else:
                    features(blk, blk[0] % RING, yh, yl)
            norm_sums("qlat")

            pe.wait_ge(normed, normed_before("qlat") + QC)
            for k in range(6):
                blk = block_no(FIRST["uq"] + k)
                wait(pe, uq_read, k - 2)
                ready(blk)
                for t in range(2):
                    for c in range(QC):
                        at = (t * QC + c) * P
                        mm = three(wk[:, k % RING, t * T:(t + 1) * T], piece(wh, blk, at, at + P), piece(wl, blk, at, at + P),
                                   lath[:, KC + c], latl[:, KC + c], c == 0, c == QC - 1)
                mm.then_inc(block_used, 1)
                if k == 0:
                    norm_sums("kvlat")
            pe.wait_ge(normed, normed_before("kvlat") + KC)
            pe.wait_ge(uq_read, 6)
            for k in range(4):
                blk = block_no(FIRST["ukv"] + k)
                wait(pe, ukv_read, k - 1)
                ready(blk)
                b = 2 * (k % 2)
                if k < 2:
                    for t in range(4):
                        for c in range(KC):
                            at = c * 512 + t * P
                            mm = three(wk[:, b + t // 2, (t % 2) * T:(t % 2 + 1) * T], piece(wh, blk, at, at + P),
                                       piece(wl, blk, at, at + P), lath[:, c], latl[:, c], c == 0, c == KC - 1)
                else:
                    for t in range(TB):
                        for c in range(KC):
                            mm = three(wk[:, b + t], lath[:, c, t * P:(t + 1) * P], latl[:, c, t * P:(t + 1) * P],
                                       piece(wh, blk, c * 512, c * 512 + 512), piece(wl, blk, c * 512, c * 512 + 512),
                                       c == 0, c == KC - 1)
                mm.then_inc(block_used, 1)

            def attention(kind, beside):
                h0 = attention_base(kind)

                def scores(i):
                    if kind == "band":
                        pe.wait_ge(masked, TB * (h0 + i))
                        r = AHD * (i % 2)
                        for b in range(TB):
                            mm = pe.matmul(wk[:, 3, b * P:b * P + (b + 1) * P], qa[r:r + AHD, i // 2, b * P:(b + 1) * P],
                                           ka[r:r + AHD, i // 2, 0:(b + 1) * P], start=True, stop=True)
                        mm.then_inc(scored, TB)
                        return
                    for b in range(TB):
                        n = (b + 1) * P
                        unit = TB * (h0 + i) + b
                        wait(pe, masked, unit - 2)
                        bank = wk[:, unit % 3, 0:n]
                        r = 32 * (i % 4)
                        pe.matmul(bank, qn[:, i, b * P:(b + 1) * P], kn[:, i, 0:n], start=True, stop=False)
                        for s in range(2):
                            mm = pe.matmul(bank, qpe[r:r + 32, s, i // 4, b * P:(b + 1) * P], kpe[r:r + 32, s, 0:n],
                                           start=False, stop=s == 1, tile_position=(r, 0))
                        mm.then_inc(scored, 1)

                def turn(i):
                    n = h0 + i
                    wait(pe, pt_ready, n - 1)
                    for b in range(TB):
                        pe.wait_ge(probs, TB * n + b + 1)
                        for k in range(b + 1):
                            at = (b + k) * P
                            mm = pe.transpose(acc[:, n % 2, at:at + P], pr[:, b, k * P:(k + 1) * P], const("ident"))
                    mm.then_inc(turned, 1)

                def mix(i):
                    n = h0 + i
                    pe.wait_ge(pt_ready, n + 1)
                    if kind == "latent":
                        wait(pe, mixed_lo, i - 1)
                        o = acc[:, 2 + n % 2, 0:T]
                        pe.matmul(o, vm[:, 0, i], pt[:, n % 2, 0:T], start=True, stop=False, skip_group_check=True)
                        pe.matmul(acc[:, 2 + n % 2, P:T], vm[:, 1, i], pt[:, n % 2, T:3 * P], start=False, stop=True,
                                  skip_group_check=True).then_inc(mixed, 1)
                    else:
                        r = AHD * (i % 2)
                        bank = 2 + (i // 2) % 2
                        wait(pe, mixed_lo, HEADS + i // 2 - 1 if i >= 4 else 0)
                        for t in range(TB):
                            mm = pe.matmul(acc[r:r + AHD, bank, t * P:T], va[:, t, i // 2, r:r + AHD],
                                           pt[:, n % 2, 2 * t * P:2 * t * P + T - t * P],
                                           start=t == 0, stop=t == 1, skip_group_check=True)
                        mm.then_inc(mixed, 1)

                scores(0)
                for i in range(HEADS):
                    if kind == "band":
                        beside(i, 0)
                    if i + 1 < HEADS:
                        scores(i + 1)
                    turn(i)
                    if kind == "band":
                        beside(i, 1)
                    else:
                        beside(i)
                    if i >= 1:
                        mix(i - 1)
                mix(HEADS - 1)

            pe.wait_ge(ukv_read, 4)
            pe.wait_ge(trig, 3)
            pe.wait_ge(ada_added, 6 * (DC - 1))

            def mod_sums(i):
                for j in range(6 * i, 6 * i + 6):
                    mm = pe.matmul(wk[:, 3, j:j + 1], ada_acc[:, j // DC, (j % DC) * P:(j % DC + 1) * P],
                                   const("ones")[:, 0:1], start=True, stop=True)
                if i == HEADS - 1:
                    mm.then_inc(mod_summed, 1)

            attention("latent", mod_sums)
            add_out("attn_out", yh, yl, mixed_lo, HEADS, "ffn2")
            ffn("ffn2", "ffn2", 1)
            norm_sums("final")

            norm_sums("mix")
            pe.wait_ge(mod_ready, 1)
            base = normed_before("mix")
            def proj(k):
                blk = block_no(FIRST["proj"] + k)
                bank = blk[0] % RING
                if k == 0:
                    tokens(blk, bank, xh, xl, 2 * BH, base)
                elif 9 <= k < 17:
                    s = (k - 9) % 4
                    ready(blk)
                    if k == 9:
                        pe.wait_ge(proj_dve, 9)
                    elif s == 0:
                        pe.wait_ge(proj_act, 1)
                    for b in range(TB):
                        for c in range(2):
                            mm = three(wk[:, b], xh[:, 2 * s + c, b * P:(b + 1) * P], xl[:, 2 * s + c, b * P:(b + 1) * P],
                                       piece(wh, blk, c * 512, c * 512 + 512), piece(wl, blk, c * 512, c * 512 + 512),
                                       s == 0 and c == 0, s == 3 and c == 1)
                    mm.then_inc(block_used, 1)
                else:
                    if 17 <= k < 20:
                        pe.wait_ge(proj_act, 2)
                    elif k >= 20:
                        pe.wait_ge(proj_act, k - 17)
                    elif k > RING:
                        pe.wait_ge(proj_dve, k - RING + 1)
                    features(blk, bank, xh, xl)

            for k in range(13):
                proj(k)

            pe.wait_ge(silu2, 2 * BH)

            def m_scores(unit):
                i, b = divmod(unit, TB)
                n = (b + 1) * P
                pe.wait_ge(decays, i + 1)
                if b == 0:
                    pe.matmul(acc[:, 0, 0:P + 1], const("upto"), rr[:, 0, 0:P + 1], start=True, stop=True)
                else:
                    pe.matmul(acc[:, 0, 0:T + 1], const("upto"), rr[:, 1], start=True, stop=False, skip_group_check=True)
                    pe.matmul(acc[:, 0, 0:P + 1], const("ones"), rr[:, 0, 0:P + 1], start=False, stop=True,
                              skip_group_check=True)
                pe.matmul(acc[:, 1, 0:n], qk[:, i, b * P:n], qk[:, BH + i, 0:n], start=True, stop=True
                          ).then_inc(decay_sums, 1)

            m_scores(0)
            for unit in range(TB * BH):
                i, b = divmod(unit, TB)
                proj(13 + 2 * unit)
                pe.wait_ge(weighted, unit + 1)
                for k in range(b + 1):
                    mm = pe.transpose(acc[:, 2, k * P:(k + 1) * P], sv[:, k * P:(k + 1) * P], const("ident"))
                mm.then_inc(w_turned, 1)
                if unit + 1 < TB * BH:
                    m_scores(unit + 1)
                proj(14 + 2 * unit)
                if unit == 0:
                    pe.wait_ge(proj_act, 1)
                pe.wait_ge(st_ready, unit + 1)
                wait(pe, m_out, unit)
                for k in range(b + 1):
                    mm = pe.matmul(acc[:, 3, 0:P], st[:, k * P:(k + 1) * P], vb[:, k, i], start=k == 0, stop=k == b)
                mm.then_inc(m_mixed, 1)
            proj(29)
            pe.wait_ge(m_normed, 1)
            for i in range(BH):
                wait(pe, m_gated, i - 1)
                for b in range(TB):
                    mm = pe.transpose(acc[:, i % 2, b * P:(b + 1) * P], hb[:, b, i], const("ident"))
                mm.then_inc(m_turned, 1)

            pe.wait_ge(m_gated, BH)

            def two_more(i, half):
                if 30 + 2 * i + half < 45:
                    proj(30 + 2 * i + half)

            attention("band", two_more)
            pe.wait_ge(mixed_lo, HEADS + AH // 2)
            pe.wait_ge(m_lo, BH)
            pe.wait_ge(proj_act, 30)
            for k in range(DC):
                blk = block_no(FIRST["branch"] + k)
                ready(blk)
                wait(pe, branch_sum, k - 1)
                for s in range(2):
                    for c in range(4):
                        at = (4 * s + c) * P
                        mm = three(wk[:, 2 * (k % 2) + s, 0:T], piece(wh, blk, at, at + P), piece(wl, blk, at, at + P),
                                   yh[:, 4 * s + c], yl[:, 4 * s + c], c == 0, c == 3)
                mm.then_inc(block_used, 1)
            add_out("mix_out", xh, xl, branch_lo, DC, "peer")

            base = normed_before("peer")
            for k in range(2 * PH):
                blk = block_no(FIRST["peer_q"] + k)
                wait(pe, qp_ready, k - 2)
                features(blk, blk[0] % RING, xh, xl, base if k == 0 else None)
            pe.wait_ge(qp_ready, 2 * PH)
            pe.wait_ge(band_in, 48)
            for n in range(4 * TB):
                b, g = divmod(n, 4)
                wait(pe, key_read, n - 3)
                for j in range(4):
                    mm = pe.matmul(acc[:, g, j * P:(j + 1) * P], qp[:, 4 * g + j, b * P:(b + 1) * P], sk[:, 4 * g + j],
                                   start=True, stop=True)
                mm.then_inc(key_scored, 1)

            p0 = FIRST["peer"]

            def early(i, k, blk):
                if not isinstance(i, int) or i >= RING:
                    pe.wait_ge(act_ready, i + (1 - RING))
                features(blk, k, xh, xl)

            for i in range(RING):
                early(i, i, block_no(p0 + i))
            with pe.Fori(1, EARLY_CHOICE // RING - 1) as t:
                for k in range(RING):
                    early(t * RING + k, k, block_no(p0 + k, t))
            for i in range(EARLY_CHOICE - RING, EARLY_CHOICE):
                if i == EARLY_CHOICE - 1:
                    pe.wait_ge(keys_ready, TB)
                    pe.wait_ge(key_read, 4 * TB)
                    for b in range(TB):
                        for s in range(3):
                            mm = pe.transpose(acc[:, b, s * P:(s + 1) * P], key[:, b, s].rearrange("p h k -> p (h k)"),
                                              const("ident"))
                        mm.then_inc(keys_turned, 1)
                early(i, i % RING, block_no(p0 + i))

            def gate_group(g, par):
                pe.wait_ge(hot_ready, g + 1)
                if not isinstance(g, int) or g >= 2:
                    pe.wait_ge(gates_kept, g - 1)
                for j in range(4):
                    mm = pe.matmul(acc[:, 2 + par, j * P:(j + 1) * P], hot[:, par, 1, j], hot[:, par, 0, j],
                                   start=True, stop=True)
                mm.then_inc(hot_used, 1)

            def gates_and_early(t, first_trip):
                for k in range(RING):
                    for par in range(2):
                        gate_group(2 * k + par if first_trip else t * (2 * RING) + (2 * k + par), par)
                    if first_trip:
                        early(EARLY_CHOICE + k, k, block_no(p0 + EARLY_CHOICE + k))
                    else:
                        early(t * RING + (EARLY_CHOICE + k), k, block_no(p0 + EARLY_CHOICE + k, t))

            gates_and_early(0, True)
            with pe.Fori(1, GATE_TRIPS) as t:
                gates_and_early(t, False)
            for k in range(RING):
                i = EARLY - RING + k
                for g in range(T // 4 - GATE_TAIL + 2 * k, min(T // 4 - GATE_TAIL + 2 * k + 2, T // 4)):
                    gate_group(g, g % 2)
                early(i, k, block_no(p0 + i))

            def experts_out(blk, i, k, start, stop):
                ready(blk)
                pe.wait_ge(w_lo, i + 1)
                for o in range(DC):
                    mm = three(acc_tile(o), piece(wh, blk, o * P, o * P + P), piece(wl, blk, o * P, o * P + P),
                               ph[:, k], pl[:, k], start and o % 2 == 0, stop, skip=True)
                mm.then_inc(block_used, 1)

            pe.wait_ge(gates_kept, T // 4)
            for i in range(RING):
                experts_out(block_no(p0 + EARLY + i), i, i, i == 0, False)
            with pe.Fori(1, EARLY // RING) as t:
                for k in range(RING):
                    experts_out(block_no(p0 + EARLY + k, t), t * RING + k, k, False, False)

            def pair(i, k, blk):
                pe.wait_ge(act_ready, i)
                features(blk, (k + 1) % RING, xh, xl)
                experts_out(after(blk, 1), i, k, False, False)

            p1 = p0 + 2 * EARLY
            pe.wait_ge(act_ready, EARLY)
            features(block_no(p1), 0, xh, xl)
            pair(EARLY, 0, block_no(p1 + 1))
            with pe.Fori(0, (NK - 2 - EARLY) // RING) as t:
                for k in range(RING):
                    pair(t * RING + (EARLY + 1 + k), (1 + k) % RING, block_no(p1 + 3 + 2 * k, t, 2))
            experts_out(block_no(BLOCKS - 1), NK - 1, (NK - 1) % RING, False, True)
            norm_sums("final2")

        @block.scalar
        def _(sc_e):
            def hi(blk):
                n = number(blk)
                sc_e.wait_ge(raw_in[blk[0] % RING], (lap(blk) + 1) * 16)
                wait(sc_e, block_used, n - (RING - 1))
                nc.scalar.activation(wh[:, blk[0] % RING], raw[:, blk[0] % RING], ACT.Copy).then_inc(hi_ready, 1)

            def ahead(blk):
                if blk[1] is None and blk[0] + LEAD >= BLOCKS:
                    return
                hi(after(blk, LEAD))

            def used(blk):
                sc_e.wait_ge(block_used, number(blk) + 1)

            def square(name, c, src, src_sem=None, src_base=0):
                if c == 0:
                    wait(sc_e, normed, normed_before(name))
                if src_sem is not None:
                    sc_e.wait_ge(src_sem, src_base + c + 1)
                nc.scalar.activation(sq[:, c], src[:, c], ACT.Square).then_inc(squares, 1)

            def norm(name, src, src_sem=None, src_base=0, splits=(), first=0):
                n = NORMS[NORM_NO[name]][1]
                sc0 = scaled_before(name)
                nc.scalar.preload_act_table(ACT.Sqrt)
                for c in range(first, n):
                    square(name, c, src, src_sem, src_base)
                sc_e.wait_ge(summed, NORM_NO[name] + 1)
                nc.scalar.activation(sd[:], wk[:, 3, 0:T], ACT.Sqrt, bias=cols[:, 0:1], scale=1.0 / (n * P)
                                     ).then_inc(rooted, 1)
                for s, (dst, off, b) in enumerate(splits):
                    for c in range(n):
                        sc_e.wait_ge(scaled, sc0 + s * n + c + 1)
                        if b is None:
                            ins = nc.scalar.activation(dst[:, off + c], sq[:, c], ACT.Copy)
                        else:
                            ins = nc.scalar.activation(dst[:, off + c], sq[:, c], ACT.Identity,
                                                       bias=mod[:, b * DC + c:b * DC + c + 1])
                        ins.then_inc(normed_hi, 1)

            sc_e.dma_start(gv[:], gains).then_inc(const_in, 16)
            sc_e.dma_start(cst[:], consts).then_inc(const_in, 16)
            sc_e.dma_start(pos_i[:], positions.partition_broadcast(P)).then_inc(const_in, 16)
            sc_e.wait_ge(const_in, 16 * CONST_LOADS)
            hi(block_no(0))
            sc_e.wait_ge(set_up, 5)
            for c in range(DC):
                sc_e.wait_ge(x_landed[c // 4], 16)
                square("conv", c, h)
            hi(block_no(1))
            norm("conv", h, splits=[(xh, 0, None)], first=DC)

            nc.scalar.activation(csilu[:], gv[:, GAIN["c"]:GAIN["c"] + DC], ACT.Silu).then_inc(csilu_ready, 1)
            sc_e.wait_ge(angles, 1)
            nc.scalar.activation(ang[:, 7], ang[:, 3], ACT.Sin).then_inc(trig, 1)
            nc.scalar.activation(ang[:, 6], ang[:, 4], ACT.Sin, bias=cols[:, 1:2], scale=-1.0).then_inc(trig, 1)


            def conv_tile(c, blk):
                ahead(blk)
                used(blk)
                wait(sc_e, gated, c)
                nc.scalar.activation(gc[:], wk[:, 0, 0:T], ACT.Copy).then_inc(gate_copied, 1)
                ahead(after(blk, 1))
                ahead(after(blk, 2))
                sc_e.wait_ge(conved, c + 1)
                dst = yh[:, c] if isinstance(c, int) else yh[:, bass.ds(c, 1)].rearrange("p a t -> p (a t)")
                nc.scalar.activation(dst, cv[:, 2], ACT.Copy).then_inc(conved_hi, 1)

            conv_tile(0, block_no(0))
            with sc_e.Fori(1, DC) as c:
                conv_tile(c, block_no(0, c))

            def add_out(stage, norm_name):
                for c in range(DC):
                    ahead(block_no(FIRST[stage] + c))
                    if c >= 1:
                        square(norm_name, c - 1, h, res_add, added[stage])

            add_out("conv_out", "ffn1")

            def ffn(stage, norm_name, turn, res):
                first = FIRST[stage]
                base = turn * FT
                b0 = first % RING
                norm(norm_name, h, res_add, res, splits=[(xh, 0, None)], first=DC - 1)

                def silu(blk, j):
                    used(blk)
                    wait(sc_e, hid_ready, base + j)
                    nc.scalar.activation(sg[:], wk[:, b0, 0:T], ACT.Silu).then_inc(silu_ready, 1)

                def split_hid(j, used_before):
                    sc_e.wait_ge(hid_ready, base + j + 1)
                    sc_e.wait_ge(block_used, used_before)
                    nc.scalar.activation(hidh[:], hid[:], ACT.Copy).then_inc(hid_hi, 1)

                ahead(block_no(first))
                silu(block_no(first), 0)
                ahead(block_no(first + 1))

                def triple(j, blk):
                    ahead(blk)
                    split_hid(j - 1, number(blk))
                    silu(blk, j)
                    ahead(after(blk, 1))
                    ahead(after(blk, 2))

                triple(1, block_no(first + 2))
                with sc_e.Fori(2, FT) as j:
                    triple(j, block_no(first - 1, j))
                last = block_no(first + 3 * FT - 1)
                split_hid(FT - 1, number(last))
                ahead(last)

            ffn("ffn1", "ffn1", 0, 0)
            norm("mla", h, res_add, DC, splits=[(xh, 0, None), (yh, 0, None)])
            for k in range(7):
                ahead(block_no(FIRST["latent"] + k))
            norm("qlat", lat[:, KC:], lat_read, 4, splits=[(lath, KC, None)])
            for k in range(6):
                ahead(block_no(FIRST["uq"] + k))
                if k == 0:
                    norm("kvlat", lat, splits=[(lath, 0, None)])
            for k in range(4):
                ahead(block_no(FIRST["ukv"] + k))

            def attention(kind, beside=None):
                h0 = attention_base(kind)

                def exps(i):
                    for b in range(TB):
                        sc_e.wait_ge(masked, TB * (h0 + i) + b + 1)
                        wait(sc_e, turned, h0 + i)
                        nc.scalar.activation(pr[:, b, 0:(b + 1) * P], sc[:, b, 0:(b + 1) * P], ACT.Exp,
                                             bias=stat[:, 0, TB * i + b:TB * i + b + 1],
                                             accum_out=stat[:, 1, TB * i + b:TB * i + b + 1]).then_inc(expd, 1)

                def keep_hi(j):
                    if kind == "latent":
                        sc_e.wait_ge(mixed, j + 1)
                        nc.scalar.activation(yh[:, j], acc[:, 2 + j % 2, 0:T], ACT.Copy).then_inc(mixed_hi, 1)
                    elif j % 2 == 1:
                        sc_e.wait_ge(mixed, h0 + j + 1)
                        nc.scalar.activation(yh[:, j // 2], acc[:, 2 + (j // 2) % 2, 0:T], ACT.Copy).then_inc(mixed_hi, 1)

                exps(0)
                for i in range(HEADS):
                    if beside:
                        beside(i, 0)
                    n = h0 + i
                    sc_e.wait_ge(turned, n + 1)
                    wait(sc_e, mixed, n - 1)
                    nc.scalar.activation(pt[:, n % 2], acc[:, n % 2, 0:3 * P], ACT.Copy).then_inc(pt_ready, 1)
                    if i + 1 < HEADS:
                        exps(i + 1)
                    if beside:
                        beside(i, 1)
                    if i >= 1:
                        keep_hi(i - 1)
                keep_hi(HEADS - 1)

            attention("latent")
            add_out("attn_out", "ffn2")
            ffn("ffn2", "ffn2", 1, 2 * DC)
            norm("final", h, res_add, 3 * DC)
            norm("mix", h, scaled, scaled_before("final"), splits=[(xh, 0, 0)])

            def proj(k):
                blk = block_no(FIRST["proj"] + k)
                ahead(blk)
                if 2 <= k < 10:
                    sc_e.wait_ge(conv2, k - 1)
                    nc.scalar.activation(qk[:, k - 2], uc[:, CK - 1], ACT.Silu).then_inc(silu2, 1)
                if k < 12 or k in (13, 14, 15):
                    return
                used(blk)
                src = wk[:, blk[0] % RING, 0:T]
                if k in (12, 16):
                    dst = vb[:].rearrange("p b h d -> p b (h d)") if k == 12 else va[:].rearrange("p b h d -> p b (h d)")
                    nc.scalar.activation(dst, wk[:, 0:2], ACT.Copy).then_inc(proj_act, 1)
                elif k < 25:
                    dst = qa[:, k - 17] if k < 21 else ka[:, k - 21]
                    nc.scalar.activation(dst, src, ACT.Copy).then_inc(proj_act, 1)
                else:
                    dst = ob[:, k - 25] if k < 29 else (ga if k < 37 else gb)[:, (k - 29) % DC]
                    nc.scalar.activation(dst, src, ACT.Tanh, scale=0.5).then_inc(proj_act, 1)
                    sc_e.wait_ge(proj_act, k - 14)
                    nc.scalar.activation(dst, dst, ACT.Copy, scale=0.5, bias=0.5).then_inc(sigmoids, 1)

            for k in range(11):
                proj(k)
            sc_e.wait_ge(gates_ready, 1)
            nc.scalar.activation(gw[:, :, 1], gw[:, :, 0], ACT.Exp, scale=-1.0).then_inc(gate_exp, 1)
            sc_e.wait_ge(gate_exp, 1)
            nc.scalar.activation(gw[:, :, 2], gw[:, :, 1], ACT.Ln, bias=cols[:, 3:4]).then_inc(gate_exp, 1)
            proj(11)
            proj(12)

            def m_exps(unit):
                n = (unit % TB + 1) * P
                sc_e.wait_ge(decay_max, unit + 1)
                nc.scalar.activation(dm[:, 1:n + 1], dm[:, 1:n + 1], ACT.Exp, bias=ms[:, 0, unit:unit + 1]
                                     ).then_inc(decay_exp, 1)
                nc.scalar.activation(ms[:, 1, unit:unit + 1], ms[:, 0, unit:unit + 1], ACT.Exp).then_inc(decay_exp, 1)

            m_exps(0)
            for unit in range(TB * BH):
                i, b = divmod(unit, TB)
                n = (b + 1) * P
                proj(13 + 2 * unit)
                sc_e.wait_ge(w_turned, unit + 1)
                wait(sc_e, m_mixed, unit)
                nc.scalar.activation(st[:, 0:n], acc[:, 2, 0:n], ACT.Copy).then_inc(st_ready, 1)
                proj(14 + 2 * unit)
                if unit + 1 < TB * BH:
                    m_exps(unit + 1)
                sc_e.wait_ge(m_out, unit + 1)
                nc.scalar.activation(uc[:, 3, 0:P], hb[:, b, i], ACT.Square, accum_out=ms[:, 4, unit:unit + 1]
                                     ).then_inc(m_sq, 1)
            sc_e.wait_ge(m_sq, TB * BH)
            nc.scalar.activation(ms[:, 5], ms[:, 4], ACT.Sqrt, bias=cols[:, 0:1], scale=1.0 / BD).then_inc(m_root, 1)
            proj(29)
            for i in range(BH):
                sc_e.wait_ge(m_gated, i + 1)
                nc.scalar.activation(yh[:, 4 + i], uc[:, i % 2], ACT.Copy).then_inc(m_hi, 1)
            attention("band", lambda i, half: proj(30 + 2 * i + half) if 30 + 2 * i + half < 45 else None)
            for k in range(DC):
                ahead(block_no(FIRST["branch"] + k))
                sc_e.wait_ge(branch_sum, k + 1)
                nc.scalar.activation(xh[:, k], uc[:, 2], ACT.Copy).then_inc(branch_hi, 1)
            add_out("mix_out", "peer")
            norm("peer", h, res_add, 4 * DC, splits=[(xh, 0, 3)], first=DC - 1)
            for k in range(2 * PH):
                blk = block_no(FIRST["peer_q"] + k)
                ahead(blk)
                used(blk)
                nc.scalar.activation(qp[:, k], wk[:, blk[0] % RING, 0:T], ACT.Copy).then_inc(qp_ready, 1)
            for n in range(4 * TB):
                b, g = divmod(n, 4)
                sc_e.wait_ge(key_scored, n + 1)
                nc.scalar.activation(ks[:, b, 4 * g:4 * g + 4], acc[:, g].rearrange("p (s k) -> p s k", s=4), ACT.Copy
                                     ).then_inc(key_read, 1)

            p0 = FIRST["peer"]

            def activate(blk, i, k):
                used(blk)
                nc.scalar.activation(acts[:, k], wk[:, k, 0:T], ACT.Gelu_apprx_tanh).then_inc(act_ready, 1)

            def early(i, k, lap_no, blk, keep=False):
                ahead(blk)
                if not isinstance(lap_no, int) or lap_no > 0:
                    sc_e.wait_ge(act_sent[k], 16 * lap_no)
                activate(blk, i, k)
                if not keep:
                    sc_e.wait_ge(act_ready, i + 1)
                    row = put_off[i] if isinstance(i, int) else put_off[bass.ds(i, 1)].rearrange("a p n -> (a p) n")
                    sc_e.dma_start(row, acts[:, k]).then_inc(act_sent[k], 16)

            for i in range(RING):
                early(i, i, 0, block_no(p0 + i))
            with sc_e.Fori(1, EARLY_CHOICE // RING - 1) as t:
                for k in range(RING):
                    early(t * RING + k, k, t, block_no(p0 + k, t))
            sc_e.wait_ge(best_sub, TB)
            nc.scalar.activation(key[:, :, 2], best[:], ACT.Exp).then_inc(best_exp, 1)
            for i in range(EARLY_CHOICE - RING, EARLY_CHOICE):
                if i == EARLY_CHOICE - 1:
                    for b in range(TB):
                        sc_e.wait_ge(keys_turned, b + 1)
                        nc.scalar.activation(i_t[:, :, b * P:(b + 1) * P],
                                             acc[:, b, 0:3 * P].rearrange("p (s t) -> p s t", s=3), ACT.Copy
                                             ).then_inc(i_ready, 1)
                early(i, i % RING, i // RING, block_no(p0 + i))

            def gate_group(g, par):
                sc_e.wait_ge(hot_used, g + 1)
                at = g * 4
                tok = (gates[:, at:at + 4] if isinstance(g, int) else gates[:, bass.ds(at, 4)]).rearrange("p t k -> p (t k)")
                nc.scalar.activation(tok, acc[:, 2 + par], ACT.Copy).then_inc(gates_kept, 1)

            with sc_e.Fori(0, GATE_TRIPS) as t:
                for k in range(RING):
                    for par in range(2):
                        gate_group(t * (2 * RING) + (2 * k + par), par)
                    early(t * RING + (EARLY_CHOICE + k), k, t + EARLY_CHOICE // RING,
                          block_no(p0 + EARLY_CHOICE + k, t))
            for k in range(RING):
                i = EARLY - RING + k
                for g in range(T // 4 - GATE_TAIL + 2 * k, min(T // 4 - GATE_TAIL + 2 * k + 2, T // 4)):
                    gate_group(g, g % 2)
                early(i, k, i // RING, block_no(p0 + i), keep=True)

            def weights_hi(i, k, blk):
                sc_e.wait_ge(w_ready, i + 1)
                if blk is not None:
                    used(blk)
                nc.scalar.activation(ph[:, k], w32[:], ACT.Copy).then_inc(w_hi, 1)

            p_out = p0 + EARLY
            weights_hi(0, 0, None)
            weights_hi(1, 1, None)
            for i in range(RING):
                ahead(block_no(p_out + i))
                weights_hi(i + 2, (i + 2) % RING, block_no(p_out + i - 1) if i >= 1 else None)
            with sc_e.Fori(1, EARLY // RING - 1) as t:
                for k in range(RING):
                    ahead(block_no(p_out + k, t))
                    weights_hi(t * RING + (k + 2), (k + 2) % RING, block_no(p_out + k - 1, t))
            for i in range(EARLY - RING, EARLY):
                ahead(block_no(p_out + i))
                if i + 2 < EARLY:
                    weights_hi(i + 2, (i + 2) % RING, block_no(p_out + i - 1))

            def later(blk, i, k):
                ahead(blk)
                used(blk)
                sc_e.wait_ge(w_ready, i - 2)
                nc.scalar.activation(acts[:, k], wk[:, k, 0:T], ACT.Gelu_apprx_tanh).then_inc(act_ready, 1)

            p1 = p0 + 2 * EARLY
            later(block_no(p1), EARLY, 0)

            def pair(i, k, blk):
                sc_e.wait_ge(w_ready, i + 1)
                sc_e.wait_ge(block_used, number(blk) - 4)
                nc.scalar.activation(ph[:, k], w32[:], ACT.Copy).then_inc(w_hi, 1)
                later(blk, i + 1, (k + 1) % RING)
                ahead(after(blk, 1))

            pair(EARLY, 0, block_no(p1 + 1))
            with sc_e.Fori(0, (NK - 2 - EARLY) // RING - 1) as t:
                for k in range(RING):
                    pair(t * RING + (EARLY + 1 + k), (1 + k) % RING, block_no(p1 + 3 + 2 * k, t, 2))
            for i in range(NK - 1 - RING, NK - 1):
                pair(i, i % RING, block_no(p1 + 1 + 2 * (i - EARLY)))
            sc_e.wait_ge(w_ready, NK)
            nc.scalar.activation(ph[:, (NK - 1) % RING], w32[:], ACT.Copy).then_inc(w_hi, 1)
            norm("final2", h, res_add, 5 * DC)

        @block.vector
        def _(dve):
            v = nc.vector
            done = [0]

            def chain(ins):
                done[0] += 1
                ins.then_inc(step, 1)
                dve.wait_ge(step, done[0])

            def lo(blk):
                s = blk[0] % RING
                dve.wait_ge(hi_ready, number(blk) + 1)
                v.tensor_tensor(wl[:, s], raw[:, s], wh[:, s].bitcast(F32), ALU.subtract).then_inc(lo_ready, 1)

            def ahead(blk):
                if blk[1] is None and blk[0] + LEAD >= BLOCKS:
                    return
                lo(after(blk, LEAD))

            def used(blk):
                dve.wait_ge(block_used, number(blk) + 1)

            def norm(name, src, splits=(), dst=None):
                n = NORMS[NORM_NO[name]][1]
                sc0, hi0 = scaled_before(name), normed_before(name)
                dve.wait_ge(rooted, NORM_NO[name] + 1)
                wait(dve, scaled, sc0)
                wait(dve, normed, hi0)
                chain(v.reciprocal(rs[:], sd[:]))

                def scale(g, c, to):
                    v.scalar_tensor_tensor(out=to, in0=src[:, c], scalar=g(c), in1=rs[:], op0=ALU.mult,
                                           op1=ALU.mult).then_inc(scaled, 1)

                if dst is not None:
                    for c in range(n):
                        scale(dst[0], c, dst[1][:, c])
                    return
                for s, (g, th, tl, off, shift) in enumerate(splits):
                    def rest(c):
                        dve.wait_ge(normed_hi, hi0 + s * n + c + 1)
                        a, b = sq[:, c], th[:, off + c].bitcast(F32)
                        if shift is None:
                            ins = v.tensor_tensor(tl[:, off + c], a, b, ALU.subtract)
                        else:
                            ins = v.scalar_tensor_tensor(out=tl[:, off + c], in0=a, in1=b, op0=ALU.add, op1=ALU.subtract,
                                                         scalar=mod[:, shift * DC + c:shift * DC + c + 1])
                        ins.then_inc(normed, 1)

                    for c in range(n):
                        if s > 0:
                            dve.wait_ge(normed, hi0 + (s - 1) * n + c + 1)
                        scale(g, c, sq[:, c])
                        if c >= 1:
                            rest(c - 1)
                    rest(n - 1)

            def gain_of(name):
                return lambda c: gain(name, c)

            def columns(t, base=0):
                return lambda c: t[:, base + c:base + c + 1]

            v.memset(cols[:, 0:1], EPS).then_inc(set_up, 1)
            v.memset(cols[:, 1:2], float(np.pi / 2)).then_inc(set_up, 1)
            v.memset(cols[:, 2:3], 0.0).then_inc(set_up, 1)
            v.memset(cols[:, 3:4], 1.0).then_inc(set_up, 1)
            v.memset(z[:, 0:CW - 1], 0.0).then_inc(set_up, 1)
            dve.wait_ge(set_up, 5)
            dve.wait_ge(const_in, 16 * CONST_LOADS)
            lo(block_no(0))
            lo(block_no(1))
            norm("conv", h, splits=[(gain_of("conv"), xh, xl, 0, None)])
            chain(v.tensor_copy(ang[:, 0], pos_i[:]))
            chain(v.tensor_scalar(ang[:, 1], ang[:, 0], gain("inv_freq"), None, ALU.mult))
            chain(v.tensor_scalar(ang[:, 2], ang[:, 1], float(1 / (2 * np.pi)), ROUND, ALU.mult, ALU.add))
            chain(v.tensor_scalar(ang[:, 2], ang[:, 2], -ROUND, None, ALU.add))
            for k, part in enumerate(TWO_PI_PARTS):
                chain(v.scalar_tensor_tensor(out=ang[:, 1], in0=ang[:, 2], scalar=-part, in1=ang[:, 1],
                                             op0=ALU.mult, op1=ALU.add))
            chain(v.tensor_scalar(ang[:, 3], ang[:, 1], PI_BELOW, -PI_BELOW, ALU.min, ALU.max))
            v.scalar_tensor_tensor(out=ang[:, 4], in0=ang[:, 3], scalar=-1.0, in1=ang[:, 3], op0=ALU.mult, op1=ALU.max
                                   ).then_inc(angles, 1)


            def conv_tile(c, blk):
                def at(t, k=0, width=1):
                    return t[:, bass.ds(c * width + k, 1)] if not isinstance(c, int) else \
                        t[:, c * width + k:c * width + k + 1]

                w0 = GAIN["conv_w"]
                taps = gv[:, w0:w0 + CW * DC]
                base = c * (CW + 1)
                ahead(blk)
                used(after(blk, 1))
                dve.wait_ge(gate_copied, c + 1)
                wait(dve, conv_step, c * CW)
                wait(dve, conved_lo, c)
                v.tensor_tensor(z[:, CW - 1:], gc[:], wk[:, 1, 0:T], ALU.mult).then_inc(gated, 1)
                ahead(after(blk, 1))
                dve.wait_ge(gated, c + 1)
                v.tensor_scalar(cv[:, 0], z[:, 0:T], at(taps, 0, CW), None, ALU.mult).then_inc(conv_step, 1)
                dve.wait_ge(conv_step, c * CW + 1)
                v.scalar_tensor_tensor(out=cv[:, 1], in0=z[:, 1:T + 1], scalar=at(taps, 1, CW), in1=cv[:, 0],
                                       op0=ALU.mult, op1=ALU.add).then_inc(conv_step, 1)
                dve.wait_ge(conv_step, c * CW + 2)
                v.scalar_tensor_tensor(out=cv[:, 0], in0=z[:, 2:T + 2], scalar=at(taps, 2, CW), in1=cv[:, 1],
                                       op0=ALU.mult, op1=ALU.add).then_inc(conv_step, 1)
                ahead(after(blk, 2))
                dve.wait_ge(conv_step, c * CW + 3)
                used(after(blk, 2))
                v.tensor_tensor(cv[:, 2], cv[:, 0], wk[:, 2, 0:T], ALU.mult).then_inc(conved, 1)
                dve.wait_ge(conved_hi, c + 1)
                tile = (lambda t: t[:, c]) if isinstance(c, int) else \
                    (lambda t: t[:, bass.ds(c, 1)].rearrange("p a t -> p (a t)"))
                v.tensor_tensor(tile(yl), cv[:, 2], tile(yh).bitcast(F32), ALU.subtract).then_inc(conved_lo, 1)

            conv_tile(0, block_no(0))
            with dve.Fori(1, DC) as c:
                conv_tile(c, block_no(0, c))

            def add_out(stage, factor=None):
                for c in range(DC):
                    blk = block_no(FIRST[stage] + c)
                    ahead(blk)
                    used(blk)
                    src = wk[:, blk[0] % RING, 0:T]
                    if factor is None:
                        ins = v.tensor_tensor(h[:, c], h[:, c], src, ALU.add)
                    else:
                        ins = v.scalar_tensor_tensor(out=h[:, c], in0=src, scalar=factor(c), in1=h[:, c], op0=ALU.mult,
                                                     op1=ALU.add)
                    ins.then_inc(res_add, 1)

            add_out("conv_out")

            def ffn(stage, norm_name, turn):
                first = FIRST[stage]
                base = turn * FT
                b0 = first % RING
                norm(norm_name, h, splits=[(gain_of(norm_name), xh, xl, 0, None)])

                def product(blk, j):
                    used(blk)
                    dve.wait_ge(silu_ready, base + j + 1)
                    wait(dve, hid_lo, base + j)
                    v.tensor_tensor(hid[:], sg[:], wk[:, (b0 + 1) % RING, 0:T], ALU.mult).then_inc(hid_ready, 1)

                def rest(j):
                    dve.wait_ge(hid_hi, base + j + 1)
                    v.tensor_tensor(hidl[:], hid[:], hidh[:].bitcast(F32), ALU.subtract).then_inc(hid_lo, 1)

                ahead(block_no(first))
                ahead(block_no(first + 1))
                product(block_no(first + 1), 0)

                def triple(j, blk):
                    ahead(blk)
                    rest(j - 1)
                    ahead(after(blk, 1))
                    product(after(blk, 1), j)
                    ahead(after(blk, 2))

                triple(1, block_no(first + 2))
                with dve.Fori(2, FT) as j:
                    triple(j, block_no(first - 1, j))
                last = block_no(first + 3 * FT - 1)
                rest(FT - 1)
                ahead(last)
                used(last)
                for c in range(DC):
                    v.tensor_tensor(h[:, c], h[:, c], acc_tile(c), ALU.add).then_inc(res_add, 1)

            ffn("ffn1", "ffn1", 0)
            norm("mla", h, splits=[(gain_of("kv"), xh, xl, 0, None), (gain_of("mla"), yh, yl, 0, None)])
            dve.wait_ge(trig, 2)
            for k in range(7):
                blk = block_no(FIRST["latent"] + k)
                ahead(blk)
                used(blk)
                b = blk[0] % RING
                if k < 2:
                    v.tensor_copy(lat[:, k], wk[:, b, 0:T]).then_inc(lat_read, 1)
                elif k == 3:
                    x1, x2 = wk[:, (b - 1) % RING, 0:T], wk[:, b, 0:T]
                    cos, sin = ang[:, 6], ang[:, 7]
                    v.tensor_tensor(rt[:, 0, 0:T], x2, sin, ALU.mult).then_inc(step, 1)
                    v.tensor_tensor(rt[:, 0, T:2 * T], x2, cos, ALU.mult).then_inc(step, 1)
                    v.tensor_tensor(rt[:, 1, 0:T], x1, cos, ALU.mult).then_inc(step, 1)
                    done[0] += 3
                    chain(v.tensor_tensor(rt[:, 1, T:2 * T], x1, sin, ALU.mult))
                    v.tensor_tensor(kpe[:, 0], rt[:, 1, 0:T], rt[:, 0, 0:T], ALU.subtract).then_inc(lat_read, 1)
                    v.tensor_tensor(kpe[:, 1], rt[:, 1, T:2 * T], rt[:, 0, T:2 * T], ALU.add).then_inc(lat_read, 1)
                elif k > 3:
                    v.tensor_copy(lat[:, KC + k - 4], wk[:, b, 0:T]).then_inc(lat_read, 1)
            norm("qlat", lat[:, KC:], splits=[(gain_of("qlat"), lath, latl, KC, None)])
            for k in range(6):
                blk = block_no(FIRST["uq"] + k)
                ahead(blk)
                if k == 0:
                    norm("kvlat", lat, splits=[(gain_of("kvlat"), lath, latl, 0, None)])
                used(blk)
                b = k % RING
                if k < 4:
                    v.tensor_copy(qn[:, 2 * k:2 * k + 2], wk[:, b].rearrange("p (a t) -> p a t", a=2)).then_inc(uq_read, 1)
                elif k == 5:
                    x1 = wk[:, (b - 1) % RING].rearrange("p (a t) -> p a t", a=2)
                    x2 = wk[:, b].rearrange("p (a t) -> p a t", a=2)
                    dve.wait_ge(lat_read, 7)
                    for s in range(2):
                        cos, sin = ang[:, 6], ang[:, 7]
                        v.tensor_tensor(rt[:, 0, 0:T], x2[:, s], sin, ALU.mult).then_inc(step, 1)
                        v.tensor_tensor(rt[:, 0, T:2 * T], x2[:, s], cos, ALU.mult).then_inc(step, 1)
                        v.tensor_tensor(rt[:, 1, 0:T], x1[:, s], cos, ALU.mult).then_inc(step, 1)
                        done[0] += 3
                        chain(v.tensor_tensor(rt[:, 1, T:2 * T], x1[:, s], sin, ALU.mult))
                        v.tensor_tensor(qpe[:, 0, s], rt[:, 1, 0:T], rt[:, 0, 0:T], ALU.subtract).then_inc(step, 1)
                        done[0] += 1
                        ins = v.tensor_tensor(qpe[:, 1, s], rt[:, 1, T:2 * T], rt[:, 0, T:2 * T], ALU.add)
                        chain(ins)
                    v.engine_nop().then_inc(uq_read, 2)
            for k in range(4):
                blk = block_no(FIRST["ukv"] + k)
                ahead(blk)
                used(blk)
                b = 2 * (k % 2)
                if k < 2:
                    v.tensor_copy(kn[:, 4 * k:4 * k + 4].rearrange("p a t -> p (a t)"),
                                  wk[:, b:b + 2].rearrange("p a t -> p (a t)")).then_inc(ukv_read, 1)
                else:
                    a = 4 * (k - 2)
                    v.tensor_copy(vm[:, :, a:a + 4].rearrange("p b a d -> p b (a d)"), wk[:, b:b + 2]).then_inc(ukv_read, 1)
            v.engine_nop().then_inc(trig, 1)

            def attention(kind, beside=None):
                h0 = attention_base(kind)

                def mask(i, b):
                    n = (b + 1) * P
                    unit = TB * (h0 + i) + b
                    dve.wait_ge(scored, unit + 1)
                    wait(dve, expd, unit - 1)
                    if kind == "latent":
                        m, scale, src = const("mask")[:, b * P:b * P + n], MLA_SCALE, wk[:, unit % 3, 0:n]
                    else:
                        m, scale, src = bias[:, i, b * P:b * P + n], AHD ** -0.5, wk[:, 3, b * P:b * P + n]
                    chain(v.scalar_tensor_tensor(out=sc[:, b, 0:n], in0=src, scalar=scale, in1=m,
                                                 op0=ALU.mult, op1=ALU.add))
                    s = TB * i + b
                    v.tensor_reduce(stat[:, 0, s:s + 1], sc[:, b, 0:n], AX, ALU.max, negate=True).then_inc(masked, 1)

                def divide(i, b):
                    n = (b + 1) * P
                    s = TB * i + b
                    dve.wait_ge(expd, TB * (h0 + i) + b + 1)
                    chain(v.reciprocal(stat[:, 2, s:s + 1], stat[:, 1, s:s + 1]))
                    v.tensor_scalar(pr[:, b, 0:n], pr[:, b, 0:n], stat[:, 2, s:s + 1], None, ALU.mult).then_inc(probs, 1)

                def softmax(i):
                    mask(i, 0)
                    mask(i, 1)
                    divide(i, 0)
                    divide(i, 1)

                softmax(0)
                for i in range(HEADS + 1):
                    if beside and i < HEADS:
                        beside(i, 0)
                    if i + 1 < HEADS:
                        softmax(i + 1)
                    if beside and i < HEADS:
                        beside(i, 1)
                    if i >= 1:
                        j = i - 1
                        if kind == "latent":
                            dve.wait_ge(mixed_hi, j + 1)
                            v.tensor_tensor(yl[:, j], acc[:, 2 + j % 2, 0:T], yh[:, j].bitcast(F32), ALU.subtract
                                            ).then_inc(mixed_lo, 1)
                        elif j % 2 == 1:
                            dve.wait_ge(mixed_hi, HEADS + j // 2 + 1)
                            v.tensor_tensor(yl[:, j // 2], acc[:, 2 + (j // 2) % 2, 0:T], yh[:, j // 2].bitcast(F32),
                                            ALU.subtract).then_inc(mixed_lo, 1)

            attention("latent")
            dve.wait_ge(mod_summed, 1)
            chain(v.tensor_tensor(mod[:], wk[:, 3, 0:6 * DC], gv[:, GAIN["b_ada"]:GAIN["b_ada"] + 6 * DC], ALU.add))
            for s, name in enumerate(["norm1", "norm2"]):
                part = mod[:, (3 * s + 1) * DC:(3 * s + 2) * DC]
                chain(v.scalar_tensor_tensor(out=modg[:, s], in0=part, scalar=1.0,
                                             in1=gv[:, GAIN[name]:GAIN[name] + DC], op0=ALU.add, op1=ALU.mult))
            v.engine_nop().then_inc(mod_ready, 1)
            add_out("attn_out")
            ffn("ffn2", "ffn2", 1)
            norm("final", h, dst=(gain_of("final"), h))
            chain(v.memset(u[:, 0:CK - 1], 0.0))

            norm("mix", h, splits=[(columns(modg[:, 0]), xh, xl, 0, 0)])
            def proj(k):
                blk = block_no(FIRST["proj"] + k)
                ahead(blk)
                if k == 0:
                    dve.wait_ge(band_in, 48)
                    used(blk)
                    for b in range(TB):
                        ins = v.tensor_tensor(gt[:, b], wk[:, blk[0] % RING, b * P:b * P + 2 * BH], gbias[:], ALU.add)
                        if b == 0:
                            ins.then_inc(step, 1)
                            done[0] += 1
                    ins.then_inc(proj_dve, 1)
                elif k < 9:
                    used(blk)
                    c = k - 1
                    w0 = GAIN["conv2_w"] + CK * c
                    wait(dve, conv2, k - 1)
                    v.tensor_copy(u[:, CK - 1:], wk[:, blk[0] % RING, 0:T]).then_inc(proj_dve, 1)
                    dve.wait_ge(proj_dve, k + 1)
                    chain(v.tensor_scalar(uc[:, 0], u[:, 0:T], gv[:, w0:w0 + 1], gain("conv2_b", c), ALU.mult, ALU.add))
                    for t in range(1, CK):
                        if t == CK - 1:
                            wait(dve, silu2, k - 1)
                        ins = v.scalar_tensor_tensor(out=uc[:, t], in0=u[:, t:t + T], scalar=gv[:, w0 + t:w0 + t + 1],
                                                     in1=uc[:, t - 1], op0=ALU.mult, op1=ALU.add)
                        if t < CK - 1:
                            chain(ins)
                        else:
                            ins.then_inc(conv2, 1)
            for k in range(10):
                proj(k)
            dve.wait_ge(proj_dve, 1)
            v.scalar_tensor_tensor(out=gw[:, :, 0], in0=gt[:, :, BH:], scalar=-1.0, in1=gt[:, :, BH:], op0=ALU.mult,
                                   op1=ALU.max).then_inc(gates_ready, 1)
            proj(10)
            dve.wait_ge(gate_exp, 2)
            for b in range(TB):
                chain(v.scalar_tensor_tensor(out=gt[:, b, BH:], in0=gt[:, b, BH:], scalar=0.0, in1=gw[:, b, 2],
                                             op0=ALU.min, op1=ALU.subtract))
            ident, past = const("ident"), (const("past0"), const("past1"))
            chain(v.memset(rr[:], 0.0))

            def m_decays(i):
                wait(dve, decay_sums, TB * i)
                for b in range(TB):
                    n = (b + 1) * P
                    chain(v.tensor_scalar(rr[:, b, 0:n + 1], past[b], gt[:, b, BH + i:BH + i + 1], None, ALU.mult))
                    ins = v.scalar_tensor_tensor(out=rr[:, b, b * P + 1:n + 1], in0=ident, scalar=gt[:, b, i:i + 1],
                                                 in1=rr[:, b, b * P + 1:n + 1], op0=ALU.mult, op1=ALU.add)
                    if b == 0:
                        chain(ins)
                    else:
                        ins.then_inc(decays, 1)

            def m_weigh(unit):
                b = unit % TB
                n = (b + 1) * P
                col = lambda r: ms[:, r, unit:unit + 1]
                dve.wait_ge(decay_sums, unit + 1)
                v.tensor_copy(dm[:, 0:1], acc[:, 0, 0:1]).then_inc(step, 1)
                done[0] += 1
                chain(v.tensor_tensor(dm[:, 1:n + 1], acc[:, 0, 1:n + 1], const("mask")[:, b * P:b * P + n], ALU.add))
                v.tensor_reduce(col(0), dm[:, 0:n + 1], AX, ALU.max, negate=True).then_inc(decay_max, 1)
                dve.wait_ge(decay_exp, 2 * unit + 2)
                v.scalar_tensor_tensor(out=sv[:, 0:n], in0=acc[:, 1, 0:n], scalar=BD ** -0.5, in1=dm[:, 1:n + 1],
                                       op0=ALU.mult, op1=ALU.mult, accum_out=col(2)).then_inc(weighted, 1)
                dve.wait_ge(weighted, unit + 1)
                chain(v.scalar_tensor_tensor(out=col(3), in0=col(2), scalar=-1.0, in1=col(2), op0=ALU.mult, op1=ALU.max))
                chain(v.tensor_scalar(col(3), col(3), col(1), None, ALU.max))
                chain(v.reciprocal(col(6), col(3)))

            m_decays(0)
            proj(11)
            m_weigh(0)
            proj(12)
            for unit in range(TB * BH):
                i, b = divmod(unit, TB)
                if b == 1 and i + 1 < BH:
                    m_decays(i + 1)
                proj(13 + 2 * unit)
                proj(14 + 2 * unit)
                if unit + 1 < TB * BH:
                    dve.wait_ge(w_turned, unit + 1)
                    m_weigh(unit + 1)
                dve.wait_ge(m_mixed, unit + 1)
                v.tensor_scalar(hb[:, b, i], acc[:, 3, 0:P], ms[:, 6, unit:unit + 1], None, ALU.mult).then_inc(m_out, 1)
            dve.wait_ge(m_root, 1)
            chain(v.reciprocal(ms[:, 7], ms[:, 5]))
            for i in range(BH):
                for b in range(TB):
                    unit = TB * i + b
                    chain(v.tensor_scalar(hb[:, b, i], hb[:, b, i], ms[:, 7, unit:unit + 1], None, ALU.mult))
            v.engine_nop().then_inc(m_normed, 1)
            proj(29)
            dve.wait_ge(sigmoids, 4)
            for i in range(BH):
                dve.wait_ge(m_turned, i + 1)
                wait(dve, m_lo, i - 1)
                wait(dve, m_hi, i - 1)
                v.scalar_tensor_tensor(out=uc[:, i % 2], in0=acc[:, i % 2, 0:T], scalar=gain("mlstm", i), in1=ob[:, i],
                                       op0=ALU.mult, op1=ALU.mult).then_inc(m_gated, 1)
                dve.wait_ge(m_hi, i + 1)
                v.tensor_tensor(yl[:, 4 + i], uc[:, i % 2], yh[:, 4 + i].bitcast(F32), ALU.subtract).then_inc(m_lo, 1)
            attention("band", lambda i, half: proj(30 + 2 * i + half) if 30 + 2 * i + half < 45 else None)
            dve.wait_ge(sigmoids, 20)
            for k in range(DC):
                blk = block_no(FIRST["branch"] + k)
                ahead(blk)
                used(blk)
                b = 2 * (k % 2)
                v.tensor_tensor(uc[:, 0], ga[:, k], wk[:, b, 0:T], ALU.mult).then_inc(step, 1)
                done[0] += 1
                chain(v.tensor_tensor(uc[:, 1], gb[:, k], wk[:, b + 1, 0:T], ALU.mult))
                wait(dve, branch_lo, k)
                v.tensor_tensor(uc[:, 2], uc[:, 0], uc[:, 1], ALU.add).then_inc(branch_sum, 1)
                dve.wait_ge(branch_hi, k + 1)
                v.tensor_tensor(xl[:, k], uc[:, 2], xh[:, k].bitcast(F32), ALU.subtract).then_inc(branch_lo, 1)
            add_out("mix_out", columns(mod, 2 * DC))
            norm("peer", h, splits=[(columns(modg[:, 1]), xh, xl, 0, 3)])
            for k in range(2 * PH):
                ahead(block_no(FIRST["peer_q"] + k))

            def top16(values, spare, out_v, out_i, last_sem=None):
                chain(v.max(out_v[:, 0:8], values))
                v.max_index(out_i[:, 0:8], out_v[:, 0:8], values).then_inc(step, 1)
                done[0] += 1
                chain(v.match_replace(spare, out_v[:, 0:8], values, LOWEST))
                chain(v.max(out_v[:, 8:16], spare))
                ins = v.max_index(out_i[:, 8:16], out_v[:, 8:16], spare)
                if last_sem is None:
                    chain(ins)
                else:
                    ins.then_inc(last_sem, 1)

            iota16 = const("iota")[:, 0:TOPK]

            def spread(ap, dims):
                for d in range(3):
                    if d not in dims:
                        ap = ap.unsqueeze(d + 1)
                return ap.to_broadcast([P, PH, TOPK, TOPK])

            for b in range(TB):
                for s in range(2 * PH):
                    if s % 4 == 0:
                        dve.wait_ge(key_read, 4 * b + s // 4 + 1)
                    top16(ks[:, b, s], s2[:], val[:, s], idx[:, s])
                chain(v.tensor_copy(idxf[:], idx[:]))
                sides = val[:].rearrange("p (h s) k -> p h s k", s=2)
                chain(v.tensor_tensor(cand[:].rearrange("p h (a b) -> p h a b", a=TOPK), spread(sides[:, :, 0], (0, 1)),
                                      spread(sides[:, :, 1], (0, 2)), ALU.add))
                for i in range(PH):
                    top16(cand[:, i], c2[:], best[:, b, i], pick[:, 0, i])
                v.tensor_single_scalar(pick[:, 1], pick[:, 0], 4, ALU.logical_shift_right).then_inc(step, 1)
                done[0] += 1
                chain(v.tensor_single_scalar(pick[:, 2], pick[:, 0], TOPK - 1, ALU.bitwise_and))
                chain(v.tensor_copy(pickf[:], pick[:, 1:3]))
                ids = idxf[:].rearrange("p (h s) k -> p h s k", s=2)
                for s in range(2):
                    chain(v.tensor_tensor(eq[:], spread(pickf[:, s], (0, 1)), spread(iota16, (2,)), ALU.is_equal))
                    chain(v.tensor_tensor(eq[:], eq[:], spread(ids[:, :, s], (0, 2)), ALU.mult))
                    chain(v.tensor_reduce(key[:, b, s], eq[:], AX, ALU.add))
                chain(v.tensor_copy(soft[:, b, 0], best[:, b, :, 0]))
                v.tensor_tensor(best[:, b], best[:, b], soft[:, b, 0].unsqueeze(2).to_broadcast([P, PH, TOPK]),
                                ALU.subtract).then_inc(best_sub, 1)
            dve.wait_ge(best_sub, TB)
            dve.wait_ge(best_exp, 1)
            for b in range(TB):
                chain(v.tensor_reduce(soft[:, b, 0], key[:, b, 2], AX, ALU.add))
                chain(v.reciprocal(soft[:, b, 1], soft[:, b, 0]))
                v.tensor_tensor(key[:, b, 2], key[:, b, 2], soft[:, b, 1].unsqueeze(2).to_broadcast([P, PH, TOPK]),
                                ALU.mult).then_inc(keys_ready, 1)
            dve.wait_ge(i_ready, TB)

            def one_hot(g, par):
                if not isinstance(g, int) or g >= 2:
                    dve.wait_ge(hot_used, g - 1)
                for j in range(4):
                    def column(s):
                        return i_t[:, s, bass.ds(g * 4 + j, 1)]
                    v.tensor_scalar(hot[:, par, 0, j], const("iota"), column(0), column(2), ALU.is_equal, ALU.mult)
                    ins = v.tensor_scalar(hot[:, par, 1, j], const("iota"), column(1), None, ALU.is_equal)
                ins.then_inc(hot_ready, 1)

            one_hot(0, 0)
            one_hot(1, 1)
            with dve.Fori(1, T // 8) as i:
                for par in range(2):
                    one_hot(i * 2 + par, par)

            p0 = FIRST["peer"]
            dve.wait_ge(gates_kept, T // 4)

            def weigh(i, k, key_1):
                wait(dve, w_hi, i)
                wait(dve, w_lo, i)
                g = gates[:, :, bass.ds(key_1, 1)].rearrange("p t a -> p (t a)")
                v.tensor_tensor(w32[:], acts[:, k], g, ALU.mult).then_inc(w_ready, 1)

            def rest(i, k):
                dve.wait_ge(w_hi, i + 1)
                v.tensor_tensor(pl[:, k], w32[:], ph[:, k].bitcast(F32), ALU.subtract).then_inc(w_lo, 1)

            def weigh_early(i, k, lap_no):
                if isinstance(i, int) and i < RING:
                    dve.wait_ge(act_ready, EARLY - RING + i + 1)
                    weigh(i, k, EARLY - RING + i)
                else:
                    dve.wait_ge(act_back[k], 16 * lap_no)
                    weigh(i, k, i - RING)

            for i in range(2):
                weigh_early(i, i, 0)
                rest(i, i)
            dve.wait_ge(lo_ready, p0 + EARLY + LEAD)
            p_out = p0 + EARLY

            def early_out(i, k, blk, lap_no):
                weigh_early(i + 2, (k + 2) % RING, lap_no)
                ahead(blk)
                rest(i + 2, (k + 2) % RING)

            for i in range(RING):
                early_out(i, i, block_no(p_out + i), (i + 2) // RING)
            with dve.Fori(1, EARLY // RING - 1) as t:
                for k in range(RING):
                    early_out(t * RING + k, k, block_no(p_out + k, t), t + (k + 2) // RING)
            early_out(EARLY - RING, 0, block_no(p_out + EARLY - RING), (EARLY - 1) // RING)
            ahead(block_no(p_out + EARLY - 2))
            ahead(block_no(p_out + EARLY - 1))

            def weigh_later(i, k):
                dve.wait_ge(act_ready, i + 1)
                weigh(i, k, i)

            p1 = p0 + 2 * EARLY
            ahead(block_no(p1))
            weigh_later(EARLY, 0)

            def pair(i, k, blk):
                rest(i, k)
                ahead(blk)
                weigh_later(i + 1, (k + 1) % RING)
                ahead(after(blk, 1))

            pair(EARLY, 0, block_no(p1 + 1))
            with dve.Fori(0, (NK - 2 - EARLY) // RING - 1) as t:
                for k in range(RING):
                    pair(t * RING + (EARLY + 1 + k), (1 + k) % RING, block_no(p1 + 3 + 2 * k, t, 2))
            for i in range(NK - 1 - RING, NK - 1):
                pair(i, i % RING, block_no(p1 + 1 + 2 * (i - EARLY)))
            rest(NK - 1, (NK - 1) % RING)
            used(block_no(BLOCKS - 1))
            for c in range(DC):
                v.scalar_tensor_tensor(out=h[:, c], in0=acc_tile(c), scalar=mod[:, 5 * DC + c:5 * DC + c + 1], in1=h[:, c],
                                       op0=ALU.mult, op1=ALU.add).then_inc(res_add, 1)
            norm("final2", h, dst=(gain_of("final2"), sq))


def pieces(w):
    k, n = w.shape
    return w.reshape(k // P, P, n // P, P).transpose(2, 1, 0, 3).reshape(n // P, P, (k // P) * P)


def padded(w, width):
    return np.concatenate([w, np.zeros(w.shape[:2] + (width - w.shape[2],), np.float32)], axis=2)


def kernel(x, positions, conv_norm_g, conv_w_in, conv_w, conv_w_out, conv_ffn_norm_g, conv_ffn_w13, conv_ffn_w2,
           kv_norm_g, w_dkv, kv_latent_norm_g, w_ukv, mla_norm_g, mla_w_dq, mla_q_norm_g, mla_w_uq, mla_w_o,
           mla_ffn_norm_g, mla_ffn_w13, mla_ffn_w2, final_norm_g, c_2, w_ada_2, b_ada_2, norm1_g_2, w_in_2, conv_w_2,
           conv_b_2, b_igate_2, b_fgate_2, rel_bias_2, mlstm_norm_g_2, w_branch_a_2, w_branch_b_2, w_out_2, norm2_g_2,
           w_peer_q_2, peer_sub_keys_2, peer_u_2, peer_v_2, final_g_2):
    import concourse.bacc as bacc
    from concourse.bass_utils import run_bass_kernel_spmd

    f = np.asarray
    blocks = []

    w = pieces(f(conv_w_in)[0]).reshape(3, DC, P, 1024)
    blocks.append(w[[1, 2, 0]].transpose(1, 0, 2, 3).reshape(-1, P, 1024))
    blocks.append(pieces(f(conv_w_out)[0]))

    def ffn(w13, w2):
        gu = pieces(f(w13)[0]).reshape(2, FT, P, 1024)
        o = f(w2)[0].reshape(FT, P, D)
        order = [gu[0, 0], gu[1, 0]]
        for j in range(1, FT):
            order += [gu[0, j], gu[1, j], o[j - 1]]
        return np.stack(order + [o[FT - 1]])

    blocks.append(ffn(conv_ffn_w13, conv_ffn_w2))
    dkv = f(w_dkv)
    half = ROPE // 2
    x1, x2 = dkv[:, KVR:KVR + half], dkv[:, KVR + half:]
    blocks.append(pieces(np.concatenate([dkv[:, :KVR]] + [x1] * 4 + [x2] * 4 + [f(mla_w_dq)[0]], axis=1)))
    uq = f(mla_w_uq)[0].reshape(QR, HEADS, NOPE + ROPE)
    uq = np.concatenate([uq[:, :, :NOPE].reshape(QR, -1), uq[:, :, NOPE:NOPE + half].reshape(QR, -1),
                         uq[:, :, NOPE + half:].reshape(QR, -1)], axis=1)
    uq = pieces(uq).reshape(6, 2, P, QC * P).transpose(0, 2, 1, 3).reshape(6, P, 2 * QC * P)
    blocks.append(padded(uq, 1024))
    ukv = f(w_ukv).reshape(KC, P, HEADS, 2, NOPE)
    ukv = ukv.transpose(3, 2, 1, 0, 4).reshape(2, 2, 4, P, KC, NOPE)
    blocks.append(ukv.transpose(0, 1, 3, 4, 2, 5).reshape(4, P, 1024))
    blocks.append(pieces(f(mla_w_o)[0]))
    blocks.append(ffn(mla_ffn_w13, mla_ffn_w2))
    win = f(w_in_2)[0]
    sizes = [512, 512, 512, 1024, 512, 512, BH, BH, D, D]
    qa, ka, va, qkb, vb, ob, ib, fb, ga, gb = np.split(win, np.cumsum(sizes)[:-1], axis=1)
    gate = np.concatenate([ib, fb, np.zeros((D, P - 2 * BH), np.float32)], axis=1)
    blocks.append(pieces(np.concatenate([gate, qkb], axis=1)))
    for v in (vb, va):
        blocks.append(v.reshape(4, 2, P, 512).transpose(0, 2, 1, 3).reshape(4, P, 1024))
    blocks.append(pieces(np.concatenate([qa, ka, ob, ga, gb], axis=1)))
    blocks.append(np.concatenate([pieces(f(w_branch_a_2)[0]), pieces(f(w_branch_b_2)[0])], axis=2))
    blocks.append(pieces(f(w_out_2)[0]))
    blocks.append(pieces(f(w_peer_q_2)[0]))
    pu = f(peer_u_2)[0].reshape(NK, NK, DC, P).transpose(0, 3, 2, 1).reshape(NK, P, 1024)
    pv = f(peer_v_2)[0].reshape(NK, NK, D)
    e = EARLY
    pairs = np.stack([pu[e + 1:], pv[e:-1]], axis=1).reshape(-1, P, 1024)
    blocks += [pu[:e], pv[e - RING:e], pv[:e - RING], pu[e:e + 1], pairs, pv[-1:]]
    stream = np.concatenate(blocks)
    del blocks, pu, pairs
    assert stream.shape == (BLOCKS, P, 1024)

    def column(a):
        return f(a).reshape(-1, P).T

    inv_freq = (np.float32(10000.0) ** (-np.arange(0, ROPE, 2, dtype=np.float32) / np.float32(ROPE))).astype(np.float32)
    gains = np.concatenate(
        [column(a) for a in (conv_norm_g, conv_ffn_norm_g, kv_norm_g, mla_norm_g, kv_latent_norm_g, mla_q_norm_g,
                             mla_ffn_norm_g, final_norm_g, norm1_g_2, norm2_g_2, final_g_2, mlstm_norm_g_2, c_2, b_ada_2)]
        + [f(conv_w)[0].reshape(CW, DC, P).transpose(2, 1, 0).reshape(P, -1),
           f(conv_w_2)[0].reshape(CK, 2 * BH, P).transpose(2, 1, 0).reshape(P, -1), column(conv_b_2),
           np.tile(inv_freq, 4)[:, None]], axis=1).astype(np.float32)

    i = np.arange(P)
    tri = np.where(i[None, :] <= i[:, None], 0.0, NEG)
    past = (i[None, :] < i[:, None]).astype(np.float32)
    one, zero = np.ones((P, 1)), np.zeros((P, P))
    consts = np.concatenate([np.eye(P), np.tile(i, (P, 1)), np.ones((P, P)), tri, zero, tri,
                             i[:, None] <= i[None, :], one, past, one, np.ones((P, P)), past], axis=1).astype(np.float32)

    q, k = np.arange(T)[:, None], np.arange(T)[None, :]
    rel = np.clip(q - k, -CLIP, CLIP) + CLIP
    band = f(rel_bias_2)[0][:, rel]
    band = np.where((k // CHUNK > q // CHUNK)[None], np.float32(NEG), band)
    band = np.concatenate([band[:, :P, :P], band[:, P:]], axis=2).transpose(1, 0, 2)
    gate_bias = np.tile(np.concatenate([f(b_igate_2)[0], f(b_fgate_2)[0]])[None], (P, 1))
    sub_keys = f(peer_sub_keys_2)[0].reshape(2 * PH, NK, P).transpose(2, 0, 1)
    x_in = f(x)[0].reshape(T, DC, P).transpose(2, 1, 0)

    arrays = {"stream": stream, "ada": f(w_ada_2)[0], "gains": gains, "consts": consts, "positions": f(positions),
              "x_in": x_in, "band_bias": band, "gate_bias": gate_bias, "sub_keys": sub_keys}
    arrays = {n: np.ascontiguousarray(a) for n, a in arrays.items()}
    nc = bacc.Bacc("TRN2", target_bir_lowering=False, num_devices=1)
    aps = {n: nc.dram_tensor(n, a.shape, mybir.dt.from_np(a.dtype), kind="ExternalInput").ap() for n, a in arrays.items()}
    aps["positions"] = aps["positions"][0]
    out = nc.dram_tensor("out", (P, DC, T), F32, kind="ExternalOutput").ap()
    put_off = nc.dram_tensor("put_off", (EARLY - RING, P, T), F32, kind="Internal").ap()
    build(nc, out=out, put_off=put_off, **aps)
    r = run_bass_kernel_spmd(nc, [arrays], core_ids=[0])
    return r.results[0]["out"].transpose(2, 1, 0).reshape(1, T, D)
```
